# Optimizing a Trainium2 kernel written in Bass

```python
import math
import jax, jax.numpy as jnp
from jax import lax
import numpy as np

D_MODEL = 1024
BATCH = 1
SEQ = 256
DEPTH = 1

ATTN_HEADS = 8
ATTN_KV_HEADS = 2
ATTN_HEAD_DIM = 128
IDX_HEADS = 4
IDX_HEAD_DIM = 64
TOPK_MAX = 256
Q_BLOCK = 128
ROPE_THETA = 500000.0
ROPE_FRACTION = 4
SSD_EXPAND = 2
SSD_D_INNER = SSD_EXPAND * D_MODEL
SSD_HEAD_DIM = 64
SSD_HEADS = SSD_D_INNER // SSD_HEAD_DIM
SSD_GROUPS = 4
SSD_STATE = 128
SSD_CONV = 4
SSD_CHUNK = 128
SSD_CONV_CH = SSD_D_INNER + 2 * SSD_GROUPS * SSD_STATE
MEM_LEN = 256
MEM_HEADS = 4
MEM_HEAD_DIM = D_MODEL // MEM_HEADS
PEER_HEADS = 8
PEER_N_KEYS = 128
PEER_N_EXPERTS = PEER_N_KEYS * PEER_N_KEYS
PEER_KEY_DIM = 128
PEER_TOPK = 16
PEER_TOKEN_BLOCK = 128
N_BRANCHES = 2
EPS = 1e-6

IN_SPLIT_SIZES = (
    ATTN_HEADS * ATTN_HEAD_DIM,
    ATTN_KV_HEADS * ATTN_HEAD_DIM,
    ATTN_KV_HEADS * ATTN_HEAD_DIM,
    IDX_HEADS * IDX_HEAD_DIM,
    IDX_HEAD_DIM,
    IDX_HEADS,
    SSD_D_INNER,
    SSD_CONV_CH,
    SSD_HEADS,
    N_BRANCHES * D_MODEL,
)
IN_WIDTH = sum(IN_SPLIT_SIZES)


def _in_offsets():
    offs, acc = [], 0
    for s in IN_SPLIT_SIZES[:-1]:
        acc += s
        offs.append(acc)
    return offs

def rmsnorm(x, g):
    xf = x.astype(jnp.float32)
    y = xf * lax.rsqrt(jnp.mean(xf * xf, axis=-1, keepdims=True) + EPS)
    return (y * g.astype(jnp.float32)).astype(x.dtype)

def partial_rope(x, pos):
    d = x.shape[-1]
    rot = d // ROPE_FRACTION
    half = rot // 2
    inv = ROPE_THETA ** (-2.0 * jnp.arange(half, dtype=jnp.float32) / rot)
    ang = pos.astype(jnp.float32)[..., None] * inv
    cos = jnp.cos(ang)[:, :, None, :]
    sin = jnp.sin(ang)[:, :, None, :]
    xf = x.astype(jnp.float32)
    x1 = xf[..., :half]
    x2 = xf[..., half:rot]
    out = jnp.concatenate([x1 * cos - x2 * sin, x2 * cos + x1 * sin, xf[..., rot:]], axis=-1)
    return out.astype(x.dtype)

def dsa_attention(q, k, v, iq, ik, iw):
    b, t, h, dh = q.shape
    kv = k.shape[2]
    grp = h // kv
    n_sel = min(TOPK_MAX, t // 4)
    nblk = t // Q_BLOCK
    idx_scale = IDX_HEAD_DIM ** -0.5
    w_scale = IDX_HEADS ** -0.5
    att_scale = dh ** -0.5
    key_idx = jnp.arange(t)

    def to_blocks(a):
        return a.reshape(b, nblk, Q_BLOCK, *a.shape[2:]).swapaxes(0, 1)

    def block(args):
        qb, iqb, iwb, start = args
        qpos = start + jnp.arange(Q_BLOCK)
        s = jax.nn.relu(jnp.einsum('bqhd,bsd->bqhs', iqb, ik).astype(jnp.float32) * idx_scale)
        score = jnp.einsum('bqhs,bqh->bqs', s, iwb.astype(jnp.float32) * w_scale)
        causal = key_idx[None, :] <= qpos[:, None]
        score = jnp.where(causal[None], score, -jnp.inf)
        _, sel = lax.top_k(score, n_sel)
        valid = sel <= qpos[None, :, None]
        ks = jax.vmap(lambda a, i: a[i])(k, sel)
        vs = jax.vmap(lambda a, i: a[i])(v, sel)
        qg = qb.reshape(b, Q_BLOCK, kv, grp, dh)
        logits = jnp.einsum('bqcgd,bqncd->bqcgn', qg, ks).astype(jnp.float32) * att_scale
        logits = jnp.where(valid[:, :, None, None, :], logits, -jnp.inf)
        p = jax.nn.softmax(logits, axis=-1).astype(vs.dtype)
        o = jnp.einsum('bqcgn,bqncd->bqcgd', p, vs)
        return o.reshape(b, Q_BLOCK, h * dh)

    starts = jnp.arange(nblk) * Q_BLOCK
    out = lax.map(block, (to_blocks(q), to_blocks(iq), to_blocks(iw), starts))
    return out.swapaxes(0, 1).reshape(b, t, h * dh)

def ssd_chunked(xs, dt, a, bm, cm):
    b, t, h, p = xs.shape
    g, n = bm.shape[2], bm.shape[3]
    j = h // g
    L = SSD_CHUNK
    nc = t // L
    xdt = (xs * dt[..., None]).reshape(b, nc, L, g, j, p)
    adt = (dt * a).reshape(b, nc, L, g, j)
    bc = bm.reshape(b, nc, L, g, n)
    cc = cm.reshape(b, nc, L, g, n)
    acs = jnp.cumsum(adt, axis=2)
    tri = jnp.tril(jnp.ones((L, L), dtype=bool))
    seg = acs[:, :, :, None] - acs[:, :, None, :]
    decay = jnp.exp(jnp.where(tri[None, None, :, :, None, None], seg, -jnp.inf))
    cb = jnp.einsum('bclgn,bcsgn->bclsg', cc, bc)
    y_diag = jnp.einsum('bclsgj,bcsgjp->bclgjp', cb[..., None] * decay, xdt)
    decay_to_end = jnp.exp(acs[:, :, -1:] - acs)
    states = jnp.einsum('bcsgn,bcsgj,bcsgjp->bcgjpn', bc, decay_to_end, xdt)
    chunk_decay = jnp.exp(acs[:, :, -1])

    def step(prev, inp):
        st, dec = inp
        return prev * dec[..., None, None] + st, prev

    init = jnp.zeros((b, g, j, p, n), xs.dtype)
    _, prev_states = lax.scan(step, init, (states.swapaxes(0, 1), chunk_decay.swapaxes(0, 1)))
    prev_states = prev_states.swapaxes(0, 1)
    y_off = jnp.einsum('bclgn,bcgjpn,bclgj->bclgjp', cc, prev_states, jnp.exp(acs))
    return (y_diag + y_off).reshape(b, t, h, p)

def ssd_branch(z, xbc, dt_raw, conv_w, conv_b, dt_bias, a_log, d_skip, norm_g):
    b, t, _ = xbc.shape
    xbc = lax.conv_general_dilated(
        xbc, conv_w, window_strides=(1,), padding=[(SSD_CONV - 1, 0)],
        dimension_numbers=('NWC', 'WIO', 'NWC'), feature_group_count=SSD_CONV_CH) + conv_b
    xbc = jax.nn.silu(xbc)
    xs, bm, cm = jnp.split(xbc, [SSD_D_INNER, SSD_D_INNER + SSD_GROUPS * SSD_STATE], axis=-1)
    xs = xs.reshape(b, t, SSD_HEADS, SSD_HEAD_DIM).astype(jnp.float32)
    bm = bm.reshape(b, t, SSD_GROUPS, SSD_STATE).astype(jnp.float32)
    cm = cm.reshape(b, t, SSD_GROUPS, SSD_STATE).astype(jnp.float32)
    dt = jax.nn.softplus(dt_raw.astype(jnp.float32) + dt_bias.astype(jnp.float32))
    a = -jnp.exp(a_log.astype(jnp.float32))
    y = ssd_chunked(xs, dt, a, bm, cm) + xs * d_skip.astype(jnp.float32)[:, None]
    y = y.reshape(b, t, SSD_D_INNER) * jax.nn.silu(z.astype(jnp.float32))
    return rmsnorm(y, norm_g).astype(z.dtype)

def memory_cross_attention(a, m, w_q, w_kv, w_o):
    b, t, _ = a.shape
    q = (a @ w_q).reshape(b, t, MEM_HEADS, MEM_HEAD_DIM)
    kk, vv = jnp.split(m @ w_kv, 2, axis=-1)
    kk = kk.reshape(b, m.shape[1], MEM_HEADS, MEM_HEAD_DIM)
    vv = vv.reshape(b, m.shape[1], MEM_HEADS, MEM_HEAD_DIM)
    logits = jnp.einsum('bthd,bmhd->bhtm', q, kk).astype(jnp.float32) * MEM_HEAD_DIM ** -0.5
    p = jax.nn.softmax(logits, axis=-1).astype(vv.dtype)
    o = jnp.einsum('bhtm,bmhd->bthd', p, vv).reshape(b, t, D_MODEL)
    return o @ w_o

def peer_ffn(a, w_q, sub_keys, u_tab, v_tab):
    b, t, d = a.shape
    n = b * t
    af = a.reshape(n, d)
    qry = (af @ w_q).reshape(n, PEER_HEADS, 2, PEER_KEY_DIM)
    s = jnp.einsum('nhpd,hpkd->nhpk', qry, sub_keys).astype(jnp.float32)
    s_top, i_top = lax.top_k(s, PEER_TOPK)
    cand = (s_top[:, :, 0, :, None] + s_top[:, :, 1, None, :]).reshape(n, PEER_HEADS, PEER_TOPK * PEER_TOPK)
    sc, ci = lax.top_k(cand, PEER_TOPK)
    e_a = jnp.take_along_axis(i_top[:, :, 0], ci // PEER_TOPK, axis=-1)
    e_b = jnp.take_along_axis(i_top[:, :, 1], ci % PEER_TOPK, axis=-1)
    experts = e_a * PEER_N_KEYS + e_b
    gw = jax.nn.softmax(sc, axis=-1)
    n_sel = PEER_HEADS * PEER_TOPK
    nb = n // PEER_TOKEN_BLOCK

    def block(args):
        xb, eb, gb = args
        u = u_tab[eb]
        act = jax.nn.gelu(jnp.einsum('td,tkd->tk', xb, u).astype(jnp.float32), approximate=False)
        wts = (gb * act).astype(v_tab.dtype)
        return jnp.einsum('tk,tkd->td', wts, v_tab[eb])

    out = lax.map(block, (af.reshape(nb, PEER_TOKEN_BLOCK, d),
                          experts.reshape(nb, PEER_TOKEN_BLOCK, n_sel),
                          gw.reshape(nb, PEER_TOKEN_BLOCK, n_sel)))
    return out.reshape(b, t, d)

def first_inputs(seed: int = 0) -> dict:
    key = jax.random.key(seed)
    ks = jax.random.split(key, 26)
    f32 = jnp.float32
    L = DEPTH

    def nrm(k, shape, scale):
        return jax.random.normal(k, shape, f32) * scale

    def gain(k, shape):
        return 1.0 + 0.02 * jax.random.normal(k, shape, f32)

    dt0 = jnp.exp(jax.random.uniform(ks[6], (L, SSD_HEADS), f32, math.log(1e-3), math.log(1e-1)))
    return {
        "x": nrm(ks[0], (BATCH, SEQ, D_MODEL), 1.0),
        "mem": nrm(ks[1], (BATCH, MEM_LEN, D_MODEL), 1.0),
        "positions": jnp.broadcast_to(jnp.arange(SEQ, dtype=jnp.int32), (BATCH, SEQ)),
        "norm_mix_g": gain(ks[2], (L, D_MODEL)),
        "w_in": nrm(ks[3], (L, D_MODEL, IN_WIDTH), D_MODEL ** -0.5),
        "conv_w": nrm(ks[4], (L, SSD_CONV, 1, SSD_CONV_CH), SSD_CONV ** -0.5),
        "conv_b": nrm(ks[5], (L, SSD_CONV_CH), 0.02),
        "dt_bias": dt0 + jnp.log(-jnp.expm1(-dt0)),
        "a_log": jnp.log(jax.random.uniform(ks[7], (L, SSD_HEADS), f32, 1.0, 16.0)),
        "d_skip": gain(ks[8], (L, SSD_HEADS)),
        "ssd_norm_g": gain(ks[9], (L, SSD_D_INNER)),
        "w_attn_branch": nrm(ks[10], (L, ATTN_HEADS * ATTN_HEAD_DIM, D_MODEL), (ATTN_HEADS * ATTN_HEAD_DIM) ** -0.5),
        "w_ssd_branch": nrm(ks[11], (L, SSD_D_INNER, D_MODEL), SSD_D_INNER ** -0.5),
        "w_out": nrm(ks[12], (L, D_MODEL, D_MODEL), D_MODEL ** -0.5),
        "norm_cross_g": gain(ks[13], (L, D_MODEL)),
        "norm_mem_g": gain(ks[14], (L, D_MODEL)),
        "w_cross_q": nrm(ks[15], (L, D_MODEL, MEM_HEADS * MEM_HEAD_DIM), D_MODEL ** -0.5),
        "w_cross_kv": nrm(ks[16], (L, D_MODEL, 2 * MEM_HEADS * MEM_HEAD_DIM), D_MODEL ** -0.5),
        "w_cross_out": nrm(ks[17], (L, MEM_HEADS * MEM_HEAD_DIM, D_MODEL), D_MODEL ** -0.5),
        "norm_ffn_g": gain(ks[18], (L, D_MODEL)),
        "w_peer_q": nrm(ks[19], (L, D_MODEL, PEER_HEADS * 2 * PEER_KEY_DIM), D_MODEL ** -0.5),
        "peer_sub_keys": nrm(ks[20], (L, PEER_HEADS, 2, PEER_N_KEYS, PEER_KEY_DIM), PEER_KEY_DIM ** -0.5),
        "peer_u": nrm(ks[21], (L, PEER_N_EXPERTS, D_MODEL), D_MODEL ** -0.5),
        "peer_v": nrm(ks[22], (L, PEER_N_EXPERTS, D_MODEL), 0.3),
        "norm_final_g": gain(ks[23], (D_MODEL,)),
    }

def first_block(x, mem, positions, norm_mix_g, w_in, conv_w, conv_b, dt_bias, a_log, d_skip,
              ssd_norm_g, w_attn_branch, w_ssd_branch, w_out, norm_cross_g, norm_mem_g,
              w_cross_q, w_cross_kv, w_cross_out, norm_ffn_g, w_peer_q, peer_sub_keys,
              peer_u, peer_v, norm_final_g):
    b, t, _ = x.shape
    offsets = _in_offsets()
    h = x
    for layer in range(DEPTH):
        a = rmsnorm(h, norm_mix_g[layer])
        proj = a @ w_in[layer]
        q, k, v, iq, ik, iw, z, xbc, dt_raw, gate = jnp.split(proj, offsets, axis=-1)
        q = partial_rope(q.reshape(b, t, ATTN_HEADS, ATTN_HEAD_DIM), positions)
        k = partial_rope(k.reshape(b, t, ATTN_KV_HEADS, ATTN_HEAD_DIM), positions)
        v = v.reshape(b, t, ATTN_KV_HEADS, ATTN_HEAD_DIM)
        iq = partial_rope(iq.reshape(b, t, IDX_HEADS, IDX_HEAD_DIM), positions)
        ik = partial_rope(ik.reshape(b, t, 1, IDX_HEAD_DIM), positions)[:, :, 0]
        attn = dsa_attention(q, k, v, iq, ik, iw)
        ssd = ssd_branch(z, xbc, dt_raw, conv_w[layer], conv_b[layer], dt_bias[layer],
                         a_log[layer], d_skip[layer], ssd_norm_g[layer])
        gates = jax.nn.sigmoid(gate.astype(jnp.float32)).reshape(b, t, N_BRANCHES, D_MODEL).astype(x.dtype)
        merged = (gates[:, :, 0] * (attn @ w_attn_branch[layer])
                  + gates[:, :, 1] * (ssd @ w_ssd_branch[layer]))
        h = h + merged @ w_out[layer]
        h = h + memory_cross_attention(rmsnorm(h, norm_cross_g[layer]), rmsnorm(mem, norm_mem_g[layer]),
                                       w_cross_q[layer], w_cross_kv[layer], w_cross_out[layer])
        h = h + peer_ffn(rmsnorm(h, norm_ffn_g[layer]), w_peer_q[layer], peer_sub_keys[layer],
                         peer_u[layer], peer_v[layer])
    return rmsnorm(h, norm_final_g)


GRID_W = 64
CTX_LEN = 256
HG_DIM = 128
HG_WIDTH = D_MODEL // 2
HG_HEADS = HG_WIDTH // HG_DIM
MLP_WIDTH = D_MODEL - HG_WIDTH
MLP_HEADS = 4
MLP_DIM = MLP_WIDTH // MLP_HEADS
MLP_CHUNK = 128
SCAN_CHUNK = 32
MIX_WIDTH = HG_WIDTH + MLP_WIDTH
PROJ_WIDTH = 5 * HG_WIDTH + 2 * MLP_WIDTH
D_FF = 2816
CONV_W = 3


def rmsnorm_2(x, gain):
    xf = x.astype(jnp.float32)
    y = xf * lax.rsqrt(jnp.mean(xf * xf, axis=-1, keepdims=True) + EPS)
    return (y * gain.astype(jnp.float32)).astype(x.dtype)

def layernorm(x, gain, bias):
    xf = x.astype(jnp.float32)
    mu = jnp.mean(xf, axis=-1, keepdims=True)
    var = jnp.mean(jnp.square(xf - mu), axis=-1, keepdims=True)
    y = (xf - mu) * lax.rsqrt(var + EPS) * gain.astype(jnp.float32) + bias.astype(jnp.float32)
    return y.astype(x.dtype)

def modulate(h, shift, scale):
    return h * (1.0 + scale) + shift

def split_heads(a, n_heads):
    b, t, w = a.shape
    return a.reshape(b, t, n_heads, w // n_heads).transpose(0, 2, 1, 3)

def merge_heads(a):
    b, h, t, d = a.shape
    return a.transpose(0, 2, 1, 3).reshape(b, t, h * d)

def flip_t(a):
    return jnp.flip(a, axis=2)

def lower_bounds(logits):
    cum = jnp.cumsum(jax.nn.softmax(logits.astype(jnp.float32), axis=0), axis=0)
    return cum - cum[0:1]

def forget_gate(f_logit, lb, first):
    f = f_logit.astype(jnp.float32)
    if first:
        return jax.nn.log_sigmoid(f), jax.nn.sigmoid(-f)
    gate = lb + (1.0 - lb) * jax.nn.sigmoid(f)
    return jnp.log(gate), 1.0 - gate

def hgrn2_gates(p, lb_f, lb_b, first):
    w = HG_WIDTH
    logf_f, k_f = forget_gate(p[..., :w], lb_f, first)
    logf_b, k_b = forget_gate(p[..., w:2 * w], lb_b, first)
    v = p[..., 2 * w:3 * w].astype(jnp.float32)
    return tuple(split_heads(a, HG_HEADS) for a in (logf_f, k_f, logf_b, k_b, v))

def advance_state(h, k, v, b):
    b_last = b[:, :, -1:, :]
    return (jnp.exp(b_last)[:, :, 0, :, None] * h
            + jnp.einsum('bhsk,bhsv->bhkv', k * jnp.exp(b_last - b), v))

def chunk_gla(q, k, v, log_f, h0):
    b_, h_, t, _ = q.shape
    n = t // SCAN_CHUNK

    def to_chunks(a):
        return jnp.moveaxis(a.reshape(b_, h_, n, SCAN_CHUNK, a.shape[-1]), 2, 0)

    mask = jnp.tril(jnp.ones((SCAN_CHUNK, SCAN_CHUNK), dtype=bool))[:, :, None]

    def step(h, blk):
        qc, kc, vc, gc = blk
        b = jnp.cumsum(gc, axis=2)
        o_inter = jnp.einsum('bhtk,bhkv->bhtv', qc * jnp.exp(b), h)
        diff = b[:, :, :, None, :] - b[:, :, None, :, :]
        decay = jnp.where(mask, jnp.exp(jnp.where(mask, diff, 0.0)), 0.0)
        scores = jnp.einsum('bhtk,bhsk,bhtsk->bhts', qc, kc, decay)
        o = o_inter + jnp.einsum('bhts,bhsv->bhtv', scores, vc)
        return advance_state(h, kc, vc, b), o

    h_end, o = lax.scan(step, h0, (to_chunks(q), to_chunks(k), to_chunks(v), to_chunks(log_f)))
    o = jnp.moveaxis(o, 0, 2).reshape(b_, h_, t, v.shape[-1])
    return o, h_end

def chunk_sgu(u, v, ln_g, ln_b, w_s, b_s):
    bsz, t, _ = u.shape
    n = t // MLP_CHUNK
    u = jax.nn.gelu(u, approximate=False).reshape(bsz, n, MLP_CHUNK, MLP_HEADS, MLP_DIM)
    v = jax.nn.gelu(v, approximate=False).reshape(bsz, n, MLP_CHUNK, MLP_HEADS, MLP_DIM)
    v = layernorm(v, ln_g.reshape(MLP_HEADS, MLP_DIM), ln_b.reshape(MLP_HEADS, MLP_DIM))
    z = jnp.einsum('hpq,bnqhc->bnphc', w_s.astype(v.dtype), v) + jnp.transpose(b_s)[None, None, :, :, None]
    return (u * z).reshape(bsz, t, MLP_WIDTH)

def token_mixers(p, lb_f, lb_b, first, h0_f, h0_b, hg_gain, sgu_g, sgu_b, w_s, b_s):
    w = HG_WIDTH
    logf_f, k_f, logf_b, k_b, v = hgrn2_gates(p, lb_f, lb_b, first)
    q = split_heads(jax.nn.silu(p[..., 3 * w:4 * w].astype(jnp.float32)), HG_HEADS) * (HG_DIM ** -0.5)
    o_f, h_f = chunk_gla(q, k_f, v, logf_f, h0_f)
    o_b, h_b = chunk_gla(flip_t(q), flip_t(k_b), flip_t(v), flip_t(logf_b), h0_b)
    o = rmsnorm_2(o_f + flip_t(o_b), hg_gain.reshape(HG_HEADS, 1, HG_DIM))
    o_hg = merge_heads(o).astype(p.dtype) * jax.nn.silu(p[..., 4 * w:5 * w])
    o_mlp = chunk_sgu(p[..., 5 * w:5 * w + MLP_WIDTH], p[..., 5 * w + MLP_WIDTH:], sgu_g, sgu_b, w_s, b_s)
    return jnp.concatenate([o_hg, o_mlp], axis=-1), h_f, h_b

def conv_ffn(h, w_up, taps, conv_b, w_down, rows):
    a, g = jnp.split(h @ w_up, 2, axis=-1)
    bsz, t, f = g.shape
    if rows is None:
        g2, tp = g.reshape(bsz, 1, t, f), taps[1:2]
    else:
        g2, tp = g.reshape(bsz, rows, GRID_W, f), taps
    gc = lax.conv_general_dilated(g2, tp[:, :, None, :].astype(g.dtype), (1, 1), 'SAME',
                                  dimension_numbers=('NHWC', 'HWIO', 'NHWC'), feature_group_count=f)
    gc = gc.reshape(bsz, t, f) + conv_b
    return (a * jax.nn.gelu(gc, approximate=False)) @ w_down

def second_inputs(seed: int = 0) -> dict:
    key = jax.random.key(seed)
    ks = jax.random.split(key, 22)
    nrm = jax.random.normal
    L, D, F = DEPTH, D_MODEL, D_FF
    return {
        "x": nrm(ks[0], (BATCH, SEQ, D), jnp.float32),
        "c": nrm(ks[1], (BATCH, D), jnp.float32),
        "ctx": nrm(ks[2], (BATCH, CTX_LEN, D), jnp.float32),
        "c_ctx": nrm(ks[3], (D,), jnp.float32),
        "w_ada": nrm(ks[4], (L, D, 6 * D), jnp.float32) * (0.5 * D ** -0.5),
        "b_ada": nrm(ks[5], (L, 6 * D), jnp.float32) * 0.02,
        "norm_mix": 1.0 + 0.1 * nrm(ks[6], (L, D), jnp.float32),
        "norm_ffn": 1.0 + 0.1 * nrm(ks[7], (L, D), jnp.float32),
        "w_in": nrm(ks[8], (L, D, PROJ_WIDTH), jnp.float32) * D ** -0.5,
        "lb_logits_fwd": nrm(ks[9], (L, HG_WIDTH), jnp.float32),
        "lb_logits_bwd": nrm(ks[10], (L, HG_WIDTH), jnp.float32),
        "hg_norm": 1.0 + 0.1 * nrm(ks[11], (L, HG_WIDTH), jnp.float32),
        "sgu_norm_g": 1.0 + 0.1 * nrm(ks[12], (L, MLP_WIDTH), jnp.float32),
        "sgu_norm_b": 0.02 * nrm(ks[13], (L, MLP_WIDTH), jnp.float32),
        "w_spatial": nrm(ks[14], (L, MLP_HEADS, MLP_CHUNK, MLP_CHUNK), jnp.float32) * MLP_CHUNK ** -0.5,
        "b_spatial": 1.0 + 0.1 * nrm(ks[15], (L, MLP_HEADS, MLP_CHUNK), jnp.float32),
        "w_out": nrm(ks[16], (L, MIX_WIDTH, D), jnp.float32) * MIX_WIDTH ** -0.5,
        "w_up": nrm(ks[17], (L, D, 2 * F), jnp.float32) * D ** -0.5,
        "conv_w": nrm(ks[18], (L, CONV_W, CONV_W, F), jnp.float32) / CONV_W,
        "conv_b": 0.02 * nrm(ks[19], (L, F), jnp.float32),
        "w_down": nrm(ks[20], (L, F, D), jnp.float32) * F ** -0.5,
        "norm_final": 1.0 + 0.1 * nrm(ks[21], (D,), jnp.float32),
    }

def second_block(x, c, ctx, c_ctx, w_ada, b_ada, norm_mix, norm_ffn, w_in, lb_logits_fwd, lb_logits_bwd,
              hg_norm, sgu_norm_g, sgu_norm_b, w_spatial, b_spatial, w_out, w_up, conv_w, conv_b, w_down,
              norm_final):
    w = HG_WIDTH
    rows = x.shape[1] // GRID_W
    bsz = x.shape[0]
    lb_f_all = lower_bounds(lb_logits_fwd)
    lb_b_all = lower_bounds(lb_logits_bwd)
    ada = jnp.einsum('bd,lde->lbe', jax.nn.silu(c), w_ada) + b_ada[:, None, :]
    ada_c = jnp.einsum('d,lde->le', jax.nn.silu(c_ctx), w_ada) + b_ada
    h0 = jnp.zeros((bsz, HG_HEADS, HG_DIM, HG_DIM), jnp.float32)
    xc = ctx
    for l in range(DEPTH):
        first, last = l == 0, l == DEPTH - 1
        sh1, sc1, g1, sh2, sc2, g2 = (m[:, None, :] for m in jnp.split(ada[l], 6, axis=-1))
        csh1, csc1, cg1, csh2, csc2, cg2 = jnp.split(ada_c[l], 6, axis=-1)
        lb_f, lb_b = lb_f_all[l], lb_b_all[l]
        mix_args = (hg_norm[l], sgu_norm_g[l], sgu_norm_b[l], w_spatial[l], b_spatial[l])

        hc = modulate(rmsnorm_2(xc, norm_mix[l]), csh1, csc1)
        if last:
            logf_f, k_f, logf_b, k_b, vc = hgrn2_gates(hc @ w_in[l][:, :3 * w], lb_f, lb_b, first)
            hf_c = advance_state(h0, k_f, vc, jnp.cumsum(logf_f, axis=2))
            hb_c = advance_state(h0, flip_t(k_b), flip_t(vc), jnp.cumsum(flip_t(logf_b), axis=2))
        else:
            oc, hf_c, hb_c = token_mixers(hc @ w_in[l], lb_f, lb_b, first, h0, h0, *mix_args)

        h = modulate(rmsnorm_2(x, norm_mix[l]), sh1, sc1)
        o, _, _ = token_mixers(h @ w_in[l], lb_f, lb_b, first, hf_c, hb_c, *mix_args)
        x = x + g1 * (o @ w_out[l])
        h2 = modulate(rmsnorm_2(x, norm_ffn[l]), sh2, sc2)
        x = x + g2 * conv_ffn(h2, w_up[l], conv_w[l], conv_b[l], w_down[l], rows)

        if not last:
            xc = xc + cg1 * (oc @ w_out[l])
            hc2 = modulate(rmsnorm_2(xc, norm_ffn[l]), csh2, csc2)
            xc = xc + cg2 * conv_ffn(hc2, w_up[l], conv_w[l], conv_b[l], w_down[l], None)
    return rmsnorm_2(x, norm_final)


def setup_inputs(seed=0):
    out = dict(first_inputs(seed))
    for name, value in second_inputs(seed + 1).items():
        if name != "x":
            out[name + "_2"] = value
    return out


def reference(
    x, mem, positions, norm_mix_g, w_in, conv_w, conv_b, dt_bias, a_log, d_skip, ssd_norm_g,
    w_attn_branch, w_ssd_branch, w_out, norm_cross_g, norm_mem_g, w_cross_q, w_cross_kv,
    w_cross_out, norm_ffn_g, w_peer_q, peer_sub_keys, peer_u, peer_v, norm_final_g, c_2, ctx_2,
    c_ctx_2, w_ada_2, b_ada_2, norm_mix_2, norm_ffn_2, w_in_2, lb_logits_fwd_2, lb_logits_bwd_2,
    hg_norm_2, sgu_norm_g_2, sgu_norm_b_2, w_spatial_2, b_spatial_2, w_out_2, w_up_2, conv_w_2,
    conv_b_2, w_down_2, norm_final_2,
):
    x = first_block(
        x, mem, positions, norm_mix_g, w_in, conv_w, conv_b, dt_bias, a_log, d_skip, ssd_norm_g,
        w_attn_branch, w_ssd_branch, w_out, norm_cross_g, norm_mem_g, w_cross_q, w_cross_kv,
        w_cross_out, norm_ffn_g, w_peer_q, peer_sub_keys, peer_u, peer_v, norm_final_g,
    )
    return second_block(
        x, c_2, ctx_2, c_ctx_2, w_ada_2, b_ada_2, norm_mix_2, norm_ffn_2, w_in_2,
        lb_logits_fwd_2, lb_logits_bwd_2, hg_norm_2, sgu_norm_g_2, sgu_norm_b_2, w_spatial_2,
        b_spatial_2, w_out_2, w_up_2, conv_w_2, conv_b_2, w_down_2, norm_final_2,
    )


_drawn_inputs = setup_inputs


def setup_inputs(seed=0):
    import zlib

    import numpy as np

    out = dict(_drawn_inputs(seed))
    spreads = {}
    factors = {'d_skip': 4.212,
     'ssd_norm_g': 3.249,
     'norm_cross_g': 7.531,
     'norm_mem_g': 6.914,
     'norm_ffn_g': 21.568,
     'norm_final_g': 7.733,
     'ctx_2': 47.303,
     'c_ctx_2': 30.348,
     'hg_norm_2': 11.442,
     'sgu_norm_g_2': 9.429,
     'sgu_norm_b_2': 50.197,
     'b_spatial_2': 10.561,
     'conv_b_2': 35.52,
     'norm_ffn_2': 5.251}
    for name, (base, spread) in spreads.items():
        noise = np.random.default_rng([zlib.crc32(name.encode()), seed]).standard_normal(out[name].shape)
        drawn = base * np.exp(spread * noise) if base else spread * noise
        out[name] = __import__('jax').numpy.asarray(drawn.astype(out[name].dtype))
    for name, factor in factors.items():
        out[name] = (out[name] * factor).astype(out[name].dtype)
    return out
```

```python
from contextlib import ExitStack

import numpy as np

import concourse.bass as bass
from concourse import mybir

P = 128
T = 256
TT = T // P
D = 1024
KC = D // P
EPS = 1e-6
TWO_PI = [6.28125, float(np.float32(2 * np.pi - 6.28125) // 2**-20 * 2**-20), 0.0]
TWO_PI[2] = float(2 * np.pi - TWO_PI[0] - TWO_PI[1])
NEG = -3.0e38
TAKEN = -3.4e38
OFF = -1.0e30

QH, KVH, DH = 8, 2, 128
IH, IDH = 4, 64
TOPK = T // 4
SH, SP_, SG, SN = 32, 64, 4, 128
SD = SH * SP_
MH, MD = 4, 256
PH, PK, PTOP = 8, 128, 16
PSLOT = PH * PTOP
HG, HH = 512, 4
FF, FC = 2816, 22
GW = 64
THETA = 500000.0

F32 = mybir.dt.float32
U32 = mybir.dt.uint32
I32 = mybir.dt.int32
ALU = mybir.AluOpType
ACT = mybir.ActivationFunctionType
AX = mybir.AxisListType

SECTIONS = [
    ("in_tok", 16), ("in_xbc", 24), ("in_z", 16), ("in_gate", 16), ("mem_k", 8), ("mem_v", 8), ("merge", 24),
    ("w_out", 8), ("cross_q", 8), ("cross_out", 8), ("peer_q", 16), ("ada", 48), ("ctx", 12),
    ("experts", 2 * P), ("in2", 28), ("out2", 8),
]
FIRST = {}
_n = 0
for _name, _count in SECTIONS:
    FIRST[_name] = _n
    _n += _count
RING = 8
N_RING = _n
assert N_RING % RING == 0
FRING = 6
N_FFN = 3 * FC
FFN0 = N_RING

CONST = {}
_c = 0
for _name, _w in [("ident", P), ("upto", P), ("ones", P), ("after", P), ("before", P), ("causal", P),
                  ("iota", P), ("freq", 24), ("iota16", 16)]:
    CONST[_name] = (_c, _w)
    _c += _w
N_CONST = _c
N_LEVELS = 7
N_SPAN = (N_LEVELS + 1) * P
COLS = {}
_c = 0
for _name, _w in [("g_mix", 8), ("g_cross", 8), ("g_mem", 8), ("g_ffn", 8), ("g_ssd", 16), ("conv_w", 96),
                  ("conv_b", 24), ("c2", 16), ("b_ada", 48), ("g_mix2", 8), ("g_ffn2", 8), ("taps", 198),
                  ("fconv_b", 22), ("b_s", 4)]:
    COLS[_name] = (_c, _w)
    _c += _w
N_COLS = _c
ROWS = {}
_c = 0
for _name, _w in [("dt_bias", 32), ("a_log", 32), ("d_skip", 32)]:
    ROWS[_name] = (_c, _w)
    _c += _w
N_ROWS = _c
ROWS2 = {}
_c = 0
for _name, _w in [("hg", 512), ("sgu_g", 512), ("sgu_b", 512)]:
    ROWS2[_name] = (_c, _w)
    _c += _w
N_ROWS2 = _c


class Banks:

    def __init__(self):
        self.fills = [0] * 8
        self.at = {}
        self.next = 0

    def job(self, *name, bank=None):
        b = self.next if bank is None else bank
        self.next = (b + 1) % 8
        self.fills[b] += 1
        self.at[name] = (b, self.fills[b])

    def loop(self, name, turns, width, banks=None):
        for j in range(width):
            self.job(name, j, bank=None if banks is None else banks[j])
        for j in range(width):
            self.fills[self.at[(name, j)][0]] += turns - 1


def plan_banks():
    B = Banks()
    B.start = {}
    for t in range(TT):
        for h in range(2):
            B.job("xT", t, h)
    for b in range(4):
        for t in range(TT):
            B.job("tok", b, t)
    B.loop("xbc", 3, 8)
    for t in range(TT):
        for h in range(2):
            B.job("qTr", t, h)
    B.job("kTr")
    B.job("iqTr")
    B.job("ikTr")
    for b in range(4):
        for t in range(TT):
            B.job("z", b, t)
    for t in range(TT):
        for r in range(2):
            B.job("idx", t, r)
    B.loop("gate", 2, 8)
    for t in range(TT):
        for p in range(4):
            B.job("lg", t, p)
    for t in range(TT):
        for q in range(4):
            B.job("xsTr", t, q)
    B.job("BTr")
    B.job("acs")
    for t in range(TT):
        for n in range(2 * (t + 1)):
            B.job("PTr", t, n)
        for kv in range(KVH):
            B.job("oT", t, kv)
    B.job("cb", 0)
    B.job("cb", 1)
    groups = [(c, g) for c in range(TT) for g in range(SG)]
    for k in range(len(groups) + 1):
        if k < len(groups):
            B.job("row", *groups[k], 0)
            B.job("row", *groups[k], 1)
        if k >= 1:
            c, g = groups[k - 1]
            B.job("yd", c, g)
            B.job("st" if c == 0 else "yo", g)
    for t in range(TT):
        for h in range(2):
            B.job("mT", t, h)
    for n in range(8):
        B.job("mk", n)
    for b in range(2):
        for t in range(TT):
            B.job("mv", b, t)
    for t in range(TT):
        for q in range(4):
            B.job("yTr", t, q)
    for n in range(8):
        B.job("ma", n)
        B.job("ms", n)
    for b in range(2):
        for t in range(TT):
            B.job("wo", b, t)
    for t in range(TT):
        for h in range(2):
            B.job("a2T", t, h)
    for n in range(8):
        B.job("cq", n)
    for t in range(TT):
        for p in range(2):
            B.job("cl", t, p)
    for t in range(TT):
        for m in range(TT):
            B.job("cP", t, m)
    for h in range(MH):
        B.job("co", h)
    for b in range(2):
        for t in range(TT):
            B.job("cw", b, t)
    for t in range(TT):
        for h in range(2):
            B.job("a3T", t, h)
    B.loop("pq", 2, 8)
    for t in range(TT):
        for q in range(4):
            B.job("sk", t, q)
    B.loop("ada", 3, 2)
    for t in range(TT):
        for h in range(2):
            B.job("cT", t, h)
    for b in range(3):
        for t in range(TT):
            B.job("cp", b, t)
    for d in range(2):
        for t in range(TT):
            B.job("ce", d, t)
    for d in range(2):
        B.job("cH", d)
    for t in range(TT):
        B.job("eTr", t)
    B.loop("w", T // 8, 2, banks=(4, 5))
    for t in range(TT):
        for h in range(2):
            B.job("y", t, h, bank=2 * t + h)
    B.job("h0", bank=4)
    B.loop("h", 31, 4, banks=(5, 6, 7, 4))
    for u in range(3):
        B.job("he", u, bank=5 + u)
    B.next = 4
    for t in range(TT):
        for h in range(2):
            B.job("x2T", t, h)
    for b in range(7):
        for t in range(TT):
            B.job("p", b, t)
    for t in range(TT):
        B.job("qT2", t)
    for d in range(2):
        for t in range(TT):
            B.job("kT2", d, t)
    for d in range(2):
        B.job("as", d)
    B.job("tot")
    for d in range(2):
        B.job("adv", d)
    for t in range(TT):
        B.job("dg", t)
        for d in range(2):
            for h in range(HH):
                B.job("e", t, d, h, 0)
                B.job("e", t, d, h, 1)
            for lev in range(N_LEVELS):
                B.job("gr", t, d, lev)
        B.job("o", t)
    for t in range(TT):
        B.job("sg", t)
    for r in range(4):
        B.job("gb", r)
    for t in range(TT):
        for h in range(2):
            B.job("ocT", t, h)
    for b in range(2):
        for t in range(TT):
            B.job("w2", b, t)
    for t in range(TT):
        for h in range(2):
            B.job("x3T", t, h)
    for t in range(TT):
        for h in range(2):
            B.job("f", t, h, bank=2 * t + h)
    B.job("g0", bank=4)
    B.job("a0", bank=6)
    B.loop("ga", (FC - 2) // 2, 4, banks=(5, 7, 4, 6))
    B.job("ge", bank=5)
    B.job("ae", bank=7)
    return B


def bc(ap, axis, n):
    ap = ap.unsqueeze(axis)
    shape = list(ap.shape)
    shape[axis] = n
    return ap.to_broadcast(shape)


class Count:

    def __init__(self, sem):
        self.sem, self.n = sem, 0

    def by(self, ins, n=1):
        ins.then_inc(self.sem, n)
        self.n += n
        return self.n


class Chain:

    def __init__(self, eng, sem):
        self.eng, self.c = eng, Count(sem)

    def __call__(self, ins):
        self.eng.wait_ge(self.c.sem, self.c.by(ins))


def build(nc, A):
    B = plan_banks()
    with ExitStack() as ctx:
        def sb(name, shape, dt=F32):
            return ctx.enter_context(nc.sbuf_tensor(name, shape, dt))

        def sem(name):
            return ctx.enter_context(nc.semaphore(name))

        ps = ctx.enter_context(nc.psum_tensor("banks", [P, 8, 512], F32))
        bank_full = [sem(f"bank_full{b}") for b in range(8)]
        bank_free = [sem(f"bank_free{b}") for b in range(8)]

        ring = sb("weight_ring", [P, RING, 1024])
        arena = sb("arena", [P, 32768])
        scratch = sb("scratch", [P, 2048])
        hres = sb("residual", [P, TT, D])
        actT = sb("act_feature_major", [P, KC, T])
        const = sb("const", [P, N_CONST])
        cols = sb("cols", [P, N_COLS])
        rows = sb("rows", [P, N_ROWS])
        stat = sb("stat", [P, 4, 10, TT])
        slots = sb("expert_slots", [P, 3, T])
        h0 = sb("state_from_context", [P, 2, HH, P])
        mods = sb("modulation", [P, 48, 2])
        modsb = sb("modulation_sums", [P, 64])
        small = sb("small", [P, 1024])

        ring_loaded = [sem(f"ring_loaded{s}") for s in range(RING)]
        ffn_loaded = [sem(f"ffn_loaded{s}") for s in range(FRING)]
        tiles_begun = sem("tiles_begun")
        in_x = sem("x_loaded")
        in_mem = sem("mem_loaded")
        in_const = sem("const_loaded")
        in_ctx = sem("ctx_loaded")
        in_keys = sem("subkeys_loaded")
        in_second = sem("second_consts_loaded")
        out_done = sem("out_stored")
        names = """norm_sq norm_ms norm_root xn_ready act_ready rope_ready xbc_ready attn_masked attn_exp
            attn_prob dt_abs dt_l adt_ready acs_ready acs_exp seg_exp m_ready adtb_ready xdtd_ready y_ready
            mem_v merged_ready cl_ready cprob gate_sc gate_exp idx_ready onehot_ready p_ready p_used silu_c
            ctx_abs ctx_l ctx_nk ctx_f ctx_k ctx_kd rope_arg rope_sin x2_ready g_abs g_l g_nk g_logf g_k
            g_kd g_H z_made o_ms o_root v_ready oc_ready gdiag x3_ready ffn_conv ffn_gelu ffn_used x4_ready
            out_ready act_step dve_step zeros_ready neg_a""".split()
        S = {n: sem(n) for n in names}

        def C(name):
            o, w = CONST[name]
            return const[:, o:o + w]

        def col(name):
            o, w = COLS[name]
            return cols[:, o:o + w]

        def row(name):
            o, w = ROWS[name]
            return rows[:, o:o + w]

        def area(off, *dims):
            n = int(np.prod(dims))
            assert off + n <= 32768, (off, dims)
            v = arena[:, off:off + n]
            if len(dims) == 1:
                return v
            names_ = "abcd"[:len(dims)]
            return v.rearrange(f"p ({' '.join(names_)}) -> p {' '.join(names_)}",
                               **{k: d for k, d in zip(names_[1:], dims[1:])})

        def bank(name):
            return ps[:, B.at[name][0], :]

        def claim(name, turn=None):
            b, n = B.at[name]
            if turn is not None:
                nc.tensor.wait_ge(bank_free[b], turn + (n - 1))
            elif n > 1:
                nc.tensor.wait_ge(bank_free[b], n - 1)
            return ps[:, b, :]

        def filled(ins, name):
            ins.then_inc(bank_full[B.at[name][0]], 1)

        def arrived(eng, name, turn=None):
            b, n = B.at[name]
            eng.wait_ge(bank_full[b], n if turn is None else turn + n)
            return ps[:, b, :]

        def freed(eng, name, turn=None):
            b, n = B.at[name]
            eng.wait_ge(bank_free[b], n if turn is None else turn + n)

        def free(ins, name):
            ins.then_inc(bank_free[B.at[name][0]], 1)

        TOK = area(0, TT, 2048)
        XBC = area(4096, 24, T)
        ZT = area(10240, TT, 2048)
        GT = area(14336, 16, T)
        QT = area(18432, 8, T)
        KT = area(20480, 2, T)
        IQT = area(20992, 2, T)
        IKT = area(21504, T)
        IKD = area(21760, TT, P)
        RELU = area(22016, 4, 2, T)
        SC = area(24064, 4, T)
        LG = [area(25088, 8, P), area(26112, 8, T)]
        PT = area(28160, 2, 8, P)
        AT = area(30208, 8, T)
        ROPE = area(32256, 2, TT, 24)
        ROPET = area(22016, 5, 96)
        RT = area(22656, 2, TT * 160)
        XS = area(18432, TT, 2048)
        YT_ = area(22528, TT, 2048)
        BTOK = area(0, SG, P)
        EM = area(26624, 2, 8, P)
        ADTB = scratch[:, :].rearrange("p (b h l) -> p b h l", b=2, h=8)
        CBM = area(28672, TT, SG, P)
        XDTD = area(4096, 2048)
        STATE = area(6144, SG, 512)
        YT = area(4096, 16, T)
        MT = area(0, KC, T)
        MEMX = area(2048, TT, D)
        MKT = area(18432, KC, T)
        MV = area(20480, TT, D)
        MG = area(26624, KC, T)
        CQT = area(8192, KC, T)
        CL = area(0, 4, T)
        CPT = area(2048, 2, 4, T)
        COT = area(10240, KC, T)
        QPT = area(0, 16, T)
        SK = area(4096, TT, 16, P)
        SK2 = area(8192, 16, P)
        CAND = area(10240, PH, 256)
        CAND2 = area(12288, PH, 256)
        OH = area(14336, 2048)
        TOPV = area(16384, 16, PTOP)
        TOPI = area(16640, 16, PTOP)
        TOPIF = area(16896, 16, PTOP)
        SCV = area(17152, PH, PTOP)
        SCI = area(17280, PH, PTOP)
        CIA = area(17408, 2, P)
        CIAF = area(17664, 2, P)
        EAB = area(17920, 3, P)
        SMX = area(18304, 8)
        KEYS = area(18432, 16, P)
        CX = area(20480, TT, D)
        CXT = area(22528, KC, T)
        CPJ = area(24576, TT, 1536)
        CLF = area(27648, TT, 1024)
        CKK = area(29696, TT, 1024)
        WT = area(0, P, T)
        FR = area(0, FRING, 1024)
        PJ = area(6144, TT, 3584)
        LF = area(13312, TT, 1024)
        K2 = area(15360, TT, 1024)
        K2T = area(17408, 2, HH, T)
        Q2T = area(19456, HH, T)
        ZQ = area(20480, HH, 8, P)
        ZK = area(24576, HH, 7, P)
        SM = area(28160, HH, P)
        ZP = area(28672, 2, HH, P)
        HS = area(29696, 2, HH, P)
        LEV = area(30720, 15, P)
        GSPAN = scratch[:, :].rearrange("p (d n) -> p d n", d=2)
        OC = area(20480, TT, D)
        T512 = area(22528, 4, 512)
        GB = area(24576, 2, D)
        GBD = area(26624, 2, KC, P)
        FIN1 = area(0, D)
        R2 = area(4096, N_ROWS2)
        FIN2 = area(30720, D)
        CV = area(17408, 2, T)
        GC = area(18432, 2, T)
        GE = area(19456, 2, T)
        HF = area(20480, 2, T)
        WSP = small[:, 0:512].rearrange("p (h n) -> p h n", h=HH)

        smx = sb("softmax_stats", [P, TT, 4, 8])
        c2s = sb("silu_of_conditions", [P, KC, 2])
        gst = sb("mixer_stats", [P, 4, 2, TT, HH])
        lo = lambda a, b: small[:, a:b]
        DT = lo(0, 64).rearrange("p (c h) -> p c h", c=TT)
        DTS = lo(64, 128).rearrange("p (c h) -> p c h", c=TT)
        DTL = lo(128, 192).rearrange("p (c h) -> p c h", c=TT)
        ADT = lo(256, 320).rearrange("p (c h) -> p c h", c=TT)
        ACS = lo(320, 448).rearrange("p (c h) -> p c h", c=4)
        EAC = lo(448, 512).rearrange("p (c h) -> p c h", c=TT)
        DTE = lo(544, 576)
        NEGA = lo(576, 608)
        IW = lo(608, 616).rearrange("p (c h) -> p c h", c=TT)
        ident = C("ident")
        XN = scratch[:, :].rearrange("p (t d) -> p t d", t=TT)
        ONEHOT = scratch[:, :].rearrange("p (u v x n) -> p u v x n", u=2, v=4, x=2)
        GELU = scratch[:, 0:512].rearrange("p (b t) -> p b t", b=2)
        GATED = scratch[:, 512:1024].rearrange("p (b t) -> p b t", b=2)
        CEX = CX
        KD = area(20480, 2, 512)
        KS = area(15360, HH, T)
        TOTE = modsb[:, 32:40]
        ZEROS = area(29696, 512)
        tsl = lambda t: slice(t * P, (t + 1) * P)
        hsl = lambda h: slice(h * P, (h + 1) * P)
        block = ctx.enter_context(nc.Block())

        @block.sync
        def _(sp):
            stream = A["stream"]
            for t in range(TT):
                sp.dma_start(hres[:, t, :], A["x"][0, t * P:(t + 1) * P, :]).then_inc(in_x, 16)
            sp.dma_start(const[:, :], A["const"]).then_inc(in_const, 16)
            sp.dma_start(cols[:, :], A["cols"]).then_inc(in_const, 16)
            sp.dma_start(rows[:, :], A["rows"].partition_broadcast(P)).then_inc(in_const, 16)
            sp.dma_start(small[:, 616:618].bitcast(I32), A["pos"]).then_inc(in_const, 16)
            for s in range(RING):
                sp.dma_start(ring[:, s, :], stream[s]).then_inc(ring_loaded[s], 16)
            with sp.Fori(1, N_RING // RING) as i:
                for s in range(RING):
                    sp.wait_ge(tiles_begun, i * RING + (s - RING + 2))
                    sp.dma_start(ring[:, s, :], stream[i * RING + s]).then_inc(ring_loaded[s], 16)
            sp.wait_ge(S["v_ready"], 1)
            for s in range(FRING):
                sp.dma_start(FR[:, s, :], stream[FFN0 + s]).then_inc(ffn_loaded[s], 16)
            with sp.Fori(1, N_FFN // FRING) as i:
                for s in range(FRING):
                    sp.wait_ge(tiles_begun, i * FRING + (FFN0 + s - FRING + 2))
                    sp.dma_start(FR[:, s, :], stream[i * FRING + (FFN0 + s)]).then_inc(ffn_loaded[s], 16)
            for t in range(TT):
                sp.wait_ge(S["out_ready"], t + 1)
                sp.dma_start(A["out"][0, t * P:(t + 1) * P, :], XN[:, t, :]).then_inc(out_done, 16)
            sp.wait_ge(out_done, 16 * TT)

        @block.gpsimd
        def _(pool):
            arrived(pool, ("oT", 1, 1))
            pool.wait_ge(S["adt_ready"], 1)
            for t in range(TT):
                pool.dma_start(MEMX[:, t, :], A["mem"][0, t * P:(t + 1) * P, :]).then_inc(in_mem, 16)
            arrived(pool, ("co", MH - 1))
            pool.dma_start(KEYS, A["keys"]).then_inc(in_keys, 16)
            for t in range(TT):
                pool.dma_start(CX[:, t, :], A["ctx"][0, t * P:(t + 1) * P, :]).then_inc(in_ctx, 16)
            pool.wait_ge(S["p_ready"], P)
            pool.dma_start(FIN1, A["fin1"].partition_broadcast(P)).then_inc(in_second, 16)
            pool.dma_start(R2, A["rows2"].partition_broadcast(P)).then_inc(in_second, 16)
            pool.dma_start(LEV[:, 0:14, :], A["levels"]).then_inc(in_second, 16)
            pool.dma_start(WSP, A["wsp"]).then_inc(in_second, 16)
            arrived(pool, ("x2T", 1, 1))
            pool.dma_start(GSPAN, A["span"]).then_inc(in_second, 16)
            freed(pool, ("gr", 1, 1, N_LEVELS - 1))
            pool.dma_start(FIN2, A["fin2"].partition_broadcast(P)).then_inc(in_second, 16)

        @block.tensor
        def _(pe):
            begun = [False]

            def mm(out, lhsT, rhs, start=True, stop=True):
                ins = nc.tensor.matmul(out, lhsT, rhs, start=start, stop=stop, skip_group_check=True)
                if begun[0]:
                    ins.then_inc(tiles_begun, 1)
                    begun[0] = False
                return ins

            def weights(g, turn=None):
                s, n = g % RING, g // RING
                pe.wait_ge(ring_loaded[s], 16 * (n + 1) if turn is None else turn * 16 + 16 * (n + 1))
                begun[0] = True
                return ring[:, s, :]

            def transposes(job, pairs):
                b = claim(job)
                for k, src in enumerate(pairs):
                    ins = nc.tensor.transpose(b[:, k * P:(k + 1) * P], src, ident)
                filled(ins, job)

            def token_block(sec, b, name, lhs):
                banks = [claim((name, b, t)) for t in range(TT)]
                for j in range(4):
                    w = weights(FIRST[sec] + 4 * b + j)
                    for t in range(TT):
                        for k in range(2):
                            ins = mm(banks[t], lhs[:, 2 * j + k, tsl(t)], w[:, k * 512:(k + 1) * 512],
                                     start=(j == 0 and k == 0), stop=(j == 3 and k == 1))
                        if j == 3:
                            filled(ins, (name, b, t))

            def feature_tile(g, job, rhs, turn=None, chunks=KC):
                b = claim(job, turn)
                for k in range(chunks):
                    if k % KC == 0:
                        w = weights(g + k // KC, turn)
                    ins = mm(b[:, 0:T], w[:, hsl(k % KC)], rhs[:, k, :], start=(k == 0), stop=(k == chunks - 1))
                filled(ins, job)

            def features_ready(name, chunks=2):
                for t in range(TT):
                    for h in range(chunks):
                        freed(pe, (name, t, h))

            def norm_transposes(name, src, n):
                for t in range(TT):
                    pe.wait_ge(S["xn_ready"], n * TT + t + 1)
                    for h in range(2):
                        transposes((name, t, h), [src[:, t, hsl(4 * h + k)] for k in range(4)])

            pe.wait_ge(in_const, 64)
            norm_transposes("xT", XN, 0)
            features_ready("xT")
            for b in range(4):
                token_block("in_tok", b, "tok", actT)
            with pe.Fori(0, 3) as i:
                for j in range(8):
                    feature_tile(FIRST["in_xbc"] + j, ("xbc", j), actT, i)
            pe.wait_ge(S["rope_ready"], 1)
            for t in range(TT):
                for h in range(2):
                    transposes(("qTr", t, h), [TOK[:, t, hsl(4 * h + k)] for k in range(4)])
            transposes(("kTr",), [TOK[:, t, 1024 + kv * P:1024 + (kv + 1) * P] for kv in range(KVH) for t in range(TT)])
            transposes(("iqTr",), [TOK[:, t, 1280 + b * P:1280 + (b + 1) * P] for b in range(2) for t in range(TT)])
            transposes(("ikTr",), [IKD[:, t, :] for t in range(TT)])
            for b in range(4):
                token_block("in_z", b, "z", actT)
            for name in (("qTr", 1, 1), ("kTr",), ("iqTr",), ("ikTr",)):
                freed(pe, name)
            for t in range(TT):
                for r in range(2):
                    b = claim(("idx", t, r))
                    rs = slice(r * IDH, (r + 1) * IDH)
                    for c in range(2):
                        ins = mm(b[:, c * T:(c + 1) * T], IQT[rs, c, tsl(t)], IKT[rs, :])
                    filled(ins, ("idx", t, r))
            with pe.Fori(0, 2) as i:
                for j in range(8):
                    feature_tile(FIRST["in_gate"] + j, ("gate", j), actT, i)
            for t in range(TT):
                w = P * (t + 1)
                for p in range(4):
                    b = claim(("lg", t, p))
                    for c in range(2):
                        h = 2 * p + c
                        ins = mm(b[:, c * T:c * T + w], QT[:, h, tsl(t)], KT[:, h // 4, 0:w])
                    filled(ins, ("lg", t, p))
            pe.wait_ge(S["xbc_ready"], 24)
            for t in range(TT):
                for q in range(4):
                    transposes(("xsTr", t, q), [XBC[:, 4 * q + k, tsl(t)] for k in range(4)])
            transposes(("BTr",), [XBC[:, 16 + g, 0:P] for g in range(SG)])
            pe.wait_ge(S["adt_ready"], 1)
            b = claim(("acs",))
            for c in range(TT):
                mm(b[:, c * 32:(c + 1) * 32], C("upto"), ADT[:, c, :])
            for c in range(TT):
                ins = mm(b[:, 64 + c * 32:64 + (c + 1) * 32], C("ones"), ADT[:, c, :])
            filled(ins, ("acs",))
            for t in range(TT):
                pe.wait_ge(S["attn_prob"], t + 1)
                blocks = [(s, h) for s in range(t + 1) for h in range(QH)]
                for n in range(2 * (t + 1)):
                    transposes(("PTr", t, n), [LG[t][:, h, tsl(s)] for s, h in blocks[4 * n:4 * n + 4]])
                for kv in range(KVH):
                    b = claim(("oT", t, kv))
                    for s in range(t + 1):
                        freed(pe, ("PTr", t, 2 * s + kv))
                        ins = mm(b, TOK[:, s, 1600 + kv * P:1600 + (kv + 1) * P],
                                 PT[:, s, 4 * kv:4 * kv + 4, :].rearrange("p h t -> p (h t)"),
                                 start=(s == 0), stop=(s == t))
                    filled(ins, ("oT", t, kv))
            for c in range(TT):
                b = claim(("cb", c))
                for g in range(SG):
                    ins = mm(b[:, hsl(g)], XBC[:, 16 + g, tsl(c)], XBC[:, 20 + g, tsl(c)])
                filled(ins, ("cb", c))
            groups = [(c, g) for c in range(TT) for g in range(SG)]
            for k in range(len(groups) + 1):
                if k < len(groups):
                    c, g = groups[k]
                    pe.wait_ge(S["adtb_ready"], k + 1)
                    for half in range(2):
                        b = claim(("row", c, g, half))
                        for j in range(4):
                            ins = mm(b[:, hsl(j)], ADTB[:, k % 2, 4 * half + j, :], C("upto"))
                        filled(ins, ("row", c, g, half))
                if k >= 1:
                    c, g = groups[k - 1]
                    if k == 1:
                        pe.wait_ge(S["xdtd_ready"], 1)
                        freed(pe, ("BTr",))
                    pe.wait_ge(S["m_ready"], k)
                    b = claim(("yd", c, g))
                    for j in range(8):
                        h = 8 * g + j
                        ins = mm(b[:, j * SP_:(j + 1) * SP_], EM[:, (k - 1) % 2, j, :],
                                 XS[:, c, h * SP_:(h + 1) * SP_])
                    filled(ins, ("yd", c, g))
                    if c == 0:
                        b = claim(("st", g))
                        filled(mm(b, BTOK[:, g, :], XDTD[:, g * 512:(g + 1) * 512]), ("st", g))
                    else:
                        freed(pe, ("st", g))
                        b = claim(("yo", g))
                        filled(mm(b, XBC[:, 20 + g, P:T], STATE[:, g, :]), ("yo", g))
            norm_transposes("mT", XN, 1)
            features_ready("mT")
            for n in range(8):
                feature_tile(FIRST["mem_k"] + n, ("mk", n), MT)
            for b in range(2):
                token_block("mem_v", b, "mv", MT)
            for t in range(TT):
                pe.wait_ge(S["xn_ready"], 2 * TT + t + 1)
                for q in range(4):
                    transposes(("yTr", t, q), [YT_[:, t, hsl(4 * q + k)] for k in range(4)])
            for kv in range(KVH):
                freed(pe, ("oT", 1, kv))
            features_ready("yTr", 4)
            for n in range(8):
                feature_tile(FIRST["merge"] + 3 * n, ("ma", n), AT)
                feature_tile(FIRST["merge"] + 3 * n + 1, ("ms", n), YT, chunks=16)
            pe.wait_ge(S["merged_ready"], 8)
            for b in range(2):
                token_block("w_out", b, "wo", MG)
            norm_transposes("a2T", XN, 3)
            features_ready("a2T")
            for n in range(8):
                feature_tile(FIRST["cross_q"] + n, ("cq", n), actT)
            for n in range(8):
                freed(pe, ("mk", n))
                freed(pe, ("cq", n))
            for t in range(TT):
                for p in range(2):
                    b = claim(("cl", t, p))
                    for c in range(2):
                        h = 2 * p + c
                        for k in range(2):
                            ins = mm(b[:, c * T:(c + 1) * T], CQT[:, 2 * h + k, tsl(t)], MKT[:, 2 * h + k, :],
                                     start=(k == 0), stop=(k == 1))
                    filled(ins, ("cl", t, p))
            for t in range(TT):
                pe.wait_ge(S["cprob"], t + 1)
                for m in range(TT):
                    transposes(("cP", t, m), [CL[:, h, tsl(m)] for h in range(MH)])
            for b in range(2):
                for t in range(TT):
                    freed(pe, ("mv", b, t))
                    freed(pe, ("cP", b, t))
            for h in range(MH):
                b = claim(("co", h))
                for c in range(2):
                    for m in range(TT):
                        ins = mm(b[:, c * T:(c + 1) * T], MV[:, m, h * MD + c * P:h * MD + (c + 1) * P],
                                 CPT[:, m, h, :], start=(m == 0), stop=(m == 1))
                filled(ins, ("co", h))
            for h in range(MH):
                freed(pe, ("co", h))
            for b in range(2):
                token_block("cross_out", b, "cw", COT)
            norm_transposes("a3T", XN, 4)
            features_ready("a3T")
            with pe.Fori(0, 2) as i:
                for j in range(8):
                    feature_tile(FIRST["peer_q"] + j, ("pq", j), actT, i)
            for j in range(8):
                freed(pe, ("pq", j), 1)
            pe.wait_ge(in_keys, 16)
            for t in range(TT):
                for q in range(4):
                    b = claim(("sk", t, q))
                    for j in range(4):
                        ins = mm(b[:, hsl(j)], QPT[:, 4 * q + j, tsl(t)], KEYS[:, 4 * q + j, :])
                    filled(ins, ("sk", t, q))
            pe.wait_ge(S["silu_c"], 1)
            with pe.Fori(0, 3) as i:
                for u in range(2):
                    b = claim(("ada", u), i)
                    for j in range(8):
                        s = (FIRST["ada"] + 8 * u + j) % RING
                        n = (FIRST["ada"] + 8 * u + j) // RING
                        pe.wait_ge(ring_loaded[s], i * 32 + 16 * (n + 1))
                        begun[0] = True
                        for k in range(KC):
                            ins = mm(b[:, 2 * j:2 * j + 2], ring[:, s, hsl(k)], c2s[:, k, :],
                                     start=(k == 0), stop=(k == KC - 1))
                    filled(ins, ("ada", u))
            norm_transposes("cT", XN, 5)
            pe.wait_ge(S["act_ready"], 4)
            for b in range(3):
                token_block("ctx", b, "cp", CXT)
            pe.wait_ge(S["ctx_f"], 1)
            for d in range(2):
                tri = C("after") if d == 0 else C("before")
                for t in range(TT):
                    b = claim(("ce", d, t))
                    far = (t == 0) if d == 0 else (t == 1)
                    ins = mm(b, tri, CLF[:, t, d * 512:(d + 1) * 512], start=True, stop=not far)
                    if far:
                        ins = mm(b, C("ones"), CLF[:, 1 - t, d * 512:(d + 1) * 512], start=False, stop=True)
                    filled(ins, ("ce", d, t))
            pe.wait_ge(S["ctx_kd"], 1)
            for d in range(2):
                b = claim(("cH", d))
                for h in range(HH):
                    for t in range(TT):
                        ins = mm(b[:, hsl(h)], CKK[:, t, d * 512 + h * P:d * 512 + (h + 1) * P],
                                 CPJ[:, t, 1024 + h * P:1024 + (h + 1) * P], start=(t == 0), stop=(t == 1))
                filled(ins, ("cH", d))
            for t in range(TT):
                pe.wait_ge(S["idx_ready"], t + 1)
                transposes(("eTr", t), [EAB[:, x, :] for x in range(3)])
            with pe.Fori(0, T // 8) as i:
                for u in range(2):
                    pe.wait_ge(S["onehot_ready"], i * 2 + (u + 1))
                    b = claim(("w", u), i)
                    for v in range(4):
                        ins = mm(b[:, hsl(v)], ONEHOT[:, u, v, 1, :], ONEHOT[:, u, v, 0, :])
                    filled(ins, ("w", u))
            for t in range(TT):
                for h in range(2):
                    b = claim(("y", t, h))
                    mm(b, ident, hres[:, t, h * 512:(h + 1) * 512], start=True, stop=False)

            def values(g, a, turn=None, last=False):
                w = weights(g, turn)
                pe.wait_ge(S["p_ready"], a + 1)
                par = parity[0]
                for t in range(TT):
                    for h in range(2):
                        cuts = (0, T, 512) if last and t == h == 0 else (0, 512)
                        for lo_, hi_ in zip(cuts, cuts[1:]):
                            ins = mm(bank(("y", t, h))[:, lo_:hi_], GATED[:, par, tsl(t)],
                                     w[:, h * 512 + lo_:h * 512 + hi_], start=False, stop=last)
                        if last:
                            filled(ins, ("y", t, h))
                if not last:
                    ins.then_inc(S["p_used"], 1)

            parity = [0]
            g0 = FIRST["experts"]
            feature_tile(g0, ("h0",), actT)
            with pe.Fori(0, 31) as i:
                for u in range(4):
                    feature_tile(g0 + 1 + 2 * u, ("h", u), actT, i)
                    parity[0] = u % 2
                    values(g0 + 2 + 2 * u, i * 4 + u, i)
            for u in range(3):
                a = 124 + u
                feature_tile(g0 + 1 + 2 * a, ("he", u), actT)
                parity[0] = a % 2
                values(g0 + 2 + 2 * a, a)
            parity[0] = 1
            values(g0 + 255, 127, last=True)
            norm_transposes("x2T", XN, 7)
            pe.wait_ge(S["act_ready"], 8)
            for b in range(7):
                token_block("in2", b, "p", actT)
            for t in range(TT):
                freed(pe, ("p", 3, t))
                transposes(("qT2", t), [PJ[:, t, 1536 + h * P:1536 + (h + 1) * P] for h in range(HH)])
            pe.wait_ge(S["g_k"], 1)
            for d in range(2):
                for t in range(TT):
                    transposes(("kT2", d, t), [K2[:, t, d * 512 + h * P:d * 512 + (h + 1) * P] for h in range(HH)])
            pe.wait_ge(S["g_logf"], 1)
            for d in range(2):
                b = claim(("as", d))
                filled(mm(b, C("after") if d == 0 else C("before"), LF[:, d, d * 512:(d + 1) * 512]), ("as", d))
            b = claim(("tot",))
            for d in range(2):
                for h in range(HH):
                    ins = mm(b[:, d * 4 + h:d * 4 + h + 1], LF[:, d, d * 512 + h * P:d * 512 + (h + 1) * P],
                             C("ones")[:, 0:1])
            filled(ins, ("tot",))
            for d in range(2):
                pe.wait_ge(S["g_kd"], d + 1)
                b = claim(("adv", d))
                for h in range(HH):
                    ins = mm(b[:, hsl(h)], KD[:, d, hsl(h)], PJ[:, d, 1024 + h * P:1024 + (h + 1) * P])
                filled(ins, ("adv", d))
            pe.wait_ge(in_second, 5 * 16)
            pe.wait_ge(S["g_H"], 1)
            for t in range(TT):
                freed(pe, ("qT2", t))
            for t in range(TT):
                b = claim(("dg", t))
                for h in range(HH):
                    ins = mm(b[:, hsl(h)], KS[:, h, tsl(t)], Q2T[:, h, tsl(t)])
                filled(ins, ("dg", t))
                for d in range(2):
                    for h in range(HH):
                        for half in range(2):
                            b = claim(("e", t, d, h, half))
                            filled(mm(b, LF[:, t, d * 512 + h * P:d * 512 + (h + 1) * P],
                                      GSPAN[:, d, half * 512:(half + 1) * 512]), ("e", t, d, h, half))
                    pe.wait_ge(S["z_made"], 2 * t + d + 1)
                    for lev in range(N_LEVELS):
                        b = claim(("gr", t, d, lev))
                        for h in range(HH):
                            ins = mm(b[:, hsl(h)], ZK[:, h, lev, :], ZQ[:, h, lev, :])
                        filled(ins, ("gr", t, d, lev))
                freed(pe, ("gr", t, 1, N_LEVELS - 1))
                b = claim(("o", t))
                hf = h0[:, 0] if t == 0 else HS[:, 0]
                hb = h0[:, 1] if t == 1 else HS[:, 1]
                for h in range(HH):
                    mm(b[:, hsl(h)], SM[:, h, :], PJ[:, t, 1024 + h * P:1024 + (h + 1) * P], start=True, stop=False)
                    mm(b[:, hsl(h)], ZP[:, 0, h, :], hf[:, h, :], start=False, stop=False)
                    ins = mm(b[:, hsl(h)], ZP[:, 1, h, :], hb[:, h, :], start=False, stop=True)
                filled(ins, ("o", t))
            for t in range(TT):
                pe.wait_ge(S["v_ready"], 1)
                b = claim(("sg", t))
                for h in range(HH):
                    ins = mm(b[:, hsl(h)], WSP[:, h, :], PJ[:, t, 3072 + h * P:3072 + (h + 1) * P])
                filled(ins, ("sg", t))
            pe.wait_ge(S["gdiag"], 1)
            for r in range(4):
                b = claim(("gb", r))
                filled(mm(b, C("ones"), GBD[:, r // 2, 4 * (r % 2):4 * (r % 2) + 4, :].rearrange("p k n -> p (k n)")),
                       ("gb", r))
            for t in range(TT):
                pe.wait_ge(S["oc_ready"], t + 1)
                for h in range(2):
                    transposes(("ocT", t, h), [OC[:, t, hsl(4 * h + k)] for k in range(4)])
            for t in range(TT):
                for h in range(2):
                    freed(pe, ("ocT", t, h))
            for b in range(2):
                token_block("out2", b, "w2", actT)
            norm_transposes("x3T", XN, 8)
            pe.wait_ge(S["act_ready"], 12)
            def ffn_weights(r, turn=None):
                s, n = r % FRING, r // FRING
                pe.wait_ge(ffn_loaded[s], 16 * (n + 1) if turn is None else turn * 16 + 16 * (n + 1))
                begun[0] = True
                return FR[:, s, :]

            def channels(r, job, turn=None):
                b = claim(job, turn)
                w = ffn_weights(r, turn)
                for k in range(KC):
                    ins = mm(b[:, 0:T], w[:, hsl(k)], actT[:, k, :], start=(k == 0), stop=(k == KC - 1))
                filled(ins, job)

            def down(r, job, par, turn=None, job_turn=None, last=False):
                w = ffn_weights(r, turn)
                freed(pe, job, job_turn)
                for t in range(TT):
                    for h in range(2):
                        cuts = (0, T, 512) if last and t == h == 0 else (0, 512)
                        for lo_, hi_ in zip(cuts, cuts[1:]):
                            ins = mm(bank(("f", t, h))[:, lo_:hi_], HF[:, par, tsl(t)],
                                     w[:, h * 512 + lo_:h * 512 + hi_], start=False, stop=last)
                        if last:
                            filled(ins, ("f", t, h))
                if not last:
                    ins.then_inc(S["ffn_used"], 1)

            pe.wait_ge(S["zeros_ready"], 1)
            for t in range(TT):
                for h in range(2):
                    mm(claim(("f", t, h)), ident, ZEROS, start=True, stop=False)
            channels(0, ("g0",))
            channels(1, ("a0",))
            with pe.Fori(0, (FC - 2) // 2) as i:
                for u in range(2):
                    channels(2 + 3 * u, ("ga", 2 * u), i)
                    channels(3 + 3 * u, ("ga", 2 * u + 1), i)
                    down(4 + 3 * u, ("a0",) if u == 0 else ("ga", 1), u, i, i)
            channels(62, ("ge",))
            channels(63, ("ae",))
            down(64, ("ga", 3), 0, job_turn=(FC - 2) // 2 - 1)
            down(65, ("ae",), 1, last=True)

        @block.scalar
        def _(act):
            step = Chain(act, S["act_step"])

            def func(out, in_, f, **kw):
                return nc.scalar.activation(out, in_, f, **kw)

            def evacuate(job, out, turn=None, f=ACT.Copy, src=None, **kw):
                b = arrived(act, job, turn)
                free(func(out, b if src is None else src(b), f, **kw), job)

            def norm(n, x, junk, ready=None):
                for t in range(TT):
                    if ready is not None:
                        ready(t)
                    if n == 2 and t == 1:
                        act.wait_ge(S["norm_sq"], 2 * n + 1)
                    func(junk(t), x(t), ACT.Square, accum_out=stat[:, 0, n, t:t + 1]).then_inc(S["norm_sq"], 1)
                act.wait_ge(S["norm_ms"], n + 1)
                func(stat[:, 2, n, :], stat[:, 1, n, :], ACT.Sqrt).then_inc(S["norm_root"], 1)

            def halves(b):
                return b.rearrange("p (c t) -> p c t", c=2)

            def quarters(b):
                return b.rearrange("p (c t) -> p c t", c=4)

            norm(0, lambda t: hres[:, t, :], lambda t: XN[:, t, :], lambda t: act.wait_ge(in_x, 16 * TT))
            act.wait_ge(S["rope_arg"], 1)
            func(ROPE.rearrange("p a b c -> p (a b c)"), ROPET[:, 4, :], ACT.Sin).then_inc(S["rope_sin"], 1)
            for b in range(4):
                for t in range(TT):
                    evacuate(("tok", b, t), TOK[:, t, b * 512:(b + 1) * 512])
            act.wait_ge(S["dt_abs"], 1)
            step(func(DTS, DTS, ACT.Exp, scale=-1.0))
            func(DTL, DTS, ACT.Ln, bias=1.0).then_inc(S["dt_l"], 1)
            func(NEGA, row("a_log"), ACT.Exp).then_inc(S["neg_a"], 1)
            with act.Fori(0, 3) as i:
                for j in range(8):
                    freed(act, ("xbc", j), i)
                    c = i * 8 + j
                    func(XBC[:, c, :], XBC[:, c, :], ACT.Silu).then_inc(S["xbc_ready"], 1)
            for t in range(TT):
                for h in range(2):
                    evacuate(("qTr", t, h), QT[:, 4 * h:4 * h + 4, tsl(t)], src=quarters)
            evacuate(("kTr",), KT.rearrange("p k t -> p (k t)"))
            evacuate(("iqTr",), IQT.rearrange("p k t -> p (k t)"))
            evacuate(("ikTr",), IKT, src=lambda b: b[:, 0:T])
            for b in range(4):
                for t in range(TT):
                    evacuate(("z", b, t), ZT[:, t, b * 512:(b + 1) * 512], f=ACT.Silu)
            for t in range(TT):
                for r in range(2):
                    evacuate(("idx", t, r), RELU[:, 2 * t + r], f=ACT.Relu, scale=IDH ** -0.5, src=halves)
            with act.Fori(0, 2) as i:
                for j in range(8):
                    evacuate(("gate", j), GT[:, i * 8 + j, :], i, f=ACT.Sigmoid, src=lambda b: b[:, 0:T])
            for t in range(TT):
                act.wait_ge(S["attn_masked"], t + 1)
                for h in range(QH):
                    ins = func(LG[t][:, h, :], LG[t][:, h, :], ACT.Exp, bias=smx[:, t, 1, h:h + 1],
                               scale=DH ** -0.5, accum_out=smx[:, t, 2, h:h + 1])
                ins.then_inc(S["attn_exp"], 1)
            for t in range(TT):
                for q in range(4):
                    evacuate(("xsTr", t, q), XS[:, t, q * 512:(q + 1) * 512])
            evacuate(("BTr",), BTOK.rearrange("p g n -> p (g n)"))
            act.wait_ge(S["acs_ready"], 1)
            step(func(EAC.rearrange("p c h -> p (c h)"), lo(320, 384), ACT.Exp))
            func(DTE, DTE, ACT.Exp).then_inc(S["acs_exp"], 1)
            for t in range(TT):
                for n in range(2 * (t + 1)):
                    s, h = n // 2, 4 * (n % 2)
                    if t == 1 and n == 0:
                        arrived(act, ("oT", 0, 1))
                    evacuate(("PTr", t, n), PT[:, s, h:h + 4, :], src=quarters)
                for kv in range(KVH):
                    evacuate(("oT", t, kv), AT[:, 4 * kv:4 * kv + 4, tsl(t)], src=quarters)
            for k in range(TT * SG):
                for half in range(2):
                    freed(act, ("row", k // SG, k % SG, half))
                func(EM[:, k % 2], EM[:, k % 2], ACT.Exp).then_inc(S["seg_exp"], 1)
            norm(1, lambda t: MEMX[:, t, :], lambda t: XN[:, t, :], lambda t: act.wait_ge(in_mem, 16 * TT))
            norm(2, lambda t: YT_[:, t, :], lambda t: EM[:, :, :, :].rearrange("p u h l -> p (u h l)"),
                 lambda t: act.wait_ge(S["y_ready"], t + 1))
            for n in range(8):
                evacuate(("mk", n), MKT[:, n, :], src=lambda b: b[:, 0:T])
            for b in range(2):
                for t in range(TT):
                    evacuate(("mv", b, t), MV[:, t, b * 512:(b + 1) * 512])
            norm(3, lambda t: hres[:, t, :], lambda t: XN[:, t, :], lambda t: [freed(act, ("wo", b, t)) for b in range(2)])
            for n in range(8):
                evacuate(("cq", n), CQT[:, n, :], src=lambda b: b[:, 0:T])
            for t in range(TT):
                act.wait_ge(S["cl_ready"], t + 1)
                if t == 1:
                    arrived(act, ("cP", 0, 1))
                for p in range(2):
                    b = arrived(act, ("cl", t, p))
                    for c in range(2):
                        h = 2 * p + c
                        ins = func(CL[:, h, :], b[:, c * T:(c + 1) * T], ACT.Exp, bias=smx[:, t, 1, h:h + 1],
                                   scale=MD ** -0.5, accum_out=smx[:, t, 2, h:h + 1])
                    free(ins, ("cl", t, p))
                for m in range(TT):
                    evacuate(("cP", t, m), CPT[:, m, :, tsl(t)], src=quarters)
            for h in range(MH):
                evacuate(("co", h), COT[:, 2 * h:2 * h + 2, :], src=halves)
            norm(4, lambda t: hres[:, t, :], lambda t: XN[:, t, :], lambda t: [freed(act, ("cw", b, t)) for b in range(2)])
            func(c2s[:, :, :].rearrange("p k c -> p (k c)"), col("c2"), ACT.Silu).then_inc(S["silu_c"], 1)
            with act.Fori(0, 2) as i:
                for j in range(8):
                    evacuate(("pq", j), QPT[:, i * 8 + j, :], i, src=lambda b: b[:, 0:T])
            for t in range(TT):
                for q in range(4):
                    evacuate(("sk", t, q), SK[:, t, 4 * q:4 * q + 4, :], src=quarters)
            with act.Fori(0, 3) as i:
                for u in range(2):
                    evacuate(("ada", u), mods[:, bass.ds(i * 16 + 8 * u, 8), :], i,
                             src=lambda b: b[:, 0:16].rearrange("p (n c) -> p n c", c=2))
            norm(5, lambda t: CX[:, t, :], lambda t: XN[:, t, :], lambda t: act.wait_ge(in_ctx, 16 * TT))
            for b in range(3):
                for t in range(TT):
                    evacuate(("cp", b, t), CPJ[:, t, b * 512:(b + 1) * 512])
            act.wait_ge(S["ctx_abs"], 1)
            step(func(CLF, CLF, ACT.Exp, scale=-1.0))
            func(CLF, CLF, ACT.Ln, bias=1.0).then_inc(S["ctx_l"], 1)
            act.wait_ge(S["ctx_nk"], 1)
            func(CKK, CKK, ACT.Exp, scale=-1.0).then_inc(S["ctx_k"], 1)
            for d in range(2):
                for t in range(TT):
                    evacuate(("ce", d, t), CEX[:, t, d * 512:(d + 1) * 512], f=ACT.Exp)
            for d in range(2):
                evacuate(("cH", d), h0[:, d], src=quarters)
            for t in range(TT):
                act.wait_ge(S["gate_sc"], t + 1)
                func(EAB[:, 2, :], EAB[:, 2, :], ACT.Exp).then_inc(S["gate_exp"], 1)
                evacuate(("eTr", t), slots[:, :, tsl(t)], src=lambda b: b[:, 0:384].rearrange("p (x n) -> p x n", x=3))
            with act.Fori(0, T // 8) as i:
                for u in range(2):
                    evacuate(("w", u), WT[:, :, bass.ds(i * 8 + 4 * u, 4)].rearrange("p n v -> p v n"), i, src=quarters)
            func(GELU[:, 0, :], arrived(act, ("h0",))[:, 0:T], ACT.Gelu).then_inc(bank_free[4], 1)
            with act.Fori(0, 31) as i:
                for u in range(4):
                    b = arrived(act, ("h", u), i)
                    act.wait_ge(S["p_ready"], i * 4 + u)
                    free(func(GELU[:, (u + 1) % 2, :], b[:, 0:T], ACT.Gelu), ("h", u))
            for u in range(3):
                a = 125 + u
                b = arrived(act, ("he", u))
                act.wait_ge(S["p_ready"], a - 1)
                free(func(GELU[:, a % 2, :], b[:, 0:T], ACT.Gelu), ("he", u))
            for t in range(TT):
                for h in range(2):
                    evacuate(("y", t, h), hres[:, t, h * 512:(h + 1) * 512])
            for t in range(TT):
                freed(act, ("y", t, 1))
            norm(6, lambda t: hres[:, t, :], lambda t: XN[:, t, :], lambda t: act.wait_ge(S["p_ready"], P))
            norm(7, lambda t: hres[:, t, :], lambda t: XN[:, t, :], lambda t: act.wait_ge(S["x2_ready"], 2))
            for b in range(3):
                for t in range(TT):
                    evacuate(("p", b, t), PJ[:, t, b * 512:(b + 1) * 512])
            for b in (3, 4):
                for t in range(TT):
                    evacuate(("p", b, t), PJ[:, t, b * 512:(b + 1) * 512], f=ACT.Silu)
            for b in (5, 6):
                for t in range(TT):
                    evacuate(("p", b, t), PJ[:, t, b * 512:(b + 1) * 512], f=ACT.Gelu)
            act.wait_ge(S["g_abs"], 1)
            step(func(LF, LF, ACT.Exp, scale=-1.0))
            func(LF, LF, ACT.Ln, bias=1.0).then_inc(S["g_l"], 1)
            act.wait_ge(S["g_nk"], 1)
            func(K2, K2, ACT.Exp, scale=-1.0).then_inc(S["g_k"], 1)
            for t in range(TT):
                evacuate(("qT2", t), Q2T[:, :, tsl(t)], src=quarters, scale=P ** -0.5)
            for d in range(2):
                for t in range(TT):
                    evacuate(("kT2", d, t), K2T[:, d, :, tsl(t)], src=quarters)
            for d in range(2):
                evacuate(("as", d), KD[:, d, :], f=ACT.Exp)
            evacuate(("tot",), TOTE, f=ACT.Exp, src=lambda b: b[:, 0:8])
            act.wait_ge(S["g_H"], 1)
            for t in range(TT):
                for d in range(2):
                    if t or d:
                        arrived(act, ("gr", t, 0, 6) if d else ("gr", t - 1, 1, 6))
                    for h in range(HH):
                        for half in range(2):
                            evacuate(("e", t, d, h, half), ZQ[:, h, 4 * half:4 * half + 4, :], f=ACT.Exp, src=quarters)
            act.wait_ge(S["o_ms"], 1)
            func(gst[:, 2], gst[:, 1], ACT.Sqrt).then_inc(S["o_root"], 1)
            act.wait_ge(S["gdiag"], 1)
            for r in range(4):
                evacuate(("gb", r), GB[:, r // 2, 512 * (r % 2):512 * (r % 2) + 512])
            for t in range(TT):
                for h in range(2):
                    evacuate(("ocT", t, h), actT[:, 4 * h:4 * h + 4, tsl(t)], src=quarters)
            norm(8, lambda t: hres[:, t, :], lambda t: XN[:, t, :], lambda t: act.wait_ge(S["x3_ready"], 4))

            def ffn_gate(job, par, turn=None):
                evacuate(job, GC[:, par, :], turn, src=lambda b: b[:, 0:T])

            def ffn_gelu(c, par):
                act.wait_ge(S["ffn_conv"], c + 1)
                func(GE[:, par, :], CV[:, par, :], ACT.Gelu).then_inc(S["ffn_gelu"], 1)

            ffn_gate(("g0",), 0)
            with act.Fori(0, (FC - 2) // 2) as i:
                for u in range(2):
                    ffn_gelu(i * 2 + u, u)
                    ffn_gate(("ga", 2 * u), (u + 1) % 2, i)
            ffn_gelu(FC - 2, 0)
            ffn_gate(("ge",), 1)
            ffn_gelu(FC - 1, 1)
            norm(9, lambda t: hres[:, t, :], lambda t: XN[:, t, :], lambda t: act.wait_ge(S["x4_ready"], 4))

        @block.vector
        def _(dve):
            V = nc.vector
            step = Chain(dve, S["dve_step"])
            ts, tt, stt, cp = V.tensor_scalar, V.tensor_tensor, V.scalar_tensor_tensor, V.tensor_copy

            def signal(ins, name, wait=None):
                ins.then_inc(S[name], 1)
                if wait is not None:
                    dve.wait_ge(S[name], wait)

            def scale_rows(n, width, x, out, gain=None):
                dve.wait_ge(S["norm_sq"], 2 * n + 2)
                signal(ts(stat[:, 1, n, :], stat[:, 0, n, :], 1.0 / width, EPS, ALU.mult, ALU.add), "norm_ms")
                dve.wait_ge(S["norm_root"], n + 1)
                step(V.reciprocal(stat[:, 3, n, :], stat[:, 2, n, :]))
                for t in range(TT):
                    signal(ts(out(t), x(t), stat[:, 3, n, t:t + 1], None, ALU.mult), "xn_ready")

            def features(name, out, gain, shift=None, chunks=2):
                for t in range(TT):
                    for h in range(chunks):
                        b = arrived(dve, (name, t, h)).rearrange("p (k n) -> p k n", k=4)
                        o = out[:, 4 * h:4 * h + 4, tsl(t)]
                        free(tt(o, b, bc(gain[:, 4 * h:4 * h + 4], 2, P), ALU.mult), (name, t, h))
                        if shift is not None:
                            freed(dve, (name, t, h))
                            signal(tt(o, o, bc(shift[:, 4 * h:4 * h + 4], 2, P), ALU.add), "act_ready")

            dve.wait_ge(in_const, 64)
            F = ROPET[:, 0, 0:48].rearrange("p (t f) -> p t f", t=TT)
            posf = ROPET[:, 3, 0:2]
            step(cp(posf, small[:, 616:618].bitcast(I32)))
            step(tt(F, bc(posf, 2, 24), bc(C("freq"), 1, TT), ALU.mult))
            ang = ROPET[:, 0, 0:48]
            for s, (q, shift) in enumerate(((0.0, 0.0), (0.25, float(np.pi / 2)))):
                k = ROPET[:, 1 + s, 0:48]
                r = ROPET[:, 4, 48 * s:48 * s + 48]
                step(ts(k, ang, float(1 / (2 * np.pi)), q, ALU.mult, ALU.add))
                step(ts(k, k, 12582912.0, None, ALU.add))
                step(ts(k, k, -12582912.0, None, ALU.add))
                step(stt(r, k, -TWO_PI[0], ang, ALU.mult, ALU.add))
                step(stt(r, k, -TWO_PI[1], r, ALU.mult, ALU.add))
                step(stt(r, k, -TWO_PI[2], r, ALU.mult, ALU.add))
                step(ts(r, r, shift, float(np.float32(3.1415925)), ALU.add, ALU.min))
                ins = ts(r, r, float(np.float32(-3.1415925)), None, ALU.max)
                if s == 0:
                    step(ins)
            signal(ins, "rope_arg")
            scale_rows(0, D, lambda t: hres[:, t, :], lambda t: XN[:, t, :])
            features("xT", actT, col("g_mix"))
            for b in range(4):
                for t in range(TT):
                    freed(dve, ("tok", b, t))
            dve.wait_ge(S["rope_sin"], 1)
            for t in range(TT):
                for a, b, hd, heads, f0 in ((0, 1280, DH, 10, 0), (1280, 1600, IDH, 5, 16)):
                    half = hd // 8
                    x = TOK[:, t, a:b].rearrange("p (h d) -> p h d", d=hd)
                    x1, x2 = x[:, :, 0:half], x[:, :, half:2 * half]
                    sin = bc(ROPE[:, 0, t, f0:f0 + half], 1, heads)
                    cos = bc(ROPE[:, 1, t, f0:f0 + half], 1, heads)
                    n = heads * half
                    m = [RT[:, k // 2, (k % 2) * 160:(k % 2) * 160 + n].rearrange("p (h d) -> p h d", d=half)
                         for k in range(4)]
                    tt(m[0], x1, cos, ALU.mult)
                    tt(m[1], x2, sin, ALU.mult)
                    tt(m[2], x2, cos, ALU.mult)
                    step(tt(m[3], x1, sin, ALU.mult))
                    step(tt(x1, m[0], m[1], ALU.subtract))
                    step(tt(x2, m[2], m[3], ALU.add))
                step(cp(IKD[:, t, :].rearrange("p (r d) -> p r d", r=2), bc(TOK[:, t, 1536:1600], 1, 2)))
            ins = ts(IW, TOK[:, :, 1856:1860], IH ** -0.5, None, ALU.mult)
            signal(ins, "rope_ready", 1)
            step(tt(DT, TOK[:, :, 1860:1892], bc(row("dt_bias"), 1, TT), ALU.add))
            signal(stt(DTS, DT, -1.0, DT, ALU.mult, ALU.max), "dt_abs")
            dve.wait_ge(S["dt_l"], 1)
            dve.wait_ge(S["neg_a"], 1)
            step(stt(DT, DT, 0.0, DTL, ALU.max, ALU.add))
            signal(stt(ADT, DT, -1.0, bc(NEGA, 1, TT), ALU.mult, ALU.mult), "adt_ready", 1)
            with dve.Fori(0, 3) as i:
                for j in range(8):
                    b = arrived(dve, ("xbc", j), i)
                    o = XBC[:, i * 8 + j, :]
                    wcol = lambda k: col("conv_w")[:, bass.ds(i * 32 + 4 * j + k, 1)]
                    base = i * 24 + (step.c.n + 3 * j)
                    ts(o, b[:, 0:T], wcol(3), col("conv_b")[:, bass.ds(i * 8 + j, 1)], ALU.mult,
                       ALU.add).then_inc(step.c.sem, 1)
                    for m, k in enumerate((2, 1)):
                        dve.wait_ge(step.c.sem, base + (1 + m))
                        stt(o[:, 3 - k:T], b[:, 0:T - 3 + k], wcol(k), o[:, 3 - k:T], ALU.mult,
                            ALU.add).then_inc(step.c.sem, 1)
                    dve.wait_ge(step.c.sem, base + 3)
                    free(stt(o[:, 3:T], b[:, 0:T - 3], wcol(0), o[:, 3:T], ALU.mult, ALU.add), ("xbc", j))
            step.c.n += 72
            best = [smx[:, 0, 0, :], smx[:, 1, 0, :]]
            for t in range(TT):
                w = P * (t + 1)
                sc, left = SC[:, 2 * t, 0:w], SC[:, 2 * t + 1, 0:w]
                for r in range(2):
                    freed(dve, ("idx", t, r))
                step(ts(sc, RELU[:, 2 * t, 0, 0:w], IW[:, t, 0:1], None, ALU.mult))
                for h in range(1, IH):
                    step(stt(sc, RELU[:, 2 * t + h % 2, h // 2, 0:w], IW[:, t, h:h + 1], sc, ALU.mult, ALU.add))
                step(tt(sc[:, w - P:w], sc[:, w - P:w], C("causal"), ALU.add))
                for n in range(TOPK // 8):
                    src = sc if n == 0 else left
                    step(V.max(best[t], src))
                    step(V.match_replace(out=left, in_to_replace=best[t], in_values=src, imm_value=TAKEN))
                step(tt(left, left, sc, ALU.not_equal))
                step(stt(left, sc, -1.0e38, left, ALU.is_gt, ALU.mult))
                step(ts(left, left, -OFF, OFF, ALU.mult, ALU.add))
            for t in range(TT):
                w = P * (t + 1)
                for p in range(4):
                    b = arrived(dve, ("lg", t, p)).rearrange("p (c n) -> p c n", c=2)
                    free(tt(LG[t][:, 2 * p:2 * p + 2, :], b[:, :, 0:w], bc(SC[:, 2 * t + 1, 0:w], 1, 2), ALU.add),
                         ("lg", t, p))
                for p in range(4):
                    freed(dve, ("lg", t, p))
                step(V.tensor_reduce(smx[:, t, 0, :], LG[t], AX.X, ALU.max))
                signal(ts(smx[:, t, 1, :], smx[:, t, 0, :], -(DH ** -0.5), None, ALU.mult), "attn_masked")
            for t in range(TT):
                dve.wait_ge(S["attn_exp"], t + 1)
                step(V.reciprocal(smx[:, t, 3, :], smx[:, t, 2, :]))
                signal(tt(LG[t], LG[t], bc(smx[:, t, 3, :], 2, P * (t + 1)), ALU.mult), "attn_prob")
            b = arrived(dve, ("acs",))
            free(cp(ACS, b[:, 0:128].rearrange("p (c h) -> p c h", c=4)), ("acs",))
            freed(dve, ("acs",))
            signal(tt(DTE, ACS[:, 2, :], ACS[:, 0, :], ALU.subtract), "acs_ready")
            for t in range(TT):
                for q in range(4):
                    freed(dve, ("xsTr", t, q))
            freed(dve, ("PTr", 1, 3))
            heads = lambda ap: ap.rearrange("p (h d) -> p h d", d=SP_)
            for t in range(TT):
                tt(heads(YT_[:, t, :]), heads(XS[:, t, :]), bc(row("d_skip"), 2, SP_), ALU.mult)
            for t in range(TT):
                ins = tt(heads(XS[:, t, :]), heads(XS[:, t, :]), bc(DT[:, t, :], 2, SP_), ALU.mult)
            step(ins)
            dve.wait_ge(S["acs_exp"], 1)
            signal(tt(heads(XDTD), heads(XS[:, 0, :]), bc(DTE, 2, SP_), ALU.mult), "xdtd_ready")
            for kv in range(KVH):
                arrived(dve, ("oT", 1, kv))
            for c in range(TT):
                b = arrived(dve, ("cb", c)).rearrange("p (g l) -> p g l", g=SG)
                free(tt(CBM[:, c], b, bc(C("upto"), 1, SG), ALU.mult), ("cb", c))
                freed(dve, ("cb", c))
            n_groups = TT * SG

            def adt_rows(k):
                c, g = k // SG, k % SG
                signal(cp(ADTB[:, k % 2], bc(ADT[:, c, 8 * g:8 * g + 8], 2, P)), "adtb_ready")

            adt_rows(0)
            for k in range(n_groups + 1):
                if k + 1 < n_groups:
                    adt_rows(k + 1)
                if k < n_groups:
                    c, g = k // SG, k % SG
                    for half in range(2):
                        b = arrived(dve, ("row", c, g, half))
                        for j in range(4):
                            h = 8 * g + 4 * half + j
                            ins = ts(EM[:, k % 2, 4 * half + j, :], b[:, hsl(j)], ACS[:, c, h:h + 1], 0.0,
                                     ALU.subtract, ALU.min)
                        free(ins, ("row", c, g, half))
                if k >= 1:
                    c, g = (k - 1) // SG, (k - 1) % SG
                    gs = slice(g * 512, (g + 1) * 512)
                    if c == 0:
                        b = arrived(dve, ("yd", c, g))
                        free(tt(YT_[:, 0, gs], YT_[:, 0, gs], b, ALU.add), ("yd", c, g))
                        free(cp(STATE[:, g, :], arrived(dve, ("st", g))), ("st", g))
                    else:
                        b = arrived(dve, ("yo", g))
                        free(tt(heads(XDTD[:, gs]), heads(b), bc(EAC[:, 1, 8 * g:8 * g + 8], 2, SP_), ALU.mult),
                             ("yo", g))
                        freed(dve, ("yo", g))
                        step(tt(YT_[:, 1, gs], YT_[:, 1, gs], XDTD[:, gs], ALU.add))
                        b = arrived(dve, ("yd", c, g))
                        free(tt(YT_[:, 1, gs], YT_[:, 1, gs], b, ALU.add), ("yd", c, g))
                if k < n_groups:
                    c, g = k // SG, k % SG
                    dve.wait_ge(S["seg_exp"], k + 1)
                    signal(tt(EM[:, k % 2], EM[:, k % 2], bc(CBM[:, c, g, :], 1, 8), ALU.mult), "m_ready")
            scale_rows(1, D, lambda t: MEMX[:, t, :], lambda t: XN[:, t, :])
            features("mT", MT, col("g_mem"))
            for b in range(4):
                for t in range(TT):
                    freed(dve, ("z", b, t))
            for g in range(SG):
                freed(dve, ("yd", 1, g))
            for t in range(TT):
                signal(tt(YT_[:, t, :], YT_[:, t, :], ZT[:, t, :], ALU.mult), "y_ready")
            scale_rows(2, SD, lambda t: YT_[:, t, :], lambda t: YT_[:, t, :])
            features("yTr", YT, col("g_ssd"), chunks=4)
            for j in range(8):
                freed(dve, ("gate", j), 1)
            for n in range(8):
                part = area(28672 + T * (n % 2), T)
                free(tt(part, GT[:, n, :], arrived(dve, ("ma", n))[:, 0:T], ALU.mult), ("ma", n))
                free(tt(MG[:, n, :], GT[:, 8 + n, :], arrived(dve, ("ms", n))[:, 0:T], ALU.mult), ("ms", n))
                freed(dve, ("ma", n))
                freed(dve, ("ms", n))
                signal(tt(MG[:, n, :], MG[:, n, :], part, ALU.add), "merged_ready")

            def add_residual(name):
                for b in range(2):
                    for t in range(TT):
                        h = hres[:, t, b * 512:(b + 1) * 512]
                        free(tt(h, h, arrived(dve, (name, b, t)), ALU.add), (name, b, t))
                for b in range(2):
                    for t in range(TT):
                        freed(dve, (name, b, t))

            add_residual("wo")
            scale_rows(3, D, lambda t: hres[:, t, :], lambda t: XN[:, t, :])
            features("a2T", actT, col("g_cross"))
            for t in range(TT):
                for p in range(2):
                    b = arrived(dve, ("cl", t, p)).rearrange("p (c n) -> p c n", c=2)
                    ins = V.tensor_reduce(smx[:, t, 0, 2 * p:2 * p + 2], b, AX.X, ALU.max)
                step(ins)
                signal(ts(smx[:, t, 1, 0:4], smx[:, t, 0, 0:4], -(MD ** -0.5), None, ALU.mult), "cl_ready")
                for p in range(2):
                    freed(dve, ("cl", t, p))
                step(V.reciprocal(smx[:, t, 3, 0:4], smx[:, t, 2, 0:4]))
                signal(tt(CL, CL, bc(smx[:, t, 3, 0:4], 2, T), ALU.mult), "cprob")
            add_residual("cw")
            scale_rows(4, D, lambda t: hres[:, t, :], lambda t: XN[:, t, :])
            features("a3T", actT, col("g_ffn"))

            def top16(groups, src, work, val, idx):
                for g in groups:
                    ins = V.max(val(g)[:, 0:8], src(g))
                step(ins)
                for g in groups:
                    V.max_index(idx(g)[:, 0:8], val(g)[:, 0:8], src(g))
                    ins = V.match_replace(out=work(g), in_to_replace=val(g)[:, 0:8], in_values=src(g),
                                          imm_value=TAKEN)
                step(ins)
                for g in groups:
                    ins = V.max(val(g)[:, 8:16], work(g))
                step(ins)
                for g in groups:
                    ins = V.max_index(idx(g)[:, 8:16], val(g)[:, 8:16], work(g))
                step(ins)

            idxu = TOPI.bitcast(U32)
            sciu = SCI.bitcast(U32)
            ciau = CIA.bitcast(U32)

            def best_keys(t):
                for q in range(4):
                    freed(dve, ("sk", t, q))
                top16(range(16), lambda g: SK[:, t, g, :], lambda g: SK2[:, g, :], lambda g: TOPV[:, g, :],
                      lambda g: idxu[:, g, :])

            def best_pairs(t):
                v = TOPV.rearrange("p (h x) k -> p h x k", x=2)
                step(tt(CAND.rearrange("p h (i j) -> p h i j", j=PTOP), bc(v[:, :, 0, :], 3, PTOP),
                        bc(v[:, :, 1, :], 2, PTOP), ALU.add))
                top16(range(PH), lambda g: CAND[:, g, :], lambda g: CAND2[:, g, :], lambda g: SCV[:, g, :],
                      lambda g: sciu[:, g, :])
                flat = sciu.rearrange("p h k -> p (h k)")
                ts(ciau[:, 0, :], flat, 4, None, ALU.logical_shift_right)
                ts(ciau[:, 1, :], flat, 15, None, ALU.bitwise_and)
                step(cp(TOPIF, idxu))
                step(cp(CIAF, ciau))
                num = TOPIF.rearrange("p (h x) k -> p h x k", x=2)
                oh4 = OH.rearrange("p (h k j) -> p h k j", h=PH, k=PTOP)
                oh3 = OH.rearrange("p (s j) -> p s j", j=PTOP)
                for x in range(2):
                    step(tt(oh3, bc(CIAF[:, x, :], 2, PTOP), bc(C("iota16"), 1, P), ALU.is_equal))
                    step(tt(oh4, oh4, bc(num[:, :, x, :], 2, PTOP), ALU.mult))
                    step(V.tensor_reduce(EAB[:, x, :], oh3, AX.X, ALU.add))

            def gates(t):
                g3 = EAB[:, 2, :].rearrange("p (h k) -> p h k", h=PH)
                signal(tt(g3, SCV, bc(SCV[:, :, 0], 2, PTOP), ALU.subtract), "gate_sc")
                dve.wait_ge(S["gate_exp"], t + 1)
                step(V.tensor_reduce(SMX, g3, AX.X, ALU.add))
                step(V.reciprocal(SMX, SMX))
                signal(tt(g3, g3, bc(SMX, 2, PTOP), ALU.mult), "idx_ready")

            best_keys(0)
            for u in range(2):
                freed(dve, ("ada", u), 2)
            step(tt(mods[:, :, :], mods[:, :, :], bc(col("b_ada"), 2, 2), ALU.add))
            stt(modsb[:, 0:8], mods[:, 8:16, 0], 1.0, col("g_mix2"), ALU.add, ALU.mult)
            stt(modsb[:, 8:16], mods[:, 8:16, 1], 1.0, col("g_mix2"), ALU.add, ALU.mult)
            stt(modsb[:, 16:24], mods[:, 32:40, 0], 1.0, col("g_ffn2"), ALU.add, ALU.mult)
            cp(modsb[:, 24:32], mods[:, 24:32, 0])
            cp(modsb[:, 40:48], mods[:, 0:8, 0])
            step(cp(modsb[:, 48:56], mods[:, 0:8, 1]))
            scale_rows(5, D, lambda t: CX[:, t, :], lambda t: XN[:, t, :])
            features("cT", CXT, modsb[:, 8:16], modsb[:, 48:56])
            best_pairs(0)

            def gate_logs(f, lf, nk, names):
                signal(stt(lf, f, -1.0, f, ALU.mult, ALU.max), names[0])
                dve.wait_ge(S[names[1]], 1)
                signal(stt(nk, f, 0.0, lf, ALU.max, ALU.add), names[2])
                signal(stt(lf, f, 0.0, lf, ALU.min, ALU.subtract), names[3], 1)

            for b in range(3):
                for t in range(TT):
                    freed(dve, ("cp", b, t))
            gate_logs(CPJ[:, :, 0:1024], CLF, CKK, ("ctx_abs", "ctx_l", "ctx_nk", "ctx_f"))
            dve.wait_ge(S["ctx_k"], 1)
            for d in range(2):
                for t in range(TT):
                    freed(dve, ("ce", d, t))
            signal(tt(CKK, CKK, CEX, ALU.mult), "ctx_kd")
            gates(0)
            best_keys(1)
            arrived(dve, ("eTr", 0))
            best_pairs(1)
            gates(1)
            for t in range(TT):
                freed(dve, ("eTr", t))
            with dve.Fori(0, T // 8) as i:
                for u in range(2):
                    dve.wait_ge(bank_full[B.at[("w", u)][0]], i + (B.at[("w", u)][1] - 1))
                    for v in range(4):
                        s = lambda x: slots[:, x, bass.ds(i * 8 + (4 * u + v), 1)]
                        ts(ONEHOT[:, u, v, 1, :], C("iota"), s(1), None, ALU.is_equal)
                        ins = ts(ONEHOT[:, u, v, 0, :], C("iota"), s(0), s(2), ALU.is_equal, ALU.mult)
                    ins.then_inc(S["onehot_ready"], 1)
            freed(dve, ("h0",))
            for u in range(2):
                freed(dve, ("w", u), T // 8 - 1)
            tt(GATED[:, 0, :], GELU[:, 0, :], WT[:, 0, :], ALU.mult).then_inc(S["p_ready"], 1)
            with dve.Fori(0, 31) as i:
                for u in range(4):
                    freed(dve, ("h", u), i)
                    dve.wait_ge(S["p_used"], i * 4 + u)
                    par = (u + 1) % 2
                    tt(GATED[:, par, :], GELU[:, par, :], WT[:, i * 4 + (u + 1), :], ALU.mult).then_inc(S["p_ready"], 1)
            for u in range(3):
                a = 125 + u
                freed(dve, ("he", u))
                dve.wait_ge(S["p_used"], a - 1)
                tt(GATED[:, a % 2, :], GELU[:, a % 2, :], WT[:, a, :], ALU.mult).then_inc(S["p_ready"], 1)
            scale_rows(6, D, lambda t: hres[:, t, :], lambda t: XN[:, t, :])
            dve.wait_ge(in_second, 4 * 16)
            for t in range(TT):
                dve.wait_ge(S["xn_ready"], 6 * TT + t + 1)
                signal(tt(hres[:, t, :], XN[:, t, :], FIN1, ALU.mult), "x2_ready")
            scale_rows(7, D, lambda t: hres[:, t, :], lambda t: XN[:, t, :])
            features("x2T", actT, modsb[:, 0:8], modsb[:, 40:48])
            for b in range(7):
                for t in range(TT):
                    freed(dve, ("p", b, t))
                if b == 1:
                    gate_logs(PJ[:, :, 0:1024], LF, K2, ("g_abs", "g_l", "g_nk", "g_logf"))
            dve.wait_ge(S["g_k"], 1)
            for d in range(2):
                freed(dve, ("as", d))
                signal(tt(KD[:, d, :], KD[:, d, :], K2[:, d, d * 512:(d + 1) * 512], ALU.mult), "g_kd")
            freed(dve, ("tot",))
            for d in range(2):
                b = arrived(dve, ("adv", d))
                for h in range(HH):
                    ins = stt(HS[:, d, h, :], h0[:, d, h, :], TOTE[:, d * 4 + h:d * 4 + h + 1], b[:, hsl(h)],
                              ALU.mult, ALU.add)
                free(ins, ("adv", d))
            for d in range(2):
                for t in range(TT):
                    freed(dve, ("kT2", d, t))
            for t in range(TT):
                freed(dve, ("qT2", t))
            signal(tt(KS, K2T[:, 0], K2T[:, 1], ALU.add), "g_H")
            dve.wait_ge(in_second, 5 * 16)
            for t in range(TT):
                b = arrived(dve, ("dg", t)).rearrange("p (h n) -> p h n", h=HH)
                free(tt(SM, b, bc(ident, 1, HH), ALU.mult), ("dg", t))
                freed(dve, ("dg", t))
                for d in range(2):
                    for h in range(HH):
                        for half in range(2):
                            freed(dve, ("e", t, d, h, half))
                        q = Q2T[:, h, tsl(t)]
                        tt(ZK[:, h], ZQ[:, h, 0:7, :], bc(K2T[:, d, h, tsl(t)], 1, 7), ALU.mult)
                        tt(ZP[:, d, h, :], ZQ[:, h, 7, :], q, ALU.mult)
                        ins = tt(ZQ[:, h, 0:7, :], ZQ[:, h, 0:7, :], bc(q, 1, 7), ALU.mult)
                    signal(ins, "z_made")
                    for lev in range(N_LEVELS):
                        b = arrived(dve, ("gr", t, d, lev)).rearrange("p (h n) -> p h n", h=HH)
                        m = bc(LEV[:, d * 7 + lev, :].bitcast(U32), 1, HH)
                        free(V.copy_predicated(SM, m, b), ("gr", t, d, lev))
                        freed(dve, ("gr", t, d, lev))
                free(cp(PJ[:, t, 0:512], arrived(dve, ("o", t))), ("o", t))
            h4 = lambda ap: ap.rearrange("p t (h n) -> p t h n", h=HH)
            O, SQ, VV = PJ[:, :, 0:512], PJ[:, :, 512:1024], PJ[:, :, 3072:3584]
            for t in range(TT):
                freed(dve, ("o", t))
            step(V.tensor_reduce(gst[:, 3, 1], h4(VV), AX.X, ALU.add))
            step(ts(gst[:, 3, 1], gst[:, 3, 1], 1.0 / P, None, ALU.mult))
            tt(SQ, O, O, ALU.mult)
            step(tt(h4(VV), h4(VV), bc(gst[:, 3, 1], 3, P), ALU.subtract))
            step(V.tensor_reduce(gst[:, 0, 0], h4(SQ), AX.X, ALU.add))
            step(tt(SQ, VV, VV, ALU.mult))
            step(V.tensor_reduce(gst[:, 0, 1], h4(SQ), AX.X, ALU.add))
            signal(ts(gst[:, 1], gst[:, 0], 1.0 / P, EPS, ALU.mult, ALU.add), "o_ms")
            dve.wait_ge(S["o_root"], 1)
            step(V.reciprocal(gst[:, 3], gst[:, 2]))
            tt(h4(O), h4(O), bc(gst[:, 3, 0], 3, P), ALU.mult)
            step(tt(h4(VV), h4(VV), bc(gst[:, 3, 1], 3, P), ALU.mult))
            tt(O, O, bc(R2[:, 0:512], 1, TT), ALU.mult)
            step(tt(VV, VV, bc(R2[:, 512:1024], 1, TT), ALU.mult))
            tt(OC[:, :, 0:512], O, PJ[:, :, 2048:2560], ALU.mult)
            signal(tt(VV, VV, bc(R2[:, 1024:1536], 1, TT), ALU.add), "v_ready")
            tt(GBD[:, 0], bc(ident, 1, KC), bc(mods[:, 16:24, 0], 2, P), ALU.mult)
            signal(tt(GBD[:, 1], bc(ident, 1, KC), bc(mods[:, 40:48, 0], 2, P), ALU.mult), "gdiag")
            signal(V.memset(ZEROS, 0.0), "zeros_ready")
            for t in range(TT):
                b = arrived(dve, ("sg", t)).rearrange("p (h n) -> p h n", h=HH)
                v = PJ[:, t, 512:1024]
                free(tt(v.rearrange("p (h n) -> p h n", h=HH), b, bc(col("b_s"), 2, P), ALU.add), ("sg", t))
                freed(dve, ("sg", t))
                signal(tt(OC[:, t, 512:1024], v, PJ[:, t, 2560:3072], ALU.mult), "oc_ready")
            for r in range(4):
                freed(dve, ("gb", r))

            def add_gated(name, g, done, order):
                for n, (b, t) in enumerate(order):
                    s = slice(b * 512, (b + 1) * 512)
                    job = (name, b, t) if name == "w2" else (name, t, b)
                    free(tt(T512[:, n, :], arrived(dve, job), GB[:, g, s], ALU.mult), job)
                    freed(dve, job)
                    signal(tt(hres[:, t, s], hres[:, t, s], T512[:, n, :], ALU.add), done)
                dve.wait_ge(S[done], 4)

            add_gated("w2", 0, "x3_ready", [(b, t) for b in range(2) for t in range(TT)])
            scale_rows(8, D, lambda t: hres[:, t, :], lambda t: XN[:, t, :])
            features("x3T", actT, modsb[:, 16:24], modsb[:, 24:32])

            grid = lambda ap: ap.rearrange("p (r w) -> p r w", w=GW)
            R = T // GW

            def conv_channels(gate_job, value_job, c, base, par, used, turn=None):
                freed(dve, gate_job, turn)
                tap = lambda k: col("taps")[:, bass.ds(c * 9 + k, 1)]
                x, o = grid(GC[:, par, :]), grid(CV[:, par, :])
                ts(CV[:, par, :], GC[:, par, :], tap(4), col("fconv_b")[:, bass.ds(c, 1)], ALU.mult,
                   ALU.add).then_inc(step.c.sem, 1)
                n = 1
                for k in (0, 1, 2, 3, 5, 6, 7, 8):
                    dr, dw = k // 3 - 1, k % 3 - 1
                    ro, wo = slice(max(0, -dr), R - max(0, dr)), slice(max(0, -dw), GW - max(0, dw))
                    ri, wi = slice(max(0, dr), R + min(0, dr)), slice(max(0, dw), GW + min(0, dw))
                    dve.wait_ge(step.c.sem, base + n)
                    ins = stt(o[:, ro, wo], x[:, ri, wi], tap(k), o[:, ro, wo], ALU.mult, ALU.add)
                    ins.then_inc(step.c.sem if k < 8 else S["ffn_conv"], 1)
                    n += 1
                dve.wait_ge(S["ffn_gelu"], c + 1)
                if used is not None:
                    dve.wait_ge(S["ffn_used"], used)
                b = arrived(dve, value_job, turn)
                free(tt(HF[:, par, :], GE[:, par, :], b[:, 0:T], ALU.mult), value_job)

            n0 = step.c.n
            conv_channels(("g0",), ("a0",), 0, n0, 0, None)
            with dve.Fori(0, (FC - 2) // 2) as i:
                for u in range(2):
                    conv_channels(("ga", 2 * u), ("ga", 2 * u + 1), i * 2 + (u + 1), i * 16 + (n0 + 8 * (u + 1)),
                                  (u + 1) % 2, i * 2 + u, i)
            conv_channels(("ge",), ("ae",), FC - 1, n0 + 8 * (FC - 1), 1, FC - 2)
            step.c.n = n0 + 8 * FC
            add_gated("f", 1, "x4_ready", [(b, t) for t in range(TT) for b in range(2)])
            scale_rows(9, D, lambda t: hres[:, t, :], lambda t: XN[:, t, :])
            dve.wait_ge(in_second, 6 * 16)
            for t in range(TT):
                dve.wait_ge(S["xn_ready"], 9 * TT + t + 1)
                signal(tt(XN[:, t, :], XN[:, t, :], FIN2, ALU.mult), "out_ready")


def chunk_columns(v):
    return v.reshape(-1, P).T


def token_tiles(w):
    n = w.shape[1] // 512
    return w.reshape(4, 2, P, n, 512).transpose(3, 0, 2, 1, 4).reshape(4 * n, P, 1024)


def feature_tiles(w):
    n = w.shape[1] // P
    return w.reshape(KC, P, n, P).transpose(2, 1, 0, 3).reshape(n, P, 1024)


def constants():
    i = np.arange(P)
    c = np.zeros((P, N_CONST), np.float32)

    def put(name, v):
        o, w = CONST[name]
        c[:, o:o + w] = v

    put("ident", np.eye(P))
    put("upto", i[:, None] <= i[None, :])
    put("ones", 1.0)
    put("after", i[:, None] > i[None, :])
    put("before", i[:, None] < i[None, :])
    put("causal", np.where(i[None, :] <= i[:, None], 0.0, NEG))
    put("iota", i[None, :])
    put("iota16", np.arange(16)[None, :])
    f = np.float32(THETA) ** (np.float32(-2.0) * np.arange(16, dtype=np.float32) / np.float32(32))
    g = np.float32(THETA) ** (np.float32(-2.0) * np.arange(8, dtype=np.float32) / np.float32(16))
    put("freq", np.concatenate([f, g])[None, :])
    u, pos = i[:, None], i[None, :]
    span = np.zeros((P, 2, N_LEVELS + 1, P), np.float32)
    lev = np.zeros((P, 14, P), np.float32)
    s, t = i[:, None], i[None, :]
    for m in range(N_LEVELS):
        w = 1 << m
        mid = pos // (2 * w) * (2 * w) + w
        up = pos >= mid
        span[:, 0, m] = np.where(up, (u >= mid) & (u <= pos), (u > pos) & (u < mid))
        span[:, 1, m] = np.where(up, (u >= mid) & (u < pos), (u >= pos) & (u < mid))
        same = s // (2 * w) == t // (2 * w)
        lev[:, m] = same & (s % (2 * w) < w) & (t % (2 * w) >= w)
        lev[:, 7 + m] = same & (s % (2 * w) >= w) & (t % (2 * w) < w)
    span[:, 0, N_LEVELS] = u <= pos
    span[:, 1, N_LEVELS] = u >= pos
    return c, span.reshape(P, 2, -1), lev


def kernel(**inputs):
    import concourse.bacc as _bacc
    from concourse.bass_utils import run_bass_kernel_spmd as _run

    a = {k: np.asarray(v) for k, v in inputs.items()}
    w_in = a["w_in"][0]
    o = np.cumsum([0, 1024, 256, 256, 256, 64, 4, 2048, 3072, 32, 2048])
    q, k, v, iq, ik, iw, z, xbc, dt, gate = (w_in[:, o[n]:o[n + 1]] for n in range(10))
    tok = np.concatenate([q, k, iq, ik, v, iw, dt, np.zeros((D, 2048 - 1892), np.float32)], axis=1)
    ws = a["w_ssd_branch"][0]
    wa, ws0, ws1 = feature_tiles(a["w_attn_branch"][0]), feature_tiles(ws[:1024]), feature_tiles(ws[1024:])
    merge = np.stack([wa, ws0, ws1], axis=1).reshape(24, P, 1024)
    kv = a["w_cross_kv"][0]
    w2 = a["w_in_2"][0]
    ut = a["peer_u"][0].reshape(P, P, KC, P).transpose(0, 3, 2, 1).reshape(P, P, 1024)
    vt = a["peer_v"][0].reshape(P, P, 1024)
    up = a["w_up_2"][0]
    gt, at = feature_tiles(up[:, FF:]), feature_tiles(up[:, :FF])
    dn = a["w_down_2"][0].reshape(FC, P, 1024)
    parts = [token_tiles(tok), feature_tiles(xbc), token_tiles(z), feature_tiles(gate), feature_tiles(kv[:, :1024]),
             token_tiles(kv[:, 1024:]), merge, token_tiles(a["w_out"][0]), feature_tiles(a["w_cross_q"][0]),
             token_tiles(a["w_cross_out"][0]), feature_tiles(a["w_peer_q"][0]), feature_tiles(a["w_ada_2"][0]),
             token_tiles(w2[:, :1536]),
             ut[0:1], np.stack([ut[1:], vt[:-1]], axis=1).reshape(254, P, 1024), vt[-1:],
             token_tiles(w2), token_tiles(a["w_out_2"][0]),
             gt[0:1], at[0:1], np.stack([gt[1:], at[1:], dn[:-1]], axis=1).reshape(63, P, 1024), dn[-1:]]
    stream = np.concatenate(parts, axis=0)
    assert stream.shape[0] == N_RING + N_FFN
    cols = np.zeros((P, N_COLS), np.float32)
    pc = chunk_columns
    conv = a["conv_w"][0][:, 0, :].T.reshape(24, P, 4).transpose(1, 0, 2).reshape(P, 96)
    taps = a["conv_w_2"][0].reshape(9, FC, P).transpose(2, 1, 0).reshape(P, 198)
    cc = np.stack([pc(a["c_2"][0]), pc(a["c_ctx_2"])], axis=2).reshape(P, 16)
    for name, val in [("g_mix", pc(a["norm_mix_g"][0])), ("g_cross", pc(a["norm_cross_g"][0])),
                      ("g_mem", pc(a["norm_mem_g"][0])), ("g_ffn", pc(a["norm_ffn_g"][0])),
                      ("g_ssd", pc(a["ssd_norm_g"][0])), ("conv_w", conv), ("conv_b", pc(a["conv_b"][0])),
                      ("c2", cc), ("b_ada", pc(a["b_ada_2"][0])), ("g_mix2", pc(a["norm_mix_2"][0])),
                      ("g_ffn2", pc(a["norm_ffn_2"][0])), ("taps", taps), ("fconv_b", pc(a["conv_b_2"][0])),
                      ("b_s", a["b_spatial_2"][0].T)]:
        c0, w = COLS[name]
        cols[:, c0:c0 + w] = val
    const, span, lev = constants()
    arrays = {
        "stream": stream, "x": a["x"], "mem": a["mem"], "ctx": a["ctx_2"], "const": const, "cols": cols,
        "rows": np.concatenate([a["dt_bias"][0], a["a_log"][0], a["d_skip"][0]]),
        "pos": np.ascontiguousarray(a["positions"][0].reshape(TT, P).T.astype(np.int32)),
        "keys": np.ascontiguousarray(a["peer_sub_keys"][0].transpose(3, 0, 1, 2).reshape(P, 16, P)),
        "fin1": a["norm_final_g"], "fin2": a["norm_final_2"],
        "rows2": np.concatenate([a["hg_norm_2"][0], a["sgu_norm_g_2"][0], a["sgu_norm_b_2"][0]]),
        "levels": lev, "span": span,
        "wsp": np.ascontiguousarray(a["w_spatial_2"][0].transpose(2, 0, 1)),
    }
    nc = _bacc.Bacc("TRN2", target_bir_lowering=False, num_devices=1)
    aps = {n: nc.dram_tensor(f"in_{n}", list(v.shape), mybir.dt.from_np(v.dtype), kind="ExternalInput").ap()
           for n, v in arrays.items()}
    aps["out"] = nc.dram_tensor("out", [1, T, D], F32, kind="ExternalOutput").ap()
    build(nc, aps)
    r = _run(nc, [{f"in_{n}": v for n, v in arrays.items()}], core_ids=[0])
    return r.results[0]["out"]
```

```python
from contextlib import ExitStack

import numpy as np

import concourse.bass as bass
from concourse import mybir

P = 128
T = 256
TT = T // P
D = 1024
KC = D // P
EPS = 1e-6
TWO_PI = [6.28125, float(np.float32(2 * np.pi - 6.28125) // 2**-20 * 2**-20), 0.0]
TWO_PI[2] = float(2 * np.pi - TWO_PI[0] - TWO_PI[1])
NEG = -3.0e38
TAKEN = -3.4e38
OFF = -1.0e30

QH, KVH, DH = 8, 2, 128
IH, IDH = 4, 64
TOPK = T // 4
SH, SP_, SG, SN = 32, 64, 4, 128
SD = SH * SP_
MH, MD = 4, 256
PH, PK, PTOP = 8, 128, 16
PSLOT = PH * PTOP
HG, HH = 512, 4
FF, FC = 2816, 22
GW = 64
THETA = 500000.0

F32 = mybir.dt.float32
U32 = mybir.dt.uint32
F32R = mybir.dt.float32r
I32 = mybir.dt.int32
ALU = mybir.AluOpType
ACT = mybir.ActivationFunctionType
AX = mybir.AxisListType

SECTIONS = [
    ("in_tok", 16), ("in_xbc", 24), ("in_z", 16), ("in_gate", 16), ("mem_k", 8), ("mem_v", 8), ("merge", 24),
    ("w_out", 8), ("cross_q", 8), ("cross_out", 8), ("peer_q", 16), ("ada0", 16), ("ctx", 12),
    ("ada1", 32),
    ("experts", 2 * P), ("in2", 28), ("out2", 8),
]
FIRST = {}
_n = 0
for _name, _count in SECTIONS:
    FIRST[_name] = _n
    _n += _count
RING = 4
N_RING = _n
EXP0 = FIRST["experts"]
EXPERTS = 2 * P
AFTER = EXP0 + EXPERTS
FRONT = FIRST["mem_k"]
X0 = FRONT
N_IN2 = FIRST["out2"] - FIRST["in2"]
I0 = X0 + EXPERTS
F0 = I0 + N_IN2
assert FRONT % RING == 0 and X0 % 2 == I0 % 2 == F0 % 2 == 0
assert EXP0 % RING == 0 and EXPERTS % RING == 0 and N_RING % RING == 0
FRING = 6
N_FFN = 3 * FC
FFN0 = N_RING

CONST = {}
_c = 0
for _name, _w in [("ident", P), ("upto", P), ("ones", P), ("after", P), ("before", P), ("causal", P),
                  ("iota", P), ("freq", 24), ("iota16", 16)]:
    CONST[_name] = (_c, _w)
    _c += _w
N_CONST = _c
N_LEVELS = 7
N_SPAN = (N_LEVELS + 1) * P
COLS = {}
_c = 0
for _name, _w in [("g_mix", 8), ("g_cross", 8), ("g_mem", 8), ("g_ffn", 8), ("g_ssd", 16), ("conv_w", 96),
                  ("conv_b", 24), ("c2", 16), ("b_ada", 48), ("g_mix2", 8), ("g_ffn2", 8), ("taps", 198),
                  ("fconv_b", 22), ("b_s", 4)]:
    COLS[_name] = (_c, _w)
    _c += _w
N_COLS = _c
ROWS = {}
_c = 0
for _name, _w in [("dt_bias", 32), ("a_log", 32), ("d_skip", 32)]:
    ROWS[_name] = (_c, _w)
    _c += _w
N_ROWS = _c
ROWS2 = {}
_c = 0
for _name, _w in [("hg", 512), ("sgu_g", 512), ("sgu_b", 512)]:
    ROWS2[_name] = (_c, _w)
    _c += _w
N_ROWS2 = _c


class Banks:

    def __init__(self):
        self.fills = [0] * 8
        self.at = {}
        self.next = 0

    def job(self, *name, bank=None):
        b = self.next if bank is None else bank
        self.next = (b + 1) % 8
        self.fills[b] += 1
        self.at[name] = (b, self.fills[b])

    def loop(self, name, turns, width, banks=None):
        for j in range(width):
            self.job(name, j, bank=None if banks is None else banks[j])
        for j in range(width):
            self.fills[self.at[(name, j)][0]] += turns - 1


def plan_banks():
    B = Banks()
    B.start = {}
    for t in range(TT):
        for h in range(2):
            B.job("xT", t, h)
    for b in range(4):
        for t in range(TT):
            B.job("tok", b, t)
    B.loop("xbc", 3, 8)
    for b in range(4):
        for t in range(TT):
            B.job("z", b, t)
    for t in range(TT):
        for h in range(2):
            B.job("qTr", t, h)
    B.job("kTr")
    B.job("iqTr")
    B.job("ikTr")
    for t in range(TT):
        for r in range(2):
            B.job("idx", t, r)
    B.loop("gate", 2, 8)
    for t in range(TT):
        for p in range(4):
            B.job("lg", t, p)
    for t in range(TT):
        for q in range(4):
            B.job("xsTr", t, q)
    B.job("BTr")
    B.job("acs")
    for t in range(TT):
        for n in range(2 * (t + 1)):
            B.job("PTr", t, n)
        for kv in range(KVH):
            B.job("oT", t, kv)
    B.job("cb", 0)
    B.job("cb", 1)
    groups = [(c, g) for c in range(TT) for g in range(SG)]
    for k in range(len(groups) + 1):
        if k < len(groups):
            B.job("row", *groups[k], 0)
            B.job("row", *groups[k], 1)
        if k >= 1:
            c, g = groups[k - 1]
            B.job("yd", c, g)
            B.job("st" if c == 0 else "yo", g)
    for t in range(TT):
        for h in range(2):
            B.job("mT", t, h)
    for n in range(8):
        B.job("mk", n)
    for b in range(2):
        for t in range(TT):
            B.job("mv", b, t)
    for t in range(TT):
        for q in range(4):
            B.job("yTr", t, q)
    for n in range(8):
        B.job("ma", n)
        B.job("ms", n)
    for b in range(2):
        for t in range(TT):
            B.job("wo", b, t)
    for t in range(TT):
        for h in range(2):
            B.job("a2T", t, h)
    for n in range(8):
        B.job("cq", n)
    for t in range(TT):
        for p in range(2):
            B.job("cl", t, p)
    for t in range(TT):
        for m in range(TT):
            B.job("cP", t, m)
    for h in range(MH):
        B.job("co", h)
    for b in range(2):
        for t in range(TT):
            B.job("cw", b, t)
    for t in range(TT):
        for h in range(2):
            B.job("a3T", t, h)
    B.loop("pq", 2, 8)
    for t in range(TT):
        for q in range(4):
            B.job("sk", t, q)
    for t in range(TT):
        for h in range(2):
            B.job("cT", t, h)
    free_banks = [(B.next + n) % 8 for n in range(4)]
    B.loop("ad0", 1, 8, banks=2 * free_banks)
    for b in range(3):
        for t in range(TT):
            B.job("cp", b, t)
    for d in range(2):
        for t in range(TT):
            B.job("ce", d, t)
    for d in range(2):
        B.job("cH", d)
    for t in range(TT):
        for h in range(2):
            B.job("y", t, h, bank=2 * t + h)
    B.loop("ad1", 2, 8, banks=(4, 5, 6, 7, 4, 5, 6, 7))
    for t in range(TT):
        B.job("eTr", t, bank=6 + t)
    B.loop("w", T // 16, 4, banks=(4, 5, 6, 7))
    B.job("h0", bank=4)
    B.loop("h", 31, 4, banks=(5, 6, 7, 4))
    for u in range(3):
        B.job("he", u, bank=5 + u)
    B.next = 4
    for t in range(TT):
        for h in range(2):
            B.job("x2T", t, h)
    for b in range(7):
        for t in range(TT):
            B.job("p", b, t)
    for t in range(TT):
        B.job("qT2", t)
    for d in range(2):
        for t in range(TT):
            B.job("kT2", d, t)
    for d in range(2):
        B.job("as", d)
    B.job("tot")
    for d in range(2):
        B.job("adv", d)
    for t in range(TT):
        B.job("dg", t)
        for d in range(2):
            for h in range(HH):
                B.job("e", t, d, h, 0)
                B.job("e", t, d, h, 1)
            for lev in range(N_LEVELS):
                B.job("gr", t, d, lev)
        B.job("o", t)
    for t in range(TT):
        B.job("sg", t)
    for r in range(4):
        B.job("gb", r)
    for t in range(TT):
        for h in range(2):
            B.job("ocT", t, h)
    for b in range(2):
        for t in range(TT):
            B.job("w2", b, t)
    for t in range(TT):
        for h in range(2):
            B.job("x3T", t, h)
    for t in range(TT):
        for h in range(2):
            B.job("f", t, h, bank=2 * t + h)
    B.job("g0", bank=4)
    B.job("a0", bank=6)
    B.loop("ga", (FC - 2) // 2, 4, banks=(5, 7, 4, 6))
    B.job("ge", bank=5)
    B.job("ae", bank=7)
    return B


ADA_ORDER = [(0, 0), (1, 0), (0, 1), (2, 0), (1, 1), (3, 0), (2, 1), (3, 1)]
ADA_JOB = {jk: n for n, jk in enumerate(ADA_ORDER)}


def bc(ap, axis, n):
    ap = ap.unsqueeze(axis)
    shape = list(ap.shape)
    shape[axis] = n
    return ap.to_broadcast(shape)


class Count:

    def __init__(self, sem):
        self.sem, self.n = sem, 0

    def by(self, ins, n=1):
        ins.then_inc(self.sem, n)
        self.n += n
        return self.n


class Chain:

    def __init__(self, eng, sem):
        self.eng, self.c = eng, Count(sem)

    def __call__(self, ins):
        self.eng.wait_ge(self.c.sem, self.c.by(ins))


def build(nc, A):
    B = plan_banks()
    with ExitStack() as ctx:
        where = {}

        def sb(name, shape, dt=F32):
            tensor = ctx.enter_context(nc.sbuf_tensor(name, shape, dt))
            where[name] = nc.sbuf_base - 4 * int(np.prod(shape[1:]))
            return tensor

        def over(name, below, offset, shape):
            return nc.alloc_sbuf_tensor_at(name, shape, F32R, offset=where[below] + 4 * offset)

        def sem(name):
            return ctx.enter_context(nc.semaphore(name))

        ps = ctx.enter_context(nc.psum_tensor("banks", [P, 8, 512], F32))
        bank_full = [sem(f"bank_full{b}") for b in range(8)]
        bank_free = [sem(f"bank_free{b}") for b in range(8)]

        ring = sb("weight_ring", [P, RING, 1024])
        w_hi = sb("weight_high", [P, 2, 1024], F32R)
        w_lo = sb("weight_rest", [P, 2, 1024], F32R)
        arena = sb("arena", [P, 32768])
        scratch = sb("scratch", [P, 2048])
        hres = sb("residual", [P, TT, D])
        actT = sb("act_feature_major", [P, KC, T])
        const = sb("const", [P, N_CONST])
        cols = sb("cols", [P, N_COLS])
        rows = sb("rows", [P, N_ROWS])
        stat = sb("stat", [P, 4, 10, TT])
        slots = sb("expert_slots", [P, 4, T])
        x1_hi = over("x1_high", "arena", 30208, [P, KC, T])
        x1_lo = over("x1_rest", "act_feature_major", 0, [P, KC, T])
        x2_hi = over("x2_high", "arena", 20480, [P, KC, T])
        x2_lo = over("x2_rest", "act_feature_major", 0, [P, KC, T])
        a3_hi = over("a3_high", "residual", 0, [P, KC, T])
        a3_lo = over("a3_rest", "act_feature_major", 0, [P, KC, T])
        gated_hi = over("gated_high", "scratch", 512, [P, 2, T])
        gated_lo = over("gated_rest", "scratch", 1024, [P, 2, T])
        x3_hi = over("x3_high", "arena", 22528, [P, KC, T])
        x3_lo = over("x3_rest", "act_feature_major", 0, [P, KC, T])
        hidden_hi = over("hidden_high", "arena", 26624, [P, 2, T])
        hidden_lo = over("hidden_rest", "arena", 27136, [P, 2, T])
        h0 = sb("state_from_context", [P, 2, HH, P])
        mods = sb("modulation", [P, 48, 2])
        modsb = sb("modulation_sums", [P, 64])
        small = sb("small", [P, 1024])
        columns2 = sb("column_onehots", [P, 4, P])

        ring_loaded = [sem(f"ring_loaded{s}") for s in range(RING)]
        ffn_loaded = [sem(f"ffn_loaded{s}") for s in range(FRING)]
        tiles_begun = sem("tiles_begun")
        in_x = sem("x_loaded")
        in_mem = sem("mem_loaded")
        in_const = sem("const_loaded")
        in_ctx = sem("ctx_loaded")
        in_keys = sem("subkeys_loaded")
        in_second = sem("second_consts_loaded")
        out_done = sem("out_stored")
        names = """norm_sq norm_ms norm_root xn_ready act_ready rope_ready xbc_ready attn_masked attn_exp
            attn_prob dt_abs dt_l adt_ready acs_ready acs_exp seg_exp m_ready adtb_ready xdtd_ready y_ready
            mem_v merged_ready cl_ready cprob gate_sc gate_exp idx_ready onehot_ready p_ready silu_c
            ctx_abs ctx_l ctx_nk ctx_f ctx_k ctx_kd rope_arg rope_sin x2_ready g_abs g_l g_nk g_logf g_k
            g_kd g_H z_made o_ms o_root v_ready oc_ready gdiag x3_ready ffn_conv ffn_gelu x4_ready
            out_ready act_step dve_step zeros_ready neg_a y_seeded a3_hi_ready a3_lo_ready x3_hi_ready
            x3_lo_ready hi_ready hi_used lo_ready ffn_lo_ready ffn_down_lo_ready x1_hi_ready x1_lo_ready x2_hi_ready x2_lo_ready rest_ready column_ready square_made
            slots_negated gated_made hidden_ready hidden_made""".split()
        S = {n: sem(n) for n in names}

        def C(name):
            o, w = CONST[name]
            return const[:, o:o + w]

        def col(name):
            o, w = COLS[name]
            return cols[:, o:o + w]

        def row(name):
            o, w = ROWS[name]
            return rows[:, o:o + w]

        def area(off, *dims):
            n = int(np.prod(dims))
            assert off + n <= 32768, (off, dims)
            v = arena[:, off:off + n]
            if len(dims) == 1:
                return v
            names_ = "abcd"[:len(dims)]
            return v.rearrange(f"p ({' '.join(names_)}) -> p {' '.join(names_)}",
                               **{k: d for k, d in zip(names_[1:], dims[1:])})

        def raw(e):
            if e < F0:
                g = e if e < FRONT else EXP0 + e - X0
                return ring[:, g % RING, :], ring_loaded[g % RING], 16 * (g // RING + 1), 32
            r = e - F0
            return FR[:, r % FRING, :], ffn_loaded[r % FRING], 16 * (r // FRING + 1), 16

        def rest_count(e):
            if e < FRONT:
                return S["rest_ready"], e + 1
            if e < I0:
                return S["lo_ready"], e - X0 + 1
            return S["rest_ready"], FRONT + e - I0 + 1

        def bank(name):
            return ps[:, B.at[name][0], :]

        def claim(name, turn=None):
            b, n = B.at[name]
            if turn is not None:
                nc.tensor.wait_ge(bank_free[b], turn + (n - 1))
            elif n > 1:
                nc.tensor.wait_ge(bank_free[b], n - 1)
            return ps[:, b, :]

        def filled(ins, name):
            ins.then_inc(bank_full[B.at[name][0]], 1)

        def arrived(eng, name, turn=None):
            b, n = B.at[name]
            eng.wait_ge(bank_full[b], n if turn is None else turn + n)
            return ps[:, b, :]

        def freed(eng, name, turn=None):
            b, n = B.at[name]
            eng.wait_ge(bank_free[b], n if turn is None else turn + n)

        def free(ins, name):
            ins.then_inc(bank_free[B.at[name][0]], 1)

        TOK = area(0, TT, 2048)
        XBC = area(4096, 24, T)
        ZT = area(10240, TT, 2048)
        GT = area(14336, 16, T)
        QT = area(18432, 8, T)
        KT = area(20480, 2, T)
        IQT = area(20992, 2, T)
        IKT = area(21504, T)
        IKD = area(21760, TT, P)
        RELU = area(22016, 4, 2, T)
        SC = area(24064, 4, T)
        LG = [area(25088, 8, P), area(26112, 8, T)]
        PT = area(28160, 2, 8, P)
        AT = area(30208, 8, T)
        ROPE = area(32256, 2, TT, 24)
        ROPET = area(22016, 5, 96)
        RT = area(22656, 2, TT * 160)
        XS = area(18432, TT, 2048)
        YT_ = area(22528, TT, 2048)
        BTOK = area(0, SG, P)
        EM = area(26624, 2, 8, P)
        ADTB = scratch[:, :].rearrange("p (b h l) -> p b h l", b=2, h=8)
        CBM = area(28672, TT, SG, P)
        XDTD = area(4096, 2048)
        STATE = area(6144, SG, 512)
        YT = area(4096, 16, T)
        MT = area(0, KC, T)
        MEMX = area(2048, TT, D)
        MKT = area(18432, KC, T)
        MV = area(20480, TT, D)
        MG = area(26624, KC, T)
        CQT = area(8192, KC, T)
        CL = area(0, 4, T)
        CPT = area(2048, 2, 4, T)
        COT = area(10240, KC, T)
        QPT = area(0, 16, T)
        SK = area(4096, TT, 16, P)
        SK2 = area(8192, 16, P)
        CAND = area(10240, PH, 256)
        CAND2 = area(12288, PH, 256)
        ADA = small[0:2, :].rearrange("p (b n) -> p b n", b=2)
        OH = area(14336, 2048)
        TOPV = area(16384, 16, PTOP)
        TOPI = area(16640, 16, PTOP)
        TOPIF = area(16896, 16, PTOP)
        SCV = area(17152, PH, PTOP)
        SCI = area(17280, PH, PTOP)
        CIA = area(17408, 2, P)
        CIAF = area(17664, 2, P)
        EAB = area(31744, TT, 3, P)
        SMX = area(18304, 8)
        KEYS = area(18432, 16, P)
        CX = area(20480, TT, D)
        CXT = area(22528, KC, T)
        CPJ = area(24576, TT, 1536)
        CLF = area(27648, TT, 1024)
        CKK = area(29696, TT, 1024)
        WT = area(0, P, T)
        FR = area(0, FRING, 1024)
        PJ = area(6144, TT, 3584)
        LF = area(13312, TT, 1024)
        K2 = area(15360, TT, 1024)
        K2T = area(17408, 2, HH, T)
        Q2T = area(19456, HH, T)
        ZQ = area(20480, HH, 8, P)
        ZK = area(24576, HH, 7, P)
        SM = area(28160, HH, P)
        ZP = area(28672, 2, HH, P)
        HS = area(29696, 2, HH, P)
        LEV = area(30720, 15, P)
        GSPAN = scratch[:, :].rearrange("p (d n) -> p d n", d=2)
        OC = area(20480, TT, D)
        T512 = area(22528, 4, 512)
        GB = area(24576, 2, D)
        GBD = area(26624, 2, KC, P)
        FIN1 = area(0, D)
        R2 = area(4096, N_ROWS2)
        FIN2 = area(30720, D)
        CV = area(17408, 2, T)
        GC = area(18432, 2, T)
        GE = area(19456, 2, T)
        HF = area(20480, T)
        WSP = small[:, 0:512].rearrange("p (h n) -> p h n", h=HH)

        smx = sb("softmax_stats", [P, TT, 4, 8])
        c2s = sb("silu_of_conditions", [P, KC, 2])
        gst = sb("mixer_stats", [P, 4, 2, TT, HH])
        lo = lambda a, b: small[:, a:b]
        DT = lo(0, 64).rearrange("p (c h) -> p c h", c=TT)
        DTS = lo(64, 128).rearrange("p (c h) -> p c h", c=TT)
        DTL = lo(128, 192).rearrange("p (c h) -> p c h", c=TT)
        ADT = lo(256, 320).rearrange("p (c h) -> p c h", c=TT)
        ACS = lo(320, 448).rearrange("p (c h) -> p c h", c=4)
        EAC = lo(448, 512).rearrange("p (c h) -> p c h", c=TT)
        DTE = lo(544, 576)
        NEGA = lo(576, 608)
        IW = lo(608, 616).rearrange("p (c h) -> p c h", c=TT)
        ident = C("ident")
        XN = scratch[:, :].rearrange("p (t d) -> p t d", t=TT)
        ONEHOT = scratch[:, :].rearrange("p (u v x n) -> p u v x n", u=2, v=4, x=2)
        COLUMN = [ONEHOT[:, 0, :, 1, :], columns2[:, :, :]]
        GELU = scratch[:, 0:512].rearrange("p (b t) -> p b t", b=2)
        GATED = scratch[:, 1536:1792]
        CEX = CX
        KD = area(20480, 2, 512)
        KS = area(15360, HH, T)
        TOTE = modsb[:, 32:40]
        ZEROS = area(29696, 512)
        tsl = lambda t: slice(t * P, (t + 1) * P)
        hsl = lambda h: slice(h * P, (h + 1) * P)
        block = ctx.enter_context(nc.Block())

        @block.sync
        def _(sp):
            stream = A["stream"]
            for t in range(TT):
                sp.dma_start(hres[:, t, :], A["x"][0, t * P:(t + 1) * P, :]).then_inc(in_x, 16)
            sp.dma_start(const[:, :], A["const"]).then_inc(in_const, 16)
            sp.dma_start(cols[:, :], A["cols"]).then_inc(in_const, 16)
            sp.dma_start(rows[:, :], A["rows"].partition_broadcast(P)).then_inc(in_const, 16)
            sp.dma_start(small[:, 616:618].bitcast(I32), A["pos"]).then_inc(in_const, 16)
            def fetch(g, s):
                sp.dma_start(ring[:, s, :], stream[g]).then_inc(ring_loaded[s], 16)

            for s in range(RING):
                fetch(s, s)
            with sp.Fori(1, FRONT // RING) as i:
                for s in range(RING):
                    sp.wait_ge(S["rest_ready"], i * RING + (s - RING + 1))
                    fetch(i * RING + s, s)
            for s in range(RING):
                sp.wait_ge(S["rest_ready"], FRONT + s - RING + 1)
                fetch(FRONT + s, s)
            with sp.Fori(1, (EXP0 - FRONT) // RING) as i:
                for s in range(RING):
                    sp.wait_ge(tiles_begun, i * RING + (s - RING + 2))
                    fetch(i * RING + (FRONT + s), s)
            for s in range(RING):
                if s < RING - 1:
                    sp.wait_ge(tiles_begun, EXP0 - FRONT + s - RING + 2)
                else:
                    freed(sp, ("ad1", ADA_JOB[3, 1]), 2)
                fetch(EXP0 + s, s)
            with sp.Fori(1, EXPERTS // RING) as i:
                for s in range(RING):
                    sp.wait_ge(S["lo_ready"], i * RING + (s - RING + 1))
                    fetch(i * RING + (EXP0 + s), s)
            for s in range(RING):
                sp.wait_ge(S["lo_ready"], EXPERTS + s - RING + 1)
                fetch(AFTER + s, s)
            with sp.Fori(1, N_IN2 // RING) as i:
                for s in range(RING):
                    sp.wait_ge(S["rest_ready"], i * RING + (FRONT + s - RING + 1))
                    fetch(i * RING + (AFTER + s), s)
            for s in range(RING):
                sp.wait_ge(S["rest_ready"], FRONT + N_IN2 + s - RING + 1)
                fetch(FIRST["out2"] + s, s)
            for s in range(RING):
                if s < RING - 1:
                    sp.wait_ge(tiles_begun, EXP0 - FRONT + s + 2)
                else:
                    arrived(sp, ("w2", 0, TT - 1))
                fetch(FIRST["out2"] + RING + s, s)
            sp.wait_ge(S["v_ready"], 1)
            for s in range(FRING):
                sp.dma_start(FR[:, s, :], stream[FFN0 + s]).then_inc(ffn_loaded[s], 16)
            with sp.Fori(1, N_FFN // FRING) as i:
                for s in range(FRING):
                    sp.wait_ge(S["hi_used"], i * FRING + (F0 + s - FRING + 2))
                    sp.dma_start(FR[:, s, :], stream[i * FRING + (FFN0 + s)]).then_inc(ffn_loaded[s], 16)
            for t in range(TT):
                sp.wait_ge(S["out_ready"], t + 1)
                sp.dma_start(A["out"][0, t * P:(t + 1) * P, :], XN[:, t, :]).then_inc(out_done, 16)
            sp.wait_ge(out_done, 16 * TT)

        @block.gpsimd
        def _(pool):
            def split_rest(e, turn=None, n=8):
                i_ = 0 if turn is None else turn
                pool.wait_ge(S["hi_ready"], i_ * n + (e + 1))
                if e > 1:
                    pool.wait_ge(S["hi_used"], i_ * n + e)
                nc.gpsimd.tensor_tensor(w_lo[:, e % 2, :], raw(e)[0], w_hi[:, e % 2, :],
                                        ALU.subtract).then_inc(S["rest_ready"], 1)

            for e in range(8):
                split_rest(e)
            with pool.Fori(1, FRONT // 8) as i:
                for e in range(8):
                    split_rest(e, i) if e > 1 else split_rest(e + 8, i - 1)
            arrived(pool, ("oT", 1, 1))
            pool.wait_ge(S["adt_ready"], 1)
            for t in range(TT):
                pool.dma_start(MEMX[:, t, :], A["mem"][0, t * P:(t + 1) * P, :]).then_inc(in_mem, 16)
            arrived(pool, ("co", MH - 1))
            pool.dma_start(KEYS, A["keys"]).then_inc(in_keys, 16)
            for t in range(TT):
                pool.dma_start(CX[:, t, :], A["ctx"][0, t * P:(t + 1) * P, :]).then_inc(in_ctx, 16)
            pool.wait_ge(S["p_ready"], P)
            pool.dma_start(FIN1, A["fin1"].partition_broadcast(P)).then_inc(in_second, 16)
            pool.dma_start(R2, A["rows2"].partition_broadcast(P)).then_inc(in_second, 16)
            pool.dma_start(LEV[:, 0:14, :], A["levels"]).then_inc(in_second, 16)
            pool.dma_start(WSP, A["wsp"]).then_inc(in_second, 16)
            arrived(pool, ("x2T", 1, 1))
            pool.dma_start(GSPAN, A["span"]).then_inc(in_second, 16)
            with pool.Fori(0, N_IN2 // RING) as i:
                for s in range(RING):
                    split_rest(I0 + s, i, RING)
            freed(pool, ("gr", 1, 1, N_LEVELS - 1))
            pool.dma_start(FIN2, A["fin2"].partition_broadcast(P)).then_inc(in_second, 16)

            def split_down(r, turn=None):
                e = F0 + r
                n = 0 if turn is None else turn * 6
                pool.wait_ge(S["hi_ready"], n + (e + 1))
                pool.wait_ge(S["hi_used"], n + e)
                nc.gpsimd.tensor_tensor(w_lo[:, e % 2, :], raw(e)[0], w_hi[:, e % 2, :],
                                        ALU.subtract).then_inc(S["ffn_down_lo_ready"], 1)

            with pool.Fori(0, (FC - 2) // 2) as i:
                for u in range(2):
                    split_down(4 + 3 * u, i)
            split_down(64)
            split_down(65)

        @block.tensor
        def _(pe):
            begun = [False]

            def mm(out, lhsT, rhs, start=True, stop=True):
                ins = nc.tensor.matmul(out, lhsT, rhs, start=start, stop=stop, skip_group_check=True)
                if begun[0]:
                    ins.then_inc(tiles_begun, 1)
                    begun[0] = False
                return ins

            def weights(g, turn=None, per=8):
                s, n = g % RING, g // RING
                pe.wait_ge(ring_loaded[s], 16 * (n + 1) if turn is None else turn * (16 * per // RING) + 16 * (n + 1))
                begun[0] = True
                return ring[:, s, :]

            def transposes(job, pairs):
                b = claim(job)
                for k, src in enumerate(pairs):
                    ins = nc.tensor.transpose(b[:, k * P:(k + 1) * P], src, ident)
                filled(ins, job)

            def token_block(sec, b, name, lhs):
                banks = [claim((name, b, t)) for t in range(TT)]
                for j in range(4):
                    w = weights(FIRST[sec] + 4 * b + j)
                    for t in range(TT):
                        for k in range(2):
                            ins = mm(banks[t], lhs[:, 2 * j + k, tsl(t)], w[:, k * 512:(k + 1) * 512],
                                     start=(j == 0 and k == 0), stop=(j == 3 and k == 1))
                        if j == 3:
                            filled(ins, (name, b, t))

            def feature_tile(g, job, rhs, turn=None, chunks=KC):
                b = claim(job, turn)
                for k in range(chunks):
                    if k % KC == 0:
                        w = weights(g + k // KC, turn)
                    ins = mm(b[:, 0:T], w[:, hsl(k % KC)], rhs[:, k, :], start=(k == 0), stop=(k == chunks - 1))
                filled(ins, job)

            def features_ready(name, chunks=2):
                for t in range(TT):
                    for h in range(chunks):
                        freed(pe, (name, t, h))

            def norm_transposes(name, src, n):
                for t in range(TT):
                    pe.wait_ge(S["xn_ready"], n * TT + t + 1)
                    for h in range(2):
                        transposes((name, t, h), [src[:, t, hsl(4 * h + k)] for k in range(4)])

            pe.wait_ge(in_const, 64)
            def split_tile(e, turn, n, high, rest, rest_ready, rest_count):
                more = 0 if turn is None else turn * n
                pe.wait_ge(S["hi_ready"], more + (e + 1))
                high(w_hi[:, e % 2, :]).then_inc(S["hi_used"], 1)
                pe.wait_ge(rest_ready, rest_count)
                return rest(w_lo[:, e % 2, :])

            def split_block(e, name, b, hi, lo_, turn=None):
                banks = [claim((name, b, t)) for t in range(TT)]
                for j in range(4):
                    def high(w):
                        for t in range(TT):
                            for k in range(2):
                                r = w[:, k * 512:(k + 1) * 512]
                                mm(banks[t], hi[:, 2 * j + k, tsl(t)], r, start=(j == k == 0), stop=False)
                                ins = mm(banks[t], lo_[:, 2 * j + k, tsl(t)], r, start=False, stop=False)
                        return ins

                    def rest(w):
                        for t in range(TT):
                            for k in range(2):
                                ins = mm(banks[t], hi[:, 2 * j + k, tsl(t)], w[:, k * 512:(k + 1) * 512],
                                         start=False, stop=(j == 3 and k == 1))
                            if j == 3:
                                filled(ins, (name, b, t))

                    split_tile(e + 4 * b + j, None, 0, high, rest, *rest_count(e + 4 * b + j))

            def split_channels(e, job, hi, lo_, turn, n, rest_ready, rest_count):
                b = claim(job, turn)

                def high(w):
                    for k in range(KC):
                        mm(b[:, 0:T], w[:, hsl(k)], hi[:, k, :], start=(k == 0), stop=False)
                        ins = mm(b[:, 0:T], w[:, hsl(k)], lo_[:, k, :], start=False, stop=False)
                    return ins

                def rest(w):
                    for k in range(KC):
                        ins = mm(b[:, 0:T], w[:, hsl(k)], hi[:, k, :], start=False, stop=(k == KC - 1))
                    return ins

                filled(split_tile(e, turn, n, high, rest, rest_ready, rest_count), job)

            norm_transposes("xT", XN, 0)
            pe.wait_ge(S["x1_hi_ready"], 4)
            pe.wait_ge(S["x1_lo_ready"], 4)
            for b in range(4):
                split_block(0, "tok", b, x1_hi, x1_lo)
            with pe.Fori(0, 3) as i:
                for j in range(8):
                    e = FIRST["in_xbc"] + j
                    split_channels(e, ("xbc", j), x1_hi, x1_lo, i, 8, S["rest_ready"], i * 8 + (e + 1))
            for b in range(4):
                split_block(FIRST["in_z"], "z", b, x1_hi, x1_lo)
            pe.wait_ge(S["rope_ready"], 1)
            for t in range(TT):
                for h in range(2):
                    transposes(("qTr", t, h), [TOK[:, t, hsl(4 * h + k)] for k in range(4)])
            transposes(("kTr",), [TOK[:, t, 1024 + kv * P:1024 + (kv + 1) * P] for kv in range(KVH) for t in range(TT)])
            transposes(("iqTr",), [TOK[:, t, 1280 + b * P:1280 + (b + 1) * P] for b in range(2) for t in range(TT)])
            transposes(("ikTr",), [IKD[:, t, :] for t in range(TT)])
            for name in (("qTr", 1, 1), ("kTr",), ("iqTr",), ("ikTr",)):
                freed(pe, name)
            for t in range(TT):
                for r in range(2):
                    b = claim(("idx", t, r))
                    rs = slice(r * IDH, (r + 1) * IDH)
                    for c in range(2):
                        ins = mm(b[:, c * T:(c + 1) * T], IQT[rs, c, tsl(t)], IKT[rs, :])
                    filled(ins, ("idx", t, r))
            with pe.Fori(0, 2) as i:
                for j in range(8):
                    e = FIRST["in_gate"] + j
                    split_channels(e, ("gate", j), x1_hi, x1_lo, i, 8, S["rest_ready"], i * 8 + (e + 1))
            for t in range(TT):
                w = P * (t + 1)
                for p in range(4):
                    b = claim(("lg", t, p))
                    for c in range(2):
                        h = 2 * p + c
                        ins = mm(b[:, c * T:c * T + w], QT[:, h, tsl(t)], KT[:, h // 4, 0:w])
                    filled(ins, ("lg", t, p))
            pe.wait_ge(S["xbc_ready"], 24)
            for t in range(TT):
                for q in range(4):
                    transposes(("xsTr", t, q), [XBC[:, 4 * q + k, tsl(t)] for k in range(4)])
            transposes(("BTr",), [XBC[:, 16 + g, 0:P] for g in range(SG)])
            pe.wait_ge(S["adt_ready"], 1)
            b = claim(("acs",))
            for c in range(TT):
                mm(b[:, c * 32:(c + 1) * 32], C("upto"), ADT[:, c, :])
            for c in range(TT):
                ins = mm(b[:, 64 + c * 32:64 + (c + 1) * 32], C("ones"), ADT[:, c, :])
            filled(ins, ("acs",))
            for t in range(TT):
                pe.wait_ge(S["attn_prob"], t + 1)
                blocks = [(s, h) for s in range(t + 1) for h in range(QH)]
                for n in range(2 * (t + 1)):
                    transposes(("PTr", t, n), [LG[t][:, h, tsl(s)] for s, h in blocks[4 * n:4 * n + 4]])
                for kv in range(KVH):
                    b = claim(("oT", t, kv))
                    for s in range(t + 1):
                        freed(pe, ("PTr", t, 2 * s + kv))
                        ins = mm(b, TOK[:, s, 1600 + kv * P:1600 + (kv + 1) * P],
                                 PT[:, s, 4 * kv:4 * kv + 4, :].rearrange("p h t -> p (h t)"),
                                 start=(s == 0), stop=(s == t))
                    filled(ins, ("oT", t, kv))
            for c in range(TT):
                b = claim(("cb", c))
                for g in range(SG):
                    ins = mm(b[:, hsl(g)], XBC[:, 16 + g, tsl(c)], XBC[:, 20 + g, tsl(c)])
                filled(ins, ("cb", c))
            groups = [(c, g) for c in range(TT) for g in range(SG)]
            for k in range(len(groups) + 1):
                if k < len(groups):
                    c, g = groups[k]
                    pe.wait_ge(S["adtb_ready"], k + 1)
                    for half in range(2):
                        b = claim(("row", c, g, half))
                        for j in range(4):
                            ins = mm(b[:, hsl(j)], ADTB[:, k % 2, 4 * half + j, :], C("upto"))
                        filled(ins, ("row", c, g, half))
                if k >= 1:
                    c, g = groups[k - 1]
                    if k == 1:
                        pe.wait_ge(S["xdtd_ready"], 1)
                        freed(pe, ("BTr",))
                    pe.wait_ge(S["m_ready"], k)
                    b = claim(("yd", c, g))
                    for j in range(8):
                        h = 8 * g + j
                        ins = mm(b[:, j * SP_:(j + 1) * SP_], EM[:, (k - 1) % 2, j, :],
                                 XS[:, c, h * SP_:(h + 1) * SP_])
                    filled(ins, ("yd", c, g))
                    if c == 0:
                        b = claim(("st", g))
                        filled(mm(b, BTOK[:, g, :], XDTD[:, g * 512:(g + 1) * 512]), ("st", g))
                    else:
                        freed(pe, ("st", g))
                        b = claim(("yo", g))
                        filled(mm(b, XBC[:, 20 + g, P:T], STATE[:, g, :]), ("yo", g))
            norm_transposes("mT", XN, 1)
            features_ready("mT")
            for n in range(8):
                feature_tile(FIRST["mem_k"] + n, ("mk", n), MT)
            for b in range(2):
                token_block("mem_v", b, "mv", MT)
            for t in range(TT):
                pe.wait_ge(S["xn_ready"], 2 * TT + t + 1)
                for q in range(4):
                    transposes(("yTr", t, q), [YT_[:, t, hsl(4 * q + k)] for k in range(4)])
            for kv in range(KVH):
                freed(pe, ("oT", 1, kv))
            features_ready("yTr", 4)
            for n in range(8):
                feature_tile(FIRST["merge"] + 3 * n, ("ma", n), AT)
                feature_tile(FIRST["merge"] + 3 * n + 1, ("ms", n), YT, chunks=16)
            pe.wait_ge(S["merged_ready"], 8)
            for b in range(2):
                token_block("w_out", b, "wo", MG)
            norm_transposes("a2T", XN, 3)
            features_ready("a2T")
            for n in range(8):
                feature_tile(FIRST["cross_q"] + n, ("cq", n), actT)
            for n in range(8):
                freed(pe, ("mk", n))
                freed(pe, ("cq", n))
            for t in range(TT):
                for p in range(2):
                    b = claim(("cl", t, p))
                    for c in range(2):
                        h = 2 * p + c
                        for k in range(2):
                            ins = mm(b[:, c * T:(c + 1) * T], CQT[:, 2 * h + k, tsl(t)], MKT[:, 2 * h + k, :],
                                     start=(k == 0), stop=(k == 1))
                    filled(ins, ("cl", t, p))
            for t in range(TT):
                pe.wait_ge(S["cprob"], t + 1)
                for m in range(TT):
                    transposes(("cP", t, m), [CL[:, h, tsl(m)] for h in range(MH)])
            for b in range(2):
                for t in range(TT):
                    freed(pe, ("mv", b, t))
                    freed(pe, ("cP", b, t))
            for h in range(MH):
                b = claim(("co", h))
                for c in range(2):
                    for m in range(TT):
                        ins = mm(b[:, c * T:(c + 1) * T], MV[:, m, h * MD + c * P:h * MD + (c + 1) * P],
                                 CPT[:, m, h, :], start=(m == 0), stop=(m == 1))
                filled(ins, ("co", h))
            for h in range(MH):
                freed(pe, ("co", h))
            for b in range(2):
                token_block("cross_out", b, "cw", COT)
            norm_transposes("a3T", XN, 4)
            features_ready("a3T")
            with pe.Fori(0, 2) as i:
                for j in range(8):
                    feature_tile(FIRST["peer_q"] + j, ("pq", j), actT, i)
            for j in range(8):
                freed(pe, ("pq", j), 1)
            pe.wait_ge(in_keys, 16)
            for t in range(TT):
                for q in range(4):
                    b = claim(("sk", t, q))
                    for j in range(4):
                        ins = mm(b[:, hsl(j)], QPT[:, 4 * q + j, tsl(t)], KEYS[:, 4 * q + j, :])
                    filled(ins, ("sk", t, q))
            norm_transposes("cT", XN, 5)

            fills = lambda turn: None if turn is None else turn * 2

            def modulation(name, turn=None):
                def rows_(j):
                    b = claim((name, ADA_JOB[j, 0]), fills(turn))
                    for m in range(4):
                        w = weights(FIRST[name.replace("ad", "ada")] + 4 * j + m, turn, 16)
                        for k in range(2):
                            ins = mm(b[0:2, :], c2s[:, 2 * m + k, :], w[:, k * 512:(k + 1) * 512],
                                     start=(m == 0 and k == 0), stop=(m == 3 and k == 1))
                    filled(ins, (name, ADA_JOB[j, 0]))

                def turned(j):
                    freed(pe, (name, ADA_JOB[j, 0]), fills(turn))
                    b = claim((name, ADA_JOB[j, 1]), fills(turn))
                    for k in range(4):
                        ins = mm(b[:, 2 * k:2 * k + 2], ADA[:, j % 2, hsl(k)], ident[0:2, 0:2])
                    filled(ins, (name, ADA_JOB[j, 1]))

                rows_(0)
                for j in range(1, 4):
                    rows_(j)
                    turned(j - 1)
                turned(3)

            pe.wait_ge(S["silu_c"], 1)
            modulation("ad0")
            pe.wait_ge(S["act_ready"], 4)
            for b in range(3):
                token_block("ctx", b, "cp", CXT)
            pe.wait_ge(S["ctx_f"], 1)
            for d in range(2):
                tri = C("after") if d == 0 else C("before")
                for t in range(TT):
                    b = claim(("ce", d, t))
                    far = (t == 0) if d == 0 else (t == 1)
                    ins = mm(b, tri, CLF[:, t, d * 512:(d + 1) * 512], start=True, stop=not far)
                    if far:
                        ins = mm(b, C("ones"), CLF[:, 1 - t, d * 512:(d + 1) * 512], start=False, stop=True)
                    filled(ins, ("ce", d, t))
            pe.wait_ge(S["ctx_kd"], 1)
            for d in range(2):
                b = claim(("cH", d))
                for h in range(HH):
                    for t in range(TT):
                        ins = mm(b[:, hsl(h)], CKK[:, t, d * 512 + h * P:d * 512 + (h + 1) * P],
                                 CPJ[:, t, 1024 + h * P:1024 + (h + 1) * P], start=(t == 0), stop=(t == 1))
                filled(ins, ("cH", d))
            for t in range(TT):
                for h in range(2):
                    b = claim(("y", t, h))
                    ins = mm(b, ident, hres[:, t, h * 512:(h + 1) * 512], start=True, stop=False)
            ins.then_inc(S["y_seeded"], 1)
            with pe.Fori(0, 2) as i:
                modulation("ad1", i)
            for t in range(TT):
                pe.wait_ge(S["idx_ready"], t + 1)
                transposes(("eTr", t), [EAB[:, t, x, :] for x in range(3)])
            with pe.Fori(0, T // 16) as i:
                for u in range(4):
                    pe.wait_ge(S["onehot_ready"], i * 4 + (u + 1))
                    if u % 2 == 0:
                        pe.wait_ge(S["column_ready"], i * 2 + (u // 2 + 1))
                    b = claim(("w", u), i)
                    for v in range(4):
                        column = ONEHOT[:, 1, v, 1, :] if u % 2 else COLUMN[u // 2][:, v, :]
                        ins = mm(b[:, hsl(v)], column, ONEHOT[:, u % 2, v, 0, :])
                    filled(ins, ("w", u))

            def split_sums(e, name, hi, lo_, turn, n, rest_ready, rest_count, last=False):
                def high(w):
                    for t in range(TT):
                        for h in range(2):
                            o = bank((name, t, h))
                            mm(o, hi[:, tsl(t)], w[:, h * 512:(h + 1) * 512], start=False, stop=False)
                            ins = mm(o, lo_[:, tsl(t)], w[:, h * 512:(h + 1) * 512], start=False, stop=False)
                    return ins

                def rest(w):
                    for t in range(TT):
                        for h in range(2):
                            ins = mm(bank((name, t, h)), hi[:, tsl(t)], w[:, h * 512:(h + 1) * 512],
                                     start=False, stop=last)
                            if last:
                                filled(ins, (name, t, h))

                split_tile(e, turn, n, high, rest, rest_ready, rest_count)

            def units(e, job, turn=None):
                split_channels(X0 + e, job, a3_hi, a3_lo, turn, 8, S["lo_ready"],
                               e + 1 if turn is None else turn * 8 + (e + 1))

            def values(e, a, par, turn=None, last=False):
                pe.wait_ge(S["p_ready"], a + 1)
                split_sums(X0 + e, "y", gated_hi[:, par, :], gated_lo[:, par, :], turn, 8, S["lo_ready"],
                           e + 1 if turn is None else turn * 8 + (e + 1), last)

            pe.wait_ge(S["a3_hi_ready"], 1)
            pe.wait_ge(S["a3_lo_ready"], 1)
            units(0, ("h0",))
            with pe.Fori(0, 31) as i:
                for u in range(4):
                    units(1 + 2 * u, ("h", u), i)
                    values(2 + 2 * u, i * 4 + u, u % 2, i)
            for u in range(3):
                a = 124 + u
                units(1 + 2 * a, ("he", u))
                values(2 + 2 * a, a, a % 2)
            values(255, 127, 1, last=True)
            norm_transposes("x2T", XN, 7)
            pe.wait_ge(S["x2_hi_ready"], 4)
            pe.wait_ge(S["x2_lo_ready"], 4)
            for b in range(7):
                split_block(I0, "p", b, x2_hi, x2_lo)
            for t in range(TT):
                freed(pe, ("p", 3, t))
                transposes(("qT2", t), [PJ[:, t, 1536 + h * P:1536 + (h + 1) * P] for h in range(HH)])
            pe.wait_ge(S["g_k"], 1)
            for d in range(2):
                for t in range(TT):
                    transposes(("kT2", d, t), [K2[:, t, d * 512 + h * P:d * 512 + (h + 1) * P] for h in range(HH)])
            pe.wait_ge(S["g_logf"], 1)
            for d in range(2):
                b = claim(("as", d))
                filled(mm(b, C("after") if d == 0 else C("before"), LF[:, d, d * 512:(d + 1) * 512]), ("as", d))
            b = claim(("tot",))
            for d in range(2):
                for h in range(HH):
                    ins = mm(b[:, d * 4 + h:d * 4 + h + 1], LF[:, d, d * 512 + h * P:d * 512 + (h + 1) * P],
                             C("ones")[:, 0:1])
            filled(ins, ("tot",))
            for d in range(2):
                pe.wait_ge(S["g_kd"], d + 1)
                b = claim(("adv", d))
                for h in range(HH):
                    ins = mm(b[:, hsl(h)], KD[:, d, hsl(h)], PJ[:, d, 1024 + h * P:1024 + (h + 1) * P])
                filled(ins, ("adv", d))
            pe.wait_ge(in_second, 5 * 16)
            pe.wait_ge(S["g_H"], 1)
            for t in range(TT):
                freed(pe, ("qT2", t))
            for t in range(TT):
                b = claim(("dg", t))
                for h in range(HH):
                    ins = mm(b[:, hsl(h)], KS[:, h, tsl(t)], Q2T[:, h, tsl(t)])
                filled(ins, ("dg", t))
                for d in range(2):
                    for h in range(HH):
                        for half in range(2):
                            b = claim(("e", t, d, h, half))
                            filled(mm(b, LF[:, t, d * 512 + h * P:d * 512 + (h + 1) * P],
                                      GSPAN[:, d, half * 512:(half + 1) * 512]), ("e", t, d, h, half))
                    pe.wait_ge(S["z_made"], 2 * t + d + 1)
                    for lev in range(N_LEVELS):
                        b = claim(("gr", t, d, lev))
                        for h in range(HH):
                            ins = mm(b[:, hsl(h)], ZK[:, h, lev, :], ZQ[:, h, lev, :])
                        filled(ins, ("gr", t, d, lev))
                freed(pe, ("gr", t, 1, N_LEVELS - 1))
                b = claim(("o", t))
                hf = h0[:, 0] if t == 0 else HS[:, 0]
                hb = h0[:, 1] if t == 1 else HS[:, 1]
                for h in range(HH):
                    mm(b[:, hsl(h)], SM[:, h, :], PJ[:, t, 1024 + h * P:1024 + (h + 1) * P], start=True, stop=False)
                    mm(b[:, hsl(h)], ZP[:, 0, h, :], hf[:, h, :], start=False, stop=False)
                    ins = mm(b[:, hsl(h)], ZP[:, 1, h, :], hb[:, h, :], start=False, stop=True)
                filled(ins, ("o", t))
            for t in range(TT):
                pe.wait_ge(S["v_ready"], 1)
                b = claim(("sg", t))
                for h in range(HH):
                    ins = mm(b[:, hsl(h)], WSP[:, h, :], PJ[:, t, 3072 + h * P:3072 + (h + 1) * P])
                filled(ins, ("sg", t))
            pe.wait_ge(S["gdiag"], 1)
            for r in range(4):
                b = claim(("gb", r))
                filled(mm(b, C("ones"), GBD[:, r // 2, 4 * (r % 2):4 * (r % 2) + 4, :].rearrange("p k n -> p (k n)")),
                       ("gb", r))
            for t in range(TT):
                pe.wait_ge(S["oc_ready"], t + 1)
                for h in range(2):
                    transposes(("ocT", t, h), [OC[:, t, hsl(4 * h + k)] for k in range(4)])
            for t in range(TT):
                for h in range(2):
                    freed(pe, ("ocT", t, h))
            for b in range(2):
                token_block("out2", b, "w2", actT)
            norm_transposes("x3T", XN, 8)
            pe.wait_ge(S["act_ready"], 12)
            def channels(r, job, count, turn=None):
                split_channels(F0 + r, job, x3_hi, x3_lo, turn, 6, S["ffn_lo_ready"],
                               count if turn is None else turn * 4 + count)

            def down(r, c, par, turn=None, last=False):
                n = 0 if turn is None else turn * 2
                pe.wait_ge(S["hidden_ready"], n + (c + 1))
                split_sums(F0 + r, "f", hidden_hi[:, par, :], hidden_lo[:, par, :], turn, 6,
                           S["ffn_down_lo_ready"], n + (c + 1), last)

            pe.wait_ge(S["zeros_ready"], 1)
            for t in range(TT):
                for h in range(2):
                    mm(claim(("f", t, h)), ident, ZEROS, start=True, stop=False)
            pe.wait_ge(S["x3_hi_ready"], 1)
            pe.wait_ge(S["x3_lo_ready"], 1)
            channels(0, ("g0",), 1)
            channels(1, ("a0",), 2)
            with pe.Fori(0, (FC - 2) // 2) as i:
                for u in range(2):
                    channels(2 + 3 * u, ("ga", 2 * u), 3 + 2 * u, i)
                    channels(3 + 3 * u, ("ga", 2 * u + 1), 4 + 2 * u, i)
                    down(4 + 3 * u, u, u, i)
            channels(62, ("ge",), 43)
            channels(63, ("ae",), 44)
            down(64, FC - 2, 0)
            down(65, FC - 1, 1, last=True)

        @block.scalar
        def _(act):
            step = Chain(act, S["act_step"])

            def func(out, in_, f, **kw):
                return nc.scalar.activation(out, in_, f, **kw)

            def evacuate(job, out, turn=None, f=ACT.Copy, src=None, **kw):
                b = arrived(act, job, turn)
                free(func(out, b if src is None else src(b), f, **kw), job)

            def norm(n, x, junk, ready=None):
                for t in range(TT):
                    if ready is not None:
                        ready(t)
                    if n == 2 and t == 1:
                        act.wait_ge(S["norm_sq"], 2 * n + 1)
                    func(junk(t), x(t), ACT.Square, accum_out=stat[:, 0, n, t:t + 1]).then_inc(S["norm_sq"], 1)
                act.wait_ge(S["norm_ms"], n + 1)
                func(stat[:, 2, n, :], stat[:, 1, n, :], ACT.Sqrt).then_inc(S["norm_root"], 1)

            def halves(b):
                return b.rearrange("p (c t) -> p c t", c=2)

            def quarters(b):
                return b.rearrange("p (c t) -> p c t", c=4)

            def split_high(e, turn=None, n=8, rests=None):
                i_ = 0 if turn is None else turn
                src, loaded, count, per = raw(e)
                act.wait_ge(loaded, i_ * per + count)
                if e > 1:
                    act.wait_ge(S["hi_used"], i_ * n + (e - 1))
                    if rests is None:
                        rests = rest_count(e - 2)
                        if turn is not None:
                            rests = rests[0], turn * 8 + rests[1]
                    act.wait_ge(*rests)
                func(w_hi[:, e % 2, :], src, ACT.Copy).then_inc(S["hi_ready"], 1)

            norm(0, lambda t: hres[:, t, :], lambda t: XN[:, t, :], lambda t: act.wait_ge(in_x, 16 * TT))
            act.wait_ge(S["rope_arg"], 1)
            func(ROPE.rearrange("p a b c -> p (a b c)"), ROPET[:, 4, :], ACT.Sin).then_inc(S["rope_sin"], 1)
            split_high(0)
            split_high(1)

            def high_quarters(name, hi, done, ready):
                for n in range(4):
                    t, h = n // 2, n % 2
                    done(n)
                    q = (slice(None), slice(4 * h, 4 * h + 4), tsl(t))
                    func(hi[q], actT[q], ACT.Copy).then_inc(S[ready], 1)

            def split_blocks(e, blocks, evacuation):
                for m in range(2, 4 * blocks):
                    split_high(e + m)
                    if m % 4 == 1:
                        evacuation(m // 4 - 1)

            high_quarters("xT", x1_hi, lambda n: freed(act, ("xT", n // 2, n % 2)), "x1_hi_ready")

            def evacuate_tok(b):
                for t in range(TT):
                    evacuate(("tok", b, t), TOK[:, t, b * 512:(b + 1) * 512])

            split_blocks(0, 4, evacuate_tok)
            split_high(16)
            split_high(17)
            evacuate_tok(3)
            split_high(18)
            with act.Fori(0, 3) as i:
                for j in range(8):
                    split_high(FIRST["in_xbc"] + j + 3, i)
                    freed(act, ("xbc", j), i)
                    c = i * 8 + j
                    func(XBC[:, c, :], XBC[:, c, :], ACT.Silu).then_inc(S["xbc_ready"], 1)

            def evacuate_z(b):
                for t in range(TT):
                    evacuate(("z", b, t), ZT[:, t, b * 512:(b + 1) * 512], f=ACT.Silu)

            z0 = FIRST["in_z"]
            for e in range(z0 + 3, z0 + 18):
                split_high(e)
                if (e - z0) % 4 == 1:
                    evacuate_z((e - z0) // 4 - 1)
            act.wait_ge(S["dt_abs"], 1)
            step(func(DTS, DTS, ACT.Exp, scale=-1.0))
            func(DTL, DTS, ACT.Ln, bias=1.0).then_inc(S["dt_l"], 1)
            func(NEGA, row("a_log"), ACT.Exp).then_inc(S["neg_a"], 1)
            for t in range(TT):
                for h in range(2):
                    evacuate(("qTr", t, h), QT[:, 4 * h:4 * h + 4, tsl(t)], src=quarters)
            evacuate(("kTr",), KT.rearrange("p k t -> p (k t)"))
            evacuate(("iqTr",), IQT.rearrange("p k t -> p (k t)"))
            evacuate(("ikTr",), IKT, src=lambda b: b[:, 0:T])
            for t in range(TT):
                for r in range(2):
                    evacuate(("idx", t, r), RELU[:, 2 * t + r], f=ACT.Relu, scale=IDH ** -0.5, src=halves)
            for n in range(16):
                if n < 14:
                    split_high(FIRST["in_gate"] + n + 2)
                i_, j = n // 8, n % 8
                evacuate(("gate", j), GT[:, n, :], i_, f=ACT.Sigmoid, src=lambda b: b[:, 0:T])
            for t in range(TT):
                act.wait_ge(S["attn_masked"], t + 1)
                for h in range(QH):
                    ins = func(LG[t][:, h, :], LG[t][:, h, :], ACT.Exp, bias=smx[:, t, 1, h:h + 1],
                               scale=DH ** -0.5, accum_out=smx[:, t, 2, h:h + 1])
                ins.then_inc(S["attn_exp"], 1)
            for t in range(TT):
                for q in range(4):
                    evacuate(("xsTr", t, q), XS[:, t, q * 512:(q + 1) * 512])
            evacuate(("BTr",), BTOK.rearrange("p g n -> p (g n)"))
            act.wait_ge(S["acs_ready"], 1)
            step(func(EAC.rearrange("p c h -> p (c h)"), lo(320, 384), ACT.Exp))
            func(DTE, DTE, ACT.Exp).then_inc(S["acs_exp"], 1)
            for t in range(TT):
                for n in range(2 * (t + 1)):
                    s, h = n // 2, 4 * (n % 2)
                    if t == 1 and n == 0:
                        arrived(act, ("oT", 0, 1))
                    evacuate(("PTr", t, n), PT[:, s, h:h + 4, :], src=quarters)
                for kv in range(KVH):
                    evacuate(("oT", t, kv), AT[:, 4 * kv:4 * kv + 4, tsl(t)], src=quarters)
            for k in range(TT * SG):
                for half in range(2):
                    freed(act, ("row", k // SG, k % SG, half))
                func(EM[:, k % 2], EM[:, k % 2], ACT.Exp).then_inc(S["seg_exp"], 1)
            norm(1, lambda t: MEMX[:, t, :], lambda t: XN[:, t, :], lambda t: act.wait_ge(in_mem, 16 * TT))
            norm(2, lambda t: YT_[:, t, :], lambda t: EM[:, :, :, :].rearrange("p u h l -> p (u h l)"),
                 lambda t: act.wait_ge(S["y_ready"], t + 1))
            for n in range(8):
                evacuate(("mk", n), MKT[:, n, :], src=lambda b: b[:, 0:T])
            for b in range(2):
                for t in range(TT):
                    evacuate(("mv", b, t), MV[:, t, b * 512:(b + 1) * 512])
            norm(3, lambda t: hres[:, t, :], lambda t: XN[:, t, :], lambda t: [freed(act, ("wo", b, t)) for b in range(2)])
            for n in range(8):
                evacuate(("cq", n), CQT[:, n, :], src=lambda b: b[:, 0:T])
            for t in range(TT):
                act.wait_ge(S["cl_ready"], t + 1)
                if t == 1:
                    arrived(act, ("cP", 0, 1))
                for p in range(2):
                    b = arrived(act, ("cl", t, p))
                    for c in range(2):
                        h = 2 * p + c
                        ins = func(CL[:, h, :], b[:, c * T:(c + 1) * T], ACT.Exp, bias=smx[:, t, 1, h:h + 1],
                                   scale=MD ** -0.5, accum_out=smx[:, t, 2, h:h + 1])
                    free(ins, ("cl", t, p))
                for m in range(TT):
                    evacuate(("cP", t, m), CPT[:, m, :, tsl(t)], src=quarters)
            for h in range(MH):
                evacuate(("co", h), COT[:, 2 * h:2 * h + 2, :], src=halves)
            norm(4, lambda t: hres[:, t, :], lambda t: XN[:, t, :], lambda t: [freed(act, ("cw", b, t)) for b in range(2)])
            func(c2s[:, :, :].rearrange("p k c -> p (k c)"), col("c2"), ACT.Silu).then_inc(S["silu_c"], 1)
            with act.Fori(0, 2) as i:
                for j in range(8):
                    evacuate(("pq", j), QPT[:, i * 8 + j, :], i, src=lambda b: b[:, 0:T])
            for t in range(TT):
                for q in range(4):
                    evacuate(("sk", t, q), SK[:, t, 4 * q:4 * q + 4, :], src=quarters)
            norm(5, lambda t: CX[:, t, :], lambda t: XN[:, t, :], lambda t: act.wait_ge(in_ctx, 16 * TT))

            def modulation(name, turn=None):
                twice = None if turn is None else turn * 2
                for n, (j, turned) in enumerate(ADA_ORDER):
                    if turned:
                        at = mods[:, 4 * j:4 * j + 4, :] if turn is None else mods[:, bass.ds(turn * 16 + (16 + 4 * j), 4), :]
                        evacuate((name, n), at, twice, src=lambda b: b[:, 0:8].rearrange("p (n c) -> p n c", c=2))
                    else:
                        evacuate((name, n), ADA[:, j % 2, :], twice, src=lambda b: b[0:2, :])

            modulation("ad0")
            for b in range(3):
                for t in range(TT):
                    evacuate(("cp", b, t), CPJ[:, t, b * 512:(b + 1) * 512])
            act.wait_ge(S["ctx_abs"], 1)
            step(func(CLF, CLF, ACT.Exp, scale=-1.0))
            func(CLF, CLF, ACT.Ln, bias=1.0).then_inc(S["ctx_l"], 1)
            act.wait_ge(S["ctx_nk"], 1)
            func(CKK, CKK, ACT.Exp, scale=-1.0).then_inc(S["ctx_k"], 1)
            for d in range(2):
                for t in range(TT):
                    evacuate(("ce", d, t), CEX[:, t, d * 512:(d + 1) * 512], f=ACT.Exp)
            for d in range(2):
                evacuate(("cH", d), h0[:, d], src=quarters)
            for t in range(TT):
                if t == 1:
                    act.wait_ge(S["y_seeded"], 1)
                    func(a3_hi[:, :, :], actT[:, :, :], ACT.Copy).then_inc(S["a3_hi_ready"], 1)
                    with act.Fori(0, 2) as i:
                        modulation("ad1", i)
                act.wait_ge(S["gate_sc"], t + 1)
                func(EAB[:, t, 2, :], EAB[:, t, 2, :], ACT.Exp).then_inc(S["gate_exp"], 1)
            for t in range(TT):
                evacuate(("eTr", t), slots[:, 0:3, tsl(t)], src=lambda b: b[:, 0:384].rearrange("p (x n) -> p x n", x=3))
            act.wait_ge(S["slots_negated"], 1)

            def columns(turn, q):
                for v in range(4):
                    ins = func(COLUMN[q][:, v, :], C("iota"), ACT.Square,
                               bias=slots[:, 3, bass.ds(turn * 16 + (8 * q + v), 1)])
                ins.then_inc(S["square_made"], 1)
                act.wait_ge(S["square_made"], turn * 2 + (q + 1))
                func(COLUMN[q], COLUMN[q], ACT.Relu, scale=-1.0, bias=1.0).then_inc(S["column_ready"], 1)

            def dense(turn, u):
                evacuate(("w", u), WT[:, :, bass.ds(turn * 16 + 4 * u, 4)].rearrange("p n v -> p v n"), turn,
                         src=quarters)

            columns(0, 0)
            columns(0, 1)
            split_high(X0)
            split_high(X0 + 1)
            with act.Fori(0, T // 16 - 1) as i:
                for q in range(2):
                    dense(i, 2 * q)
                    columns(i + 1, q)
                    dense(i, 2 * q + 1)
            for u in range(4):
                dense(T // 16 - 1, u)
            func(GELU[:, 0, :], arrived(act, ("h0",))[:, 0:T], ACT.Gelu).then_inc(bank_free[4], 1)
            split_high(X0 + 2)

            def expert_row(a, e, job, turn=None):
                b = arrived(act, job, turn)
                act.wait_ge(S["p_ready"], (0 if turn is None else turn * 4) + a)
                free(func(GELU[:, a % 2, :], b[:, 0:T], ACT.Gelu), job)
                split_high(X0 + e, turn)
                if e + 1 < EXPERTS:
                    split_high(X0 + e + 1, turn)

            with act.Fori(0, 31) as i:
                for u in range(4):
                    expert_row(u + 1, 2 * u + 3, ("h", u), i)
            for u in range(3):
                expert_row(125 + u, 2 * (124 + u) + 3, ("he", u))
            for t in range(TT):
                for h in range(2):
                    evacuate(("y", t, h), hres[:, t, h * 512:(h + 1) * 512])
            for t in range(TT):
                freed(act, ("y", t, 1))
            norm(6, lambda t: hres[:, t, :], lambda t: XN[:, t, :], lambda t: act.wait_ge(S["p_ready"], P))
            norm(7, lambda t: hres[:, t, :], lambda t: XN[:, t, :], lambda t: act.wait_ge(S["x2_ready"], 2))
            split_high(I0)
            split_high(I0 + 1)
            high_quarters("x2T", x2_hi, lambda n: act.wait_ge(S["act_ready"], 5 + n), "x2_hi_ready")

            def evacuate_p(b):
                for t in range(TT):
                    evacuate(("p", b, t), PJ[:, t, b * 512:(b + 1) * 512],
                             f=ACT.Copy if b < 3 else ACT.Silu if b < 5 else ACT.Gelu)

            split_blocks(I0, 7, evacuate_p)
            evacuate_p(6)
            act.wait_ge(S["g_abs"], 1)
            step(func(LF, LF, ACT.Exp, scale=-1.0))
            func(LF, LF, ACT.Ln, bias=1.0).then_inc(S["g_l"], 1)
            act.wait_ge(S["g_nk"], 1)
            func(K2, K2, ACT.Exp, scale=-1.0).then_inc(S["g_k"], 1)
            for t in range(TT):
                evacuate(("qT2", t), Q2T[:, :, tsl(t)], src=quarters, scale=P ** -0.5)
            for d in range(2):
                for t in range(TT):
                    evacuate(("kT2", d, t), K2T[:, d, :, tsl(t)], src=quarters)
            for d in range(2):
                evacuate(("as", d), KD[:, d, :], f=ACT.Exp)
            evacuate(("tot",), TOTE, f=ACT.Exp, src=lambda b: b[:, 0:8])
            act.wait_ge(S["g_H"], 1)
            for t in range(TT):
                for d in range(2):
                    if t or d:
                        arrived(act, ("gr", t, 0, 6) if d else ("gr", t - 1, 1, 6))
                    for h in range(HH):
                        for half in range(2):
                            evacuate(("e", t, d, h, half), ZQ[:, h, 4 * half:4 * half + 4, :], f=ACT.Exp, src=quarters)
            act.wait_ge(S["o_ms"], 1)
            func(gst[:, 2], gst[:, 1], ACT.Sqrt).then_inc(S["o_root"], 1)
            act.wait_ge(S["gdiag"], 1)
            for r in range(4):
                evacuate(("gb", r), GB[:, r // 2, 512 * (r % 2):512 * (r % 2) + 512])
            for t in range(TT):
                for h in range(2):
                    evacuate(("ocT", t, h), actT[:, 4 * h:4 * h + 4, tsl(t)], src=quarters)
            norm(8, lambda t: hres[:, t, :], lambda t: XN[:, t, :], lambda t: act.wait_ge(S["x3_ready"], 4))

            for r in range(2):
                split_high(F0 + r)
            act.wait_ge(S["act_ready"], 12)
            func(x3_hi[:, :, :], actT[:, :, :], ACT.Copy).then_inc(S["x3_hi_ready"], 1)

            def ffn_gate(job, c, par, turn=None):
                b = arrived(act, job, turn)[:, 0:T]
                func(CV[:, par, :], b, ACT.Identity, scale=col("taps")[:, bass.ds(c * 9 + 4, 1)],
                     bias=col("fconv_b")[:, bass.ds(c, 1)])
                free(func(GC[:, par, :], b, ACT.Copy), job)

            def ffn_gelu(c, par):
                act.wait_ge(S["ffn_conv"], c + 1)
                func(GE[:, par, :], CV[:, par, :], ACT.Gelu).then_inc(S["ffn_gelu"], 1)

            ffn_gate(("g0",), 0, 0)
            split_high(F0 + 2, rests=(S["ffn_lo_ready"], 1))
            split_high(F0 + 3, rests=(S["ffn_lo_ready"], 2))
            with act.Fori(0, (FC - 2) // 2) as i:
                for u in range(2):
                    ffn_gelu(i * 2 + u, u)
                    ffn_gate(("ga", 2 * u), i * 2 + (u + 1), (u + 1) % 2, i)
                    split_high(F0 + 4 + 3 * u, i, 6, (S["ffn_lo_ready"], i * 4 + (3 + 2 * u)))
                    split_high(F0 + 5 + 3 * u, i, 6, (S["ffn_lo_ready"], i * 4 + (4 + 2 * u)))
                    split_high(F0 + 6 + 3 * u, i, 6, (S["ffn_down_lo_ready"], i * 2 + (u + 1)))
            ffn_gelu(FC - 2, 0)
            ffn_gate(("ge",), FC - 1, 1)
            split_high(F0 + 64, rests=(S["ffn_lo_ready"], 43))
            split_high(F0 + 65, rests=(S["ffn_lo_ready"], 44))
            ffn_gelu(FC - 1, 1)
            norm(9, lambda t: hres[:, t, :], lambda t: XN[:, t, :], lambda t: act.wait_ge(S["x4_ready"], 4))

        @block.vector
        def _(dve):
            V = nc.vector
            step = Chain(dve, S["dve_step"])
            ts, tt, stt, cp = V.tensor_scalar, V.tensor_tensor, V.scalar_tensor_tensor, V.tensor_copy

            def signal(ins, name, wait=None):
                ins.then_inc(S[name], 1)
                if wait is not None:
                    dve.wait_ge(S[name], wait)

            def scale_rows(n, width, x, out, gain=None):
                dve.wait_ge(S["norm_sq"], 2 * n + 2)
                signal(ts(stat[:, 1, n, :], stat[:, 0, n, :], 1.0 / width, EPS, ALU.mult, ALU.add), "norm_ms")
                dve.wait_ge(S["norm_root"], n + 1)
                step(V.reciprocal(stat[:, 3, n, :], stat[:, 2, n, :]))
                for t in range(TT):
                    signal(ts(out(t), x(t), stat[:, 3, n, t:t + 1], None, ALU.mult), "xn_ready")

            def features(name, out, gain, shift=None, chunks=2):
                for t in range(TT):
                    for h in range(chunks):
                        b = arrived(dve, (name, t, h)).rearrange("p (k n) -> p k n", k=4)
                        o = out[:, 4 * h:4 * h + 4, tsl(t)]
                        free(tt(o, b, bc(gain[:, 4 * h:4 * h + 4], 2, P), ALU.mult), (name, t, h))
                        if shift is not None:
                            freed(dve, (name, t, h))
                            signal(tt(o, o, bc(shift[:, 4 * h:4 * h + 4], 2, P), ALU.add), "act_ready")

            dve.wait_ge(in_const, 64)
            F = ROPET[:, 0, 0:48].rearrange("p (t f) -> p t f", t=TT)
            posf = ROPET[:, 3, 0:2]
            step(cp(posf, small[:, 616:618].bitcast(I32)))
            step(tt(F, bc(posf, 2, 24), bc(C("freq"), 1, TT), ALU.mult))
            ang = ROPET[:, 0, 0:48]
            for s, (q, shift) in enumerate(((0.0, 0.0), (0.25, float(np.pi / 2)))):
                k = ROPET[:, 1 + s, 0:48]
                r = ROPET[:, 4, 48 * s:48 * s + 48]
                step(ts(k, ang, float(1 / (2 * np.pi)), q, ALU.mult, ALU.add))
                step(ts(k, k, 12582912.0, None, ALU.add))
                step(ts(k, k, -12582912.0, None, ALU.add))
                step(stt(r, k, -TWO_PI[0], ang, ALU.mult, ALU.add))
                step(stt(r, k, -TWO_PI[1], r, ALU.mult, ALU.add))
                step(stt(r, k, -TWO_PI[2], r, ALU.mult, ALU.add))
                step(ts(r, r, shift, float(np.float32(3.1415925)), ALU.add, ALU.min))
                ins = ts(r, r, float(np.float32(-3.1415925)), None, ALU.max)
                if s == 0:
                    step(ins)
            signal(ins, "rope_arg")
            scale_rows(0, D, lambda t: hres[:, t, :], lambda t: XN[:, t, :])
            features("xT", actT, col("g_mix"))

            def rest_quarters(hi, lo_, hi_ready, ready):
                for n in range(4):
                    t, h = n // 2, n % 2
                    dve.wait_ge(S[hi_ready], n + 1)
                    q = (slice(None), slice(4 * h, 4 * h + 4), tsl(t))
                    tt(lo_[q], actT[q], hi[q], ALU.subtract).then_inc(S[ready], 1)

            rest_quarters(x1_hi, x1_lo, "x1_hi_ready", "x1_lo_ready")
            with dve.Fori(0, 3) as i:
                for j in range(8):
                    b = arrived(dve, ("xbc", j), i)
                    o = XBC[:, i * 8 + j, :]
                    wcol = lambda k: col("conv_w")[:, bass.ds(i * 32 + 4 * j + k, 1)]
                    base = i * 24 + (step.c.n + 3 * j)
                    ts(o, b[:, 0:T], wcol(3), col("conv_b")[:, bass.ds(i * 8 + j, 1)], ALU.mult,
                       ALU.add).then_inc(step.c.sem, 1)
                    for m, k in enumerate((2, 1)):
                        dve.wait_ge(step.c.sem, base + (1 + m))
                        stt(o[:, 3 - k:T], b[:, 0:T - 3 + k], wcol(k), o[:, 3 - k:T], ALU.mult,
                            ALU.add).then_inc(step.c.sem, 1)
                    dve.wait_ge(step.c.sem, base + 3)
                    free(stt(o[:, 3:T], b[:, 0:T - 3], wcol(0), o[:, 3:T], ALU.mult, ALU.add), ("xbc", j))
            step.c.n += 72
            for b in range(4):
                for t in range(TT):
                    freed(dve, ("tok", b, t))
            dve.wait_ge(S["rope_sin"], 1)
            for t in range(TT):
                for a, b, hd, heads, f0 in ((0, 1280, DH, 10, 0), (1280, 1600, IDH, 5, 16)):
                    half = hd // 8
                    x = TOK[:, t, a:b].rearrange("p (h d) -> p h d", d=hd)
                    x1, x2 = x[:, :, 0:half], x[:, :, half:2 * half]
                    sin = bc(ROPE[:, 0, t, f0:f0 + half], 1, heads)
                    cos = bc(ROPE[:, 1, t, f0:f0 + half], 1, heads)
                    n = heads * half
                    m = [RT[:, k // 2, (k % 2) * 160:(k % 2) * 160 + n].rearrange("p (h d) -> p h d", d=half)
                         for k in range(4)]
                    tt(m[0], x1, cos, ALU.mult)
                    tt(m[1], x2, sin, ALU.mult)
                    tt(m[2], x2, cos, ALU.mult)
                    step(tt(m[3], x1, sin, ALU.mult))
                    step(tt(x1, m[0], m[1], ALU.subtract))
                    step(tt(x2, m[2], m[3], ALU.add))
                step(cp(IKD[:, t, :].rearrange("p (r d) -> p r d", r=2), bc(TOK[:, t, 1536:1600], 1, 2)))
            ins = ts(IW, TOK[:, :, 1856:1860], IH ** -0.5, None, ALU.mult)
            signal(ins, "rope_ready", 1)
            step(tt(DT, TOK[:, :, 1860:1892], bc(row("dt_bias"), 1, TT), ALU.add))
            signal(stt(DTS, DT, -1.0, DT, ALU.mult, ALU.max), "dt_abs")
            dve.wait_ge(S["dt_l"], 1)
            dve.wait_ge(S["neg_a"], 1)
            step(stt(DT, DT, 0.0, DTL, ALU.max, ALU.add))
            signal(stt(ADT, DT, -1.0, bc(NEGA, 1, TT), ALU.mult, ALU.mult), "adt_ready", 1)
            best = [smx[:, 0, 0, :], smx[:, 1, 0, :]]
            for t in range(TT):
                w = P * (t + 1)
                sc, left = SC[:, 2 * t, 0:w], SC[:, 2 * t + 1, 0:w]
                for r in range(2):
                    freed(dve, ("idx", t, r))
                step(ts(sc, RELU[:, 2 * t, 0, 0:w], IW[:, t, 0:1], None, ALU.mult))
                for h in range(1, IH):
                    step(stt(sc, RELU[:, 2 * t + h % 2, h // 2, 0:w], IW[:, t, h:h + 1], sc, ALU.mult, ALU.add))
                step(tt(sc[:, w - P:w], sc[:, w - P:w], C("causal"), ALU.add))
                for n in range(TOPK // 8):
                    src = sc if n == 0 else left
                    step(V.max(best[t], src))
                    step(V.match_replace(out=left, in_to_replace=best[t], in_values=src, imm_value=TAKEN))
                step(tt(left, left, sc, ALU.not_equal))
                step(stt(left, sc, -1.0e38, left, ALU.is_gt, ALU.mult))
                step(ts(left, left, -OFF, OFF, ALU.mult, ALU.add))
            for t in range(TT):
                w = P * (t + 1)
                for p in range(4):
                    b = arrived(dve, ("lg", t, p)).rearrange("p (c n) -> p c n", c=2)
                    free(tt(LG[t][:, 2 * p:2 * p + 2, :], b[:, :, 0:w], bc(SC[:, 2 * t + 1, 0:w], 1, 2), ALU.add),
                         ("lg", t, p))
                for p in range(4):
                    freed(dve, ("lg", t, p))
                step(V.tensor_reduce(smx[:, t, 0, :], LG[t], AX.X, ALU.max))
                signal(ts(smx[:, t, 1, :], smx[:, t, 0, :], -(DH ** -0.5), None, ALU.mult), "attn_masked")
            for t in range(TT):
                dve.wait_ge(S["attn_exp"], t + 1)
                step(V.reciprocal(smx[:, t, 3, :], smx[:, t, 2, :]))
                signal(tt(LG[t], LG[t], bc(smx[:, t, 3, :], 2, P * (t + 1)), ALU.mult), "attn_prob")
            b = arrived(dve, ("acs",))
            free(cp(ACS, b[:, 0:128].rearrange("p (c h) -> p c h", c=4)), ("acs",))
            freed(dve, ("acs",))
            signal(tt(DTE, ACS[:, 2, :], ACS[:, 0, :], ALU.subtract), "acs_ready")
            for t in range(TT):
                for q in range(4):
                    freed(dve, ("xsTr", t, q))
            freed(dve, ("PTr", 1, 3))
            heads = lambda ap: ap.rearrange("p (h d) -> p h d", d=SP_)
            for t in range(TT):
                tt(heads(YT_[:, t, :]), heads(XS[:, t, :]), bc(row("d_skip"), 2, SP_), ALU.mult)
            for t in range(TT):
                ins = tt(heads(XS[:, t, :]), heads(XS[:, t, :]), bc(DT[:, t, :], 2, SP_), ALU.mult)
            step(ins)
            dve.wait_ge(S["acs_exp"], 1)
            signal(tt(heads(XDTD), heads(XS[:, 0, :]), bc(DTE, 2, SP_), ALU.mult), "xdtd_ready")
            for kv in range(KVH):
                arrived(dve, ("oT", 1, kv))
            for c in range(TT):
                b = arrived(dve, ("cb", c)).rearrange("p (g l) -> p g l", g=SG)
                free(tt(CBM[:, c], b, bc(C("upto"), 1, SG), ALU.mult), ("cb", c))
                freed(dve, ("cb", c))
            n_groups = TT * SG

            def adt_rows(k):
                c, g = k // SG, k % SG
                signal(cp(ADTB[:, k % 2], bc(ADT[:, c, 8 * g:8 * g + 8], 2, P)), "adtb_ready")

            adt_rows(0)
            for k in range(n_groups + 1):
                if k + 1 < n_groups:
                    adt_rows(k + 1)
                if k < n_groups:
                    c, g = k // SG, k % SG
                    for half in range(2):
                        b = arrived(dve, ("row", c, g, half))
                        for j in range(4):
                            h = 8 * g + 4 * half + j
                            ins = ts(EM[:, k % 2, 4 * half + j, :], b[:, hsl(j)], ACS[:, c, h:h + 1], 0.0,
                                     ALU.subtract, ALU.min)
                        free(ins, ("row", c, g, half))
                if k >= 1:
                    c, g = (k - 1) // SG, (k - 1) % SG
                    gs = slice(g * 512, (g + 1) * 512)
                    if c == 0:
                        b = arrived(dve, ("yd", c, g))
                        free(tt(YT_[:, 0, gs], YT_[:, 0, gs], b, ALU.add), ("yd", c, g))
                        free(cp(STATE[:, g, :], arrived(dve, ("st", g))), ("st", g))
                    else:
                        b = arrived(dve, ("yo", g))
                        free(tt(heads(XDTD[:, gs]), heads(b), bc(EAC[:, 1, 8 * g:8 * g + 8], 2, SP_), ALU.mult),
                             ("yo", g))
                        freed(dve, ("yo", g))
                        step(tt(YT_[:, 1, gs], YT_[:, 1, gs], XDTD[:, gs], ALU.add))
                        b = arrived(dve, ("yd", c, g))
                        free(tt(YT_[:, 1, gs], YT_[:, 1, gs], b, ALU.add), ("yd", c, g))
                if k < n_groups:
                    c, g = k // SG, k % SG
                    dve.wait_ge(S["seg_exp"], k + 1)
                    signal(tt(EM[:, k % 2], EM[:, k % 2], bc(CBM[:, c, g, :], 1, 8), ALU.mult), "m_ready")
            scale_rows(1, D, lambda t: MEMX[:, t, :], lambda t: XN[:, t, :])
            features("mT", MT, col("g_mem"))
            for b in range(4):
                for t in range(TT):
                    freed(dve, ("z", b, t))
            for g in range(SG):
                freed(dve, ("yd", 1, g))
            for t in range(TT):
                signal(tt(YT_[:, t, :], YT_[:, t, :], ZT[:, t, :], ALU.mult), "y_ready")
            scale_rows(2, SD, lambda t: YT_[:, t, :], lambda t: YT_[:, t, :])
            features("yTr", YT, col("g_ssd"), chunks=4)
            for j in range(8):
                freed(dve, ("gate", j), 1)
            for n in range(8):
                part = area(28672 + T * (n % 2), T)
                free(tt(part, GT[:, n, :], arrived(dve, ("ma", n))[:, 0:T], ALU.mult), ("ma", n))
                free(tt(MG[:, n, :], GT[:, 8 + n, :], arrived(dve, ("ms", n))[:, 0:T], ALU.mult), ("ms", n))
                freed(dve, ("ma", n))
                freed(dve, ("ms", n))
                signal(tt(MG[:, n, :], MG[:, n, :], part, ALU.add), "merged_ready")

            def add_residual(name):
                for b in range(2):
                    for t in range(TT):
                        h = hres[:, t, b * 512:(b + 1) * 512]
                        free(tt(h, h, arrived(dve, (name, b, t)), ALU.add), (name, b, t))
                for b in range(2):
                    for t in range(TT):
                        freed(dve, (name, b, t))

            add_residual("wo")
            scale_rows(3, D, lambda t: hres[:, t, :], lambda t: XN[:, t, :])
            features("a2T", actT, col("g_cross"))
            for t in range(TT):
                for p in range(2):
                    b = arrived(dve, ("cl", t, p)).rearrange("p (c n) -> p c n", c=2)
                    ins = V.tensor_reduce(smx[:, t, 0, 2 * p:2 * p + 2], b, AX.X, ALU.max)
                step(ins)
                signal(ts(smx[:, t, 1, 0:4], smx[:, t, 0, 0:4], -(MD ** -0.5), None, ALU.mult), "cl_ready")
                for p in range(2):
                    freed(dve, ("cl", t, p))
                step(V.reciprocal(smx[:, t, 3, 0:4], smx[:, t, 2, 0:4]))
                signal(tt(CL, CL, bc(smx[:, t, 3, 0:4], 2, T), ALU.mult), "cprob")
            add_residual("cw")
            scale_rows(4, D, lambda t: hres[:, t, :], lambda t: XN[:, t, :])
            features("a3T", actT, col("g_ffn"))

            def top16(groups, src, work, val, idx):
                for g in groups:
                    ins = V.max(val(g)[:, 0:8], src(g))
                step(ins)
                for g in groups:
                    V.max_index(idx(g)[:, 0:8], val(g)[:, 0:8], src(g))
                    ins = V.match_replace(out=work(g), in_to_replace=val(g)[:, 0:8], in_values=src(g),
                                          imm_value=TAKEN)
                step(ins)
                for g in groups:
                    ins = V.max(val(g)[:, 8:16], work(g))
                step(ins)
                for g in groups:
                    ins = V.max_index(idx(g)[:, 8:16], val(g)[:, 8:16], work(g))
                step(ins)

            idxu = TOPI.bitcast(U32)
            sciu = SCI.bitcast(U32)
            ciau = CIA.bitcast(U32)

            def best_keys(t):
                for q in range(4):
                    freed(dve, ("sk", t, q))
                top16(range(16), lambda g: SK[:, t, g, :], lambda g: SK2[:, g, :], lambda g: TOPV[:, g, :],
                      lambda g: idxu[:, g, :])

            def best_pairs(t):
                v = TOPV.rearrange("p (h x) k -> p h x k", x=2)
                step(tt(CAND.rearrange("p h (i j) -> p h i j", j=PTOP), bc(v[:, :, 0, :], 3, PTOP),
                        bc(v[:, :, 1, :], 2, PTOP), ALU.add))
                top16(range(PH), lambda g: CAND[:, g, :], lambda g: CAND2[:, g, :], lambda g: SCV[:, g, :],
                      lambda g: sciu[:, g, :])
                flat = sciu.rearrange("p h k -> p (h k)")
                ts(ciau[:, 0, :], flat, 4, None, ALU.logical_shift_right)
                ts(ciau[:, 1, :], flat, 15, None, ALU.bitwise_and)
                step(cp(TOPIF, idxu))
                step(cp(CIAF, ciau))
                num = TOPIF.rearrange("p (h x) k -> p h x k", x=2)
                oh4 = OH.rearrange("p (h k j) -> p h k j", h=PH, k=PTOP)
                oh3 = OH.rearrange("p (s j) -> p s j", j=PTOP)
                for x in range(2):
                    step(tt(oh3, bc(CIAF[:, x, :], 2, PTOP), bc(C("iota16"), 1, P), ALU.is_equal))
                    step(tt(oh4, oh4, bc(num[:, :, x, :], 2, PTOP), ALU.mult))
                    step(V.tensor_reduce(EAB[:, t, x, :], oh3, AX.X, ALU.add))

            def gates(t):
                g3 = EAB[:, t, 2, :].rearrange("p (h k) -> p h k", h=PH)
                signal(tt(g3, SCV, bc(SCV[:, :, 0], 2, PTOP), ALU.subtract), "gate_sc")
                dve.wait_ge(S["gate_exp"], t + 1)
                step(V.tensor_reduce(SMX, g3, AX.X, ALU.add))
                step(V.reciprocal(SMX, SMX))
                signal(tt(g3, g3, bc(SMX, 2, PTOP), ALU.mult), "idx_ready")

            scale_rows(5, D, lambda t: CX[:, t, :], lambda t: XN[:, t, :])
            best_keys(0)
            freed(dve, ("ad0", ADA_JOB[3, 1]))
            step(tt(mods[:, 0:16, :], mods[:, 0:16, :], bc(col("b_ada")[:, 0:16], 2, 2), ALU.add))
            stt(modsb[:, 0:8], mods[:, 8:16, 0], 1.0, col("g_mix2"), ALU.add, ALU.mult)
            stt(modsb[:, 8:16], mods[:, 8:16, 1], 1.0, col("g_mix2"), ALU.add, ALU.mult)
            cp(modsb[:, 40:48], mods[:, 0:8, 0])
            step(cp(modsb[:, 48:56], mods[:, 0:8, 1]))
            features("cT", CXT, modsb[:, 8:16], modsb[:, 48:56])
            best_pairs(0)

            def gate_logs(f, lf, nk, names):
                signal(stt(lf, f, -1.0, f, ALU.mult, ALU.max), names[0])
                dve.wait_ge(S[names[1]], 1)
                signal(stt(nk, f, 0.0, lf, ALU.max, ALU.add), names[2])
                signal(stt(lf, f, 0.0, lf, ALU.min, ALU.subtract), names[3], 1)

            for b in range(3):
                for t in range(TT):
                    freed(dve, ("cp", b, t))
            gate_logs(CPJ[:, :, 0:1024], CLF, CKK, ("ctx_abs", "ctx_l", "ctx_nk", "ctx_f"))
            dve.wait_ge(S["ctx_k"], 1)
            for d in range(2):
                for t in range(TT):
                    freed(dve, ("ce", d, t))
            signal(tt(CKK, CKK, CEX, ALU.mult), "ctx_kd")
            gates(0)
            best_keys(1)
            best_pairs(1)
            gates(1)
            freed(dve, ("ad1", ADA_JOB[3, 1]), 2)
            step(tt(mods[:, 16:48, :], mods[:, 16:48, :], bc(col("b_ada")[:, 16:48], 2, 2), ALU.add))
            stt(modsb[:, 16:24], mods[:, 32:40, 0], 1.0, col("g_ffn2"), ALU.add, ALU.mult)
            cp(modsb[:, 24:32], mods[:, 24:32, 0])
            for t in range(TT):
                freed(dve, ("eTr", t))
            ts(slots[:, 3, :], slots[:, 1, :], -1.0, None, ALU.mult).then_inc(S["slots_negated"], 1)
            dve.wait_ge(S["a3_hi_ready"], 1)
            tt(a3_lo[:, :, :], actT[:, :, :], a3_hi[:, :, :], ALU.subtract).then_inc(S["a3_lo_ready"], 1)
            with dve.Fori(0, T // 16) as i:
                for u in range(4):
                    job = ("w", (u + 2) % 4)
                    dve.wait_ge(bank_full[B.at[job][0]], i + (B.at[job][1] - (u < 2)))
                    if u % 2:
                        tt(ONEHOT[:, 1, :, 1, :], bc(C("iota"), 1, 4),
                           bc(slots[:, 1, bass.ds(i * 16 + 4 * u, 4)], 2, P), ALU.is_equal)
                    for v in range(4):
                        s = lambda x: slots[:, x, bass.ds(i * 16 + (4 * u + v), 1)]
                        ins = ts(ONEHOT[:, u % 2, v, 0, :], C("iota"), s(0), s(2), ALU.is_equal, ALU.mult)
                    ins.then_inc(S["onehot_ready"], 1)

            def split_rest(e, ready, turn=None, n=8):
                i_ = 0 if turn is None else turn
                dve.wait_ge(S["hi_ready"], i_ * n + (e + 1))
                dve.wait_ge(S["hi_used"], i_ * n + e)
                tt(w_lo[:, e % 2, :], raw(e)[0], w_hi[:, e % 2, :], ALU.subtract).then_inc(S[ready], 1)

            def split_product(out, hi, lo_, x, y, made, count, ready):
                tt(out, x, y, ALU.mult).then_inc(made, 1)
                ins = tt(hi, x, y, ALU.mult)
                ins.then_inc(made, 1)
                dve.wait_ge(made, count)
                tt(lo_, out, hi, ALU.subtract).then_inc(S[ready], 1)
                return ins

            for e in range(2):
                split_rest(X0 + e, "lo_ready")
            freed(dve, ("h0",))
            for u in range(4):
                freed(dve, ("w", u), T // 16 - 1)

            def gate_row(a, turn=None):
                n = 0 if turn is None else turn * 4
                row_ = WT[:, a, :] if turn is None else WT[:, turn * 4 + a, :]
                split_product(GATED, gated_hi[:, a % 2, :], gated_lo[:, a % 2, :], GELU[:, a % 2, :], row_,
                              S["gated_made"], n * 2 + (2 * a + 2), "p_ready")

            gate_row(0)
            split_rest(X0 + 2, "lo_ready")
            with dve.Fori(0, 31) as i:
                for u in range(4):
                    freed(dve, ("h", u), i)
                    gate_row(u + 1, i)
                    split_rest(X0 + 2 * u + 3, "lo_ready", i)
                    split_rest(X0 + 2 * u + 4, "lo_ready", i)
            for u in range(3):
                a = 125 + u
                freed(dve, ("he", u))
                gate_row(a)
                split_rest(X0 + 2 * a + 1, "lo_ready")
                if a < 127:
                    split_rest(X0 + 2 * a + 2, "lo_ready")
            scale_rows(6, D, lambda t: hres[:, t, :], lambda t: XN[:, t, :])
            dve.wait_ge(in_second, 4 * 16)
            for t in range(TT):
                dve.wait_ge(S["xn_ready"], 6 * TT + t + 1)
                signal(tt(hres[:, t, :], XN[:, t, :], FIN1, ALU.mult), "x2_ready")
            scale_rows(7, D, lambda t: hres[:, t, :], lambda t: XN[:, t, :])
            features("x2T", actT, modsb[:, 0:8], modsb[:, 40:48])
            rest_quarters(x2_hi, x2_lo, "x2_hi_ready", "x2_lo_ready")
            for b in range(7):
                for t in range(TT):
                    freed(dve, ("p", b, t))
                if b == 1:
                    gate_logs(PJ[:, :, 0:1024], LF, K2, ("g_abs", "g_l", "g_nk", "g_logf"))
            dve.wait_ge(S["g_k"], 1)
            for d in range(2):
                freed(dve, ("as", d))
                signal(tt(KD[:, d, :], KD[:, d, :], K2[:, d, d * 512:(d + 1) * 512], ALU.mult), "g_kd")
            freed(dve, ("tot",))
            for d in range(2):
                b = arrived(dve, ("adv", d))
                for h in range(HH):
                    ins = stt(HS[:, d, h, :], h0[:, d, h, :], TOTE[:, d * 4 + h:d * 4 + h + 1], b[:, hsl(h)],
                              ALU.mult, ALU.add)
                free(ins, ("adv", d))
            for d in range(2):
                for t in range(TT):
                    freed(dve, ("kT2", d, t))
            for t in range(TT):
                freed(dve, ("qT2", t))
            signal(tt(KS, K2T[:, 0], K2T[:, 1], ALU.add), "g_H")
            dve.wait_ge(in_second, 5 * 16)
            for t in range(TT):
                b = arrived(dve, ("dg", t)).rearrange("p (h n) -> p h n", h=HH)
                free(tt(SM, b, bc(ident, 1, HH), ALU.mult), ("dg", t))
                freed(dve, ("dg", t))
                for d in range(2):
                    for h in range(HH):
                        for half in range(2):
                            freed(dve, ("e", t, d, h, half))
                        q = Q2T[:, h, tsl(t)]
                        tt(ZK[:, h], ZQ[:, h, 0:7, :], bc(K2T[:, d, h, tsl(t)], 1, 7), ALU.mult)
                        tt(ZP[:, d, h, :], ZQ[:, h, 7, :], q, ALU.mult)
                        ins = tt(ZQ[:, h, 0:7, :], ZQ[:, h, 0:7, :], bc(q, 1, 7), ALU.mult)
                    signal(ins, "z_made")
                    for lev in range(N_LEVELS):
                        b = arrived(dve, ("gr", t, d, lev)).rearrange("p (h n) -> p h n", h=HH)
                        m = bc(LEV[:, d * 7 + lev, :].bitcast(U32), 1, HH)
                        free(V.copy_predicated(SM, m, b), ("gr", t, d, lev))
                        freed(dve, ("gr", t, d, lev))
                free(cp(PJ[:, t, 0:512], arrived(dve, ("o", t))), ("o", t))
            h4 = lambda ap: ap.rearrange("p t (h n) -> p t h n", h=HH)
            O, SQ, VV = PJ[:, :, 0:512], PJ[:, :, 512:1024], PJ[:, :, 3072:3584]
            for t in range(TT):
                freed(dve, ("o", t))
            step(V.tensor_reduce(gst[:, 3, 1], h4(VV), AX.X, ALU.add))
            step(ts(gst[:, 3, 1], gst[:, 3, 1], 1.0 / P, None, ALU.mult))
            tt(SQ, O, O, ALU.mult)
            step(tt(h4(VV), h4(VV), bc(gst[:, 3, 1], 3, P), ALU.subtract))
            step(V.tensor_reduce(gst[:, 0, 0], h4(SQ), AX.X, ALU.add))
            step(tt(SQ, VV, VV, ALU.mult))
            step(V.tensor_reduce(gst[:, 0, 1], h4(SQ), AX.X, ALU.add))
            signal(ts(gst[:, 1], gst[:, 0], 1.0 / P, EPS, ALU.mult, ALU.add), "o_ms")
            dve.wait_ge(S["o_root"], 1)
            step(V.reciprocal(gst[:, 3], gst[:, 2]))
            tt(h4(O), h4(O), bc(gst[:, 3, 0], 3, P), ALU.mult)
            step(tt(h4(VV), h4(VV), bc(gst[:, 3, 1], 3, P), ALU.mult))
            tt(O, O, bc(R2[:, 0:512], 1, TT), ALU.mult)
            step(tt(VV, VV, bc(R2[:, 512:1024], 1, TT), ALU.mult))
            tt(OC[:, :, 0:512], O, PJ[:, :, 2048:2560], ALU.mult)
            signal(tt(VV, VV, bc(R2[:, 1024:1536], 1, TT), ALU.add), "v_ready")
            tt(GBD[:, 0], bc(ident, 1, KC), bc(mods[:, 16:24, 0], 2, P), ALU.mult)
            signal(tt(GBD[:, 1], bc(ident, 1, KC), bc(mods[:, 40:48, 0], 2, P), ALU.mult), "gdiag")
            signal(V.memset(ZEROS, 0.0), "zeros_ready")
            for t in range(TT):
                b = arrived(dve, ("sg", t)).rearrange("p (h n) -> p h n", h=HH)
                v = PJ[:, t, 512:1024]
                free(tt(v.rearrange("p (h n) -> p h n", h=HH), b, bc(col("b_s"), 2, P), ALU.add), ("sg", t))
                freed(dve, ("sg", t))
                signal(tt(OC[:, t, 512:1024], v, PJ[:, t, 2560:3072], ALU.mult), "oc_ready")
            for r in range(4):
                freed(dve, ("gb", r))

            def add_gated(name, g, done, order):
                for n, (b, t) in enumerate(order):
                    s = slice(b * 512, (b + 1) * 512)
                    job = (name, b, t) if name == "w2" else (name, t, b)
                    free(tt(T512[:, n, :], arrived(dve, job), GB[:, g, s], ALU.mult), job)
                    freed(dve, job)
                    signal(tt(hres[:, t, s], hres[:, t, s], T512[:, n, :], ALU.add), done)
                dve.wait_ge(S[done], 4)

            add_gated("w2", 0, "x3_ready", [(b, t) for b in range(2) for t in range(TT)])
            scale_rows(8, D, lambda t: hres[:, t, :], lambda t: XN[:, t, :])
            features("x3T", actT, modsb[:, 16:24], modsb[:, 24:32])

            grid = lambda ap: ap.rearrange("p (r w) -> p r w", w=GW)
            R = T // GW

            dve.wait_ge(S["x3_hi_ready"], 1)
            tt(x3_lo[:, :, :], actT[:, :, :], x3_hi[:, :, :], ALU.subtract).then_inc(S["x3_lo_ready"], 1)
            for r in range(2):
                split_rest(F0 + r, "ffn_lo_ready")

            def conv_channels(gate_job, c, base, par, turn=None, meanwhile=None):
                freed(dve, gate_job, turn)
                tap = lambda k: col("taps")[:, bass.ds(c * 9 + k, 1)]
                x, o = grid(GC[:, par, :]), grid(CV[:, par, :])
                for n, k in enumerate((0, 1, 2, 3, 5, 6, 7, 8)):
                    dr, dw = k // 3 - 1, k % 3 - 1
                    ro, wo = slice(max(0, -dr), R - max(0, dr)), slice(max(0, -dw), GW - max(0, dw))
                    ri, wi = slice(max(0, dr), R + min(0, dr)), slice(max(0, dw), GW + min(0, dw))
                    if n:
                        dve.wait_ge(step.c.sem, base + n)
                    ins = stt(o[:, ro, wo], x[:, ri, wi], tap(k), o[:, ro, wo], ALU.mult, ALU.add)
                    ins.then_inc(step.c.sem if k < 8 else S["ffn_conv"], 1)
                    if n == 5 and meanwhile:
                        meanwhile()

            def hidden_channels(value_job, c, par, turn=None):
                dve.wait_ge(S["ffn_gelu"], c + 1)
                b = arrived(dve, value_job, turn)[:, 0:T]
                tt(HF, GE[:, par, :], b, ALU.mult).then_inc(S["hidden_made"], 1)
                free(tt(hidden_hi[:, par, :], GE[:, par, :], b, ALU.mult), value_job)
                dve.wait_ge(S["hidden_made"], c + 1)
                freed(dve, value_job, turn)
                tt(hidden_lo[:, par, :], HF, hidden_hi[:, par, :], ALU.subtract).then_inc(S["hidden_ready"], 1)

            n0 = step.c.n
            per = 7
            conv_channels(("g0",), 0, n0, 0, meanwhile=lambda: split_rest(F0 + 2, "ffn_lo_ready"))
            split_rest(F0 + 3, "ffn_lo_ready")
            hidden_channels(("a0",), 0, 0)
            with dve.Fori(0, (FC - 2) // 2) as i:
                for u in range(2):
                    conv_channels(("ga", 2 * u), i * 2 + (u + 1), i * (2 * per) + (n0 + per * (u + 1)), (u + 1) % 2, i,
                                  lambda: split_rest(F0 + 5 + 3 * u, "ffn_lo_ready", i, 6))
                    split_rest(F0 + 6 + 3 * u, "ffn_lo_ready", i, 6)
                    hidden_channels(("ga", 2 * u + 1), i * 2 + (u + 1), (u + 1) % 2, i)
            conv_channels(("ge",), FC - 1, n0 + per * (FC - 1), 1)
            hidden_channels(("ae",), FC - 1, 1)
            step.c.n = n0 + per * FC
            add_gated("f", 1, "x4_ready", [(b, t) for t in range(TT) for b in range(2)])
            scale_rows(9, D, lambda t: hres[:, t, :], lambda t: XN[:, t, :])
            dve.wait_ge(in_second, 6 * 16)
            for t in range(TT):
                dve.wait_ge(S["xn_ready"], 9 * TT + t + 1)
                signal(tt(XN[:, t, :], XN[:, t, :], FIN2, ALU.mult), "out_ready")


def chunk_columns(v):
    return v.reshape(-1, P).T


def token_tiles(w):
    n = w.shape[1] // 512
    return w.reshape(4, 2, P, n, 512).transpose(3, 0, 2, 1, 4).reshape(4 * n, P, 1024)


def feature_tiles(w):
    n = w.shape[1] // P
    return w.reshape(KC, P, n, P).transpose(2, 1, 0, 3).reshape(n, P, 1024)


def constants():
    i = np.arange(P)
    c = np.zeros((P, N_CONST), np.float32)

    def put(name, v):
        o, w = CONST[name]
        c[:, o:o + w] = v

    put("ident", np.eye(P))
    put("upto", i[:, None] <= i[None, :])
    put("ones", 1.0)
    put("after", i[:, None] > i[None, :])
    put("before", i[:, None] < i[None, :])
    put("causal", np.where(i[None, :] <= i[:, None], 0.0, NEG))
    put("iota", i[None, :])
    put("iota16", np.arange(16)[None, :])
    f = np.float32(THETA) ** (np.float32(-2.0) * np.arange(16, dtype=np.float32) / np.float32(32))
    g = np.float32(THETA) ** (np.float32(-2.0) * np.arange(8, dtype=np.float32) / np.float32(16))
    put("freq", np.concatenate([f, g])[None, :])
    u, pos = i[:, None], i[None, :]
    span = np.zeros((P, 2, N_LEVELS + 1, P), np.float32)
    lev = np.zeros((P, 14, P), np.float32)
    s, t = i[:, None], i[None, :]
    for m in range(N_LEVELS):
        w = 1 << m
        mid = pos // (2 * w) * (2 * w) + w
        up = pos >= mid
        span[:, 0, m] = np.where(up, (u >= mid) & (u <= pos), (u > pos) & (u < mid))
        span[:, 1, m] = np.where(up, (u >= mid) & (u < pos), (u >= pos) & (u < mid))
        same = s // (2 * w) == t // (2 * w)
        lev[:, m] = same & (s % (2 * w) < w) & (t % (2 * w) >= w)
        lev[:, 7 + m] = same & (s % (2 * w) >= w) & (t % (2 * w) < w)
    span[:, 0, N_LEVELS] = u <= pos
    span[:, 1, N_LEVELS] = u >= pos
    return c, span.reshape(P, 2, -1), lev


def kernel(**inputs):
    import concourse.bacc as _bacc
    from concourse.bass_utils import run_bass_kernel_spmd as _run

    a = {k: np.asarray(v) for k, v in inputs.items()}
    w_in = a["w_in"][0]
    o = np.cumsum([0, 1024, 256, 256, 256, 64, 4, 2048, 3072, 32, 2048])
    q, k, v, iq, ik, iw, z, xbc, dt, gate = (w_in[:, o[n]:o[n + 1]] for n in range(10))
    tok = np.concatenate([q, k, iq, ik, v, iw, dt, np.zeros((D, 2048 - 1892), np.float32)], axis=1)
    ws = a["w_ssd_branch"][0]
    wa, ws0, ws1 = feature_tiles(a["w_attn_branch"][0]), feature_tiles(ws[:1024]), feature_tiles(ws[1024:])
    merge = np.stack([wa, ws0, ws1], axis=1).reshape(24, P, 1024)
    kv = a["w_cross_kv"][0]
    w2 = a["w_in_2"][0]
    ut = a["peer_u"][0].reshape(P, P, KC, P).transpose(0, 3, 2, 1).reshape(P, P, 1024)
    vt = a["peer_v"][0].reshape(P, P, 1024)
    up = a["w_up_2"][0]
    gt, at = feature_tiles(up[:, FF:]), feature_tiles(up[:, :FF])
    dn = a["w_down_2"][0].reshape(FC, P, 1024)
    ada = token_tiles(a["w_ada_2"][0])
    parts = [token_tiles(tok), feature_tiles(xbc), token_tiles(z), feature_tiles(gate), feature_tiles(kv[:, :1024]),
             token_tiles(kv[:, 1024:]), merge, token_tiles(a["w_out"][0]), feature_tiles(a["w_cross_q"][0]),
             token_tiles(a["w_cross_out"][0]), feature_tiles(a["w_peer_q"][0]), ada[:16],
             token_tiles(w2[:, :1536]), ada[16:],
             ut[0:1], np.stack([ut[1:], vt[:-1]], axis=1).reshape(254, P, 1024), vt[-1:],
             token_tiles(w2), token_tiles(a["w_out_2"][0]),
             gt[0:1], at[0:1], np.stack([gt[1:], at[1:], dn[:-1]], axis=1).reshape(63, P, 1024), dn[-1:]]
    stream = np.concatenate(parts, axis=0)
    assert stream.shape[0] == N_RING + N_FFN
    cols = np.zeros((P, N_COLS), np.float32)
    pc = chunk_columns
    conv = a["conv_w"][0][:, 0, :].T.reshape(24, P, 4).transpose(1, 0, 2).reshape(P, 96)
    taps = a["conv_w_2"][0].reshape(9, FC, P).transpose(2, 1, 0).reshape(P, 198)
    cc = np.stack([pc(a["c_2"][0]), pc(a["c_ctx_2"])], axis=2).reshape(P, 16)
    for name, val in [("g_mix", pc(a["norm_mix_g"][0])), ("g_cross", pc(a["norm_cross_g"][0])),
                      ("g_mem", pc(a["norm_mem_g"][0])), ("g_ffn", pc(a["norm_ffn_g"][0])),
                      ("g_ssd", pc(a["ssd_norm_g"][0])), ("conv_w", conv), ("conv_b", pc(a["conv_b"][0])),
                      ("c2", cc), ("b_ada", pc(a["b_ada_2"][0])), ("g_mix2", pc(a["norm_mix_2"][0])),
                      ("g_ffn2", pc(a["norm_ffn_2"][0])), ("taps", taps), ("fconv_b", pc(a["conv_b_2"][0])),
                      ("b_s", a["b_spatial_2"][0].T)]:
        c0, w = COLS[name]
        cols[:, c0:c0 + w] = val
    const, span, lev = constants()
    arrays = {
        "stream": stream, "x": a["x"], "mem": a["mem"], "ctx": a["ctx_2"], "const": const, "cols": cols,
        "rows": np.concatenate([a["dt_bias"][0], a["a_log"][0], a["d_skip"][0]]),
        "pos": np.ascontiguousarray(a["positions"][0].reshape(TT, P).T.astype(np.int32)),
        "keys": np.ascontiguousarray(a["peer_sub_keys"][0].transpose(3, 0, 1, 2).reshape(P, 16, P)),
        "fin1": a["norm_final_g"], "fin2": a["norm_final_2"],
        "rows2": np.concatenate([a["hg_norm_2"][0], a["sgu_norm_g_2"][0], a["sgu_norm_b_2"][0]]),
        "levels": lev, "span": span,
        "wsp": np.ascontiguousarray(a["w_spatial_2"][0].transpose(2, 0, 1)),
    }
    nc = _bacc.Bacc("TRN2", target_bir_lowering=False, num_devices=1)
    aps = {n: nc.dram_tensor(f"in_{n}", list(v.shape), mybir.dt.from_np(v.dtype), kind="ExternalInput").ap()
           for n, v in arrays.items()}
    aps["out"] = nc.dram_tensor("out", [1, T, D], F32, kind="ExternalOutput").ap()
    build(nc, aps)
    r = _run(nc, [{f"in_{n}": v for n, v in arrays.items()}], core_ids=[0])
    return r.results[0]["out"]
```

```python
from contextlib import ExitStack

import numpy as np

import concourse.bass as bass
from concourse import mybir

P = 128
T = 256
TT = T // P
D = 1024
KC = D // P
EPS = 1e-6
TWO_PI = [6.28125, float(np.float32(2 * np.pi - 6.28125) // 2**-20 * 2**-20), 0.0]
TWO_PI[2] = float(2 * np.pi - TWO_PI[0] - TWO_PI[1])
NEG = -3.0e38
TAKEN = -3.4e38
OFF = -1.0e30

QH, KVH, DH = 8, 2, 128
IH, IDH = 4, 64
TOPK = T // 4
SH, SP_, SG, SN = 32, 64, 4, 128
SD = SH * SP_
MH, MD = 4, 256
PH, PK, PTOP = 8, 128, 16
PSLOT = PH * PTOP
HG, HH = 512, 4
FF, FC = 2816, 22
GW = 64
THETA = 500000.0

F32 = mybir.dt.float32
U32 = mybir.dt.uint32
F32R = mybir.dt.float32r
I32 = mybir.dt.int32
ALU = mybir.AluOpType
ACT = mybir.ActivationFunctionType
AX = mybir.AxisListType

SECTIONS = [
    ("in_tok", 16), ("in_xbc", 24), ("in_z", 16), ("in_gate", 16), ("mem_k", 8), ("mem_v", 8), ("merge", 24),
    ("w_out", 8), ("cross_q", 8), ("cross_out", 8), ("peer_q", 16), ("ada0", 16), ("ctx", 12),
    ("ada1", 16), ("ada2", 16),
    ("experts", 2 * P), ("in2", 28), ("out2", 8),
]
FIRST = {}
_n = 0
for _name, _count in SECTIONS:
    FIRST[_name] = _n
    _n += _count
RING = 4
N_RING = _n
EXP0 = FIRST["experts"]
EXPERTS = 2 * P
AFTER = EXP0 + EXPERTS
FRONT = FIRST["ada0"]
X0 = FRONT
N_IN2 = FIRST["out2"] - FIRST["in2"]
I0 = X0 + EXPERTS
F0 = I0 + N_IN2
assert FRONT % RING == 0 and X0 % 2 == I0 % 2 == F0 % 2 == 0
assert EXP0 % RING == 0 and EXPERTS % RING == 0 and N_RING % RING == 0
FRING = 6
N_FFN = 3 * FC
FFN0 = N_RING

CONST = {}
_c = 0
for _name, _w in [("ident", P), ("upto", P), ("ones", P), ("after", P), ("before", P), ("causal", P),
                  ("iota", P), ("freq", 24), ("iota16", 16)]:
    CONST[_name] = (_c, _w)
    _c += _w
N_CONST = _c
N_LEVELS = 7
N_SPAN = (N_LEVELS + 1) * P
POOL_LEVELS = 2
COLS = {}
_c = 0
for _name, _w in [("g_mix", 8), ("g_cross", 8), ("g_mem", 8), ("g_ffn", 8), ("g_ssd", 16), ("conv_w", 96),
                  ("conv_b", 24), ("c2", 16), ("b_ada", 48), ("g_mix2", 8), ("g_ffn2", 8), ("taps", 198),
                  ("fconv_b", 22), ("b_s", 4)]:
    COLS[_name] = (_c, _w)
    _c += _w
N_COLS = _c
ROWS = {}
_c = 0
for _name, _w in [("dt_bias", 32), ("a_log", 32), ("d_skip", 32)]:
    ROWS[_name] = (_c, _w)
    _c += _w
N_ROWS = _c
ROWS2 = {}
_c = 0
for _name, _w in [("hg", 512), ("sgu_g", 512), ("sgu_b", 512)]:
    ROWS2[_name] = (_c, _w)
    _c += _w
N_ROWS2 = _c


class Banks:

    def __init__(self):
        self.fills = [0] * 8
        self.at = {}
        self.next = 0

    def job(self, *name, bank=None):
        b = self.next if bank is None else bank
        self.next = (b + 1) % 8
        self.fills[b] += 1
        self.at[name] = (b, self.fills[b])

    def loop(self, name, turns, width, banks=None):
        for j in range(width):
            self.job(name, j, bank=None if banks is None else banks[j])
        for j in range(width):
            self.fills[self.at[(name, j)][0]] += turns - 1


def plan_banks():
    B = Banks()
    B.start = {}
    for t in range(TT):
        for h in range(2):
            B.job("xT", t, h)
    for b in range(4):
        for t in range(TT):
            B.job("tok", b, t)
    B.loop("xbc", 3, 8)
    for b in range(4):
        for t in range(TT):
            B.job("z", b, t)
    for t in range(TT):
        for h in range(2):
            B.job("qTr", t, h)
    B.job("kTr")
    B.job("iqTr")
    B.job("ikTr")
    for t in range(TT):
        for r in range(2):
            B.job("idx", t, r)
    B.loop("gate", 2, 8)
    for t in range(TT):
        for p in range(4):
            B.job("lg", t, p)
    for t in range(TT):
        for q in range(4):
            B.job("xsTr", t, q)
    B.job("BTr")
    B.job("acs")
    for t in range(TT):
        for n in range(2 * (t + 1)):
            B.job("PTr", t, n)
        for kv in range(KVH):
            B.job("oT", t, kv)
    B.job("cb", 0)
    B.job("cb", 1)
    groups = [(c, g) for c in range(TT) for g in range(SG)]
    for k in range(len(groups) + 1):
        if k < len(groups):
            B.job("row", *groups[k], 0)
            B.job("row", *groups[k], 1)
        if k >= 1:
            c, g = groups[k - 1]
            B.job("yd", c, g)
            B.job("st" if c == 0 else "yo", g)
    for t in range(TT):
        for h in range(2):
            B.job("mT", t, h)
    for n in range(8):
        B.job("mk", n)
    for t in range(TT):
        for q in range(4):
            B.job("yTr", t, q)
    for b in range(2):
        for t in range(TT):
            B.job("mv", b, t)
    for n in range(8):
        B.job("ma", n)
        B.job("ms", n)
    for b in range(2):
        for t in range(TT):
            B.job("wo", b, t)
    for t in range(TT):
        for h in range(2):
            B.job("a2T", t, h)
    for n in range(8):
        B.job("cq", n)
    for t in range(TT):
        for p in range(2):
            B.job("cl", t, p)
    for t in range(TT):
        for m in range(TT):
            B.job("cP", t, m)
    for h in range(MH):
        B.job("co", h)
    for b in range(2):
        for t in range(TT):
            B.job("cw", b, t)
    for t in range(TT):
        for h in range(2):
            B.job("a3T", t, h)
    B.loop("pq", 2, 8)
    for t in range(TT):
        for q in range(4):
            B.job("sk", t, q)
    for t in range(TT):
        for h in range(2):
            B.job("cT", t, h)
    free_banks = [(B.next + n) % 8 for n in range(4)]
    B.loop("ad0", 1, 8, banks=2 * free_banks)
    for b in range(3):
        for t in range(TT):
            B.job("cp", b, t)
    for t in range(TT):
        for h in range(2):
            B.job("y", t, h, bank=2 * t + h)
    B.loop("ad1", 1, 8, banks=(4, 5, 6, 7, 4, 5, 6, 7))
    for d in range(2):
        for t in range(TT):
            B.job("ce", d, t, bank=4 + 2 * d + t)
    for d in range(2):
        B.job("cH", d, bank=4 + d)
    B.loop("ad2", 1, 8, banks=(6, 7, 4, 5, 6, 7, 4, 5))
    for t in range(TT):
        B.job("eTr", t, bank=6 + t)
    B.loop("w", T // 16, 4, banks=(4, 5, 6, 7))
    B.job("h0", bank=4)
    B.loop("h", 31, 4, banks=(5, 6, 7, 4))
    for u in range(3):
        B.job("he", u, bank=5 + u)
    B.next = 4
    for t in range(TT):
        for h in range(2):
            B.job("x2T", t, h)
    for b in P_ORDER:
        for t in range(TT):
            B.job("p", b, t)
    for t in range(TT):
        B.job("qT2", t)
    for t in range(TT):
        B.job("sg", t)
    for d in range(2):
        for t in range(TT):
            B.job("kT2", d, t)
    for d in range(2):
        B.job("as", d)
    B.job("tot")
    for d in range(2):
        B.job("adv", d)
    for t in range(TT):
        B.job("dg", t)
        for d in range(2):
            for h in range(HH):
                B.job("e", t, d, h, 0)
                B.job("e", t, d, h, 1)
            for lev in range(N_LEVELS):
                B.job("gr", t, d, lev)
        B.job("o", t)
    for r in range(4):
        B.job("gb", r)
    for t in range(TT):
        for h in range(2):
            B.job("ocT", t, h)
    for b in range(2):
        for t in range(TT):
            B.job("w2", b, t)
    for t in range(TT):
        for h in range(2):
            B.job("x3T", t, h)
    for t in range(TT):
        for h in range(2):
            B.job("f", t, h, bank=2 * t + h)
    B.job("g0", bank=4)
    B.job("a0", bank=6)
    B.loop("ga", (FC - 2) // 2, 4, banks=(5, 7, 4, 6))
    B.job("ge", bank=5)
    B.job("ae", bank=7)
    return B


ADA_ORDER = [(0, 0), (1, 0), (0, 1), (2, 0), (1, 1), (3, 0), (2, 1), (3, 1)]
ADA_JOB = {jk: n for n, jk in enumerate(ADA_ORDER)}


P_ORDER = [6, 0, 1, 2, 3, 4, 5]


def bc(ap, axis, n):
    ap = ap.unsqueeze(axis)
    shape = list(ap.shape)
    shape[axis] = n
    return ap.to_broadcast(shape)


class Count:

    def __init__(self, sem):
        self.sem, self.n = sem, 0

    def by(self, ins, n=1):
        ins.then_inc(self.sem, n)
        self.n += n
        return self.n


class Chain:

    def __init__(self, eng, sem):
        self.eng, self.c = eng, Count(sem)

    def __call__(self, ins):
        self.eng.wait_ge(self.c.sem, self.c.by(ins))


def build(nc, A):
    B = plan_banks()
    with ExitStack() as ctx:
        where = {}

        def sb(name, shape, dt=F32):
            tensor = ctx.enter_context(nc.sbuf_tensor(name, shape, dt))
            where[name] = nc.sbuf_base - 4 * int(np.prod(shape[1:]))
            return tensor

        def over(name, below, offset, shape):
            return nc.alloc_sbuf_tensor_at(name, shape, F32R, offset=where[below] + 4 * offset)

        def sem(name):
            return ctx.enter_context(nc.semaphore(name))

        ps = ctx.enter_context(nc.psum_tensor("banks", [P, 8, 512], F32))
        bank_full = [sem(f"bank_full{b}") for b in range(8)]
        bank_free = [sem(f"bank_free{b}") for b in range(8)]

        ring = sb("weight_ring", [P, RING, 1024])
        w_hi = sb("weight_high", [P, 2, 1024], F32R)
        w_lo = sb("weight_rest", [P, 2, 1024], F32R)
        arena = sb("arena", [P, 32768])
        scratch = sb("scratch", [P, 2048])
        hres = sb("residual", [P, TT, D])
        actT = sb("act_feature_major", [P, KC, T])
        const = sb("const", [P, N_CONST])
        cols = sb("cols", [P, N_COLS])
        rows = sb("rows", [P, N_ROWS])
        stat = sb("stat", [P, 4, 10, TT])
        slots = sb("expert_slots", [P, 4, T])
        x1_hi = over("x1_high", "arena", 30208, [P, KC, T])
        x1_lo = over("x1_rest", "act_feature_major", 0, [P, KC, T])
        m_hi = over("memory_high", "arena", 8192, [P, KC, T])
        m_lo = over("memory_rest", "arena", 0, [P, KC, T])
        at_hi = over("attention_high", "arena", 10240, [P, KC, T])
        at_lo = over("attention_rest", "arena", 30208, [P, KC, T])
        y_hi = over("ssd_high", "arena", 22528, [P, 16, T])
        y_lo = over("ssd_rest", "arena", 4096, [P, 16, T])
        mg_hi = over("merged_high", "arena", 12288, [P, KC, T])
        mg_lo = over("merged_rest", "arena", 26624, [P, KC, T])
        a2_hi = over("a2_high", "arena", 4096, [P, KC, T])
        a2_lo = over("a2_rest", "act_feature_major", 0, [P, KC, T])
        co_hi = over("cross_high", "arena", 12288, [P, KC, T])
        co_lo = over("cross_rest", "arena", 10240, [P, KC, T])
        pq_hi = over("peer_query_high", "arena", 22528, [P, KC, T])
        pq_lo = over("peer_query_rest", "arena", 24576, [P, KC, T])
        x2_hi = over("x2_high", "arena", 20480, [P, KC, T])
        x2_lo = over("x2_rest", "act_feature_major", 0, [P, KC, T])
        a3_hi = over("a3_high", "residual", 0, [P, KC, T])
        a3_lo = over("a3_rest", "act_feature_major", 0, [P, KC, T])
        gated_hi = over("gated_high", "scratch", 512, [P, 2, T])
        gated_lo = over("gated_rest", "scratch", 1024, [P, 2, T])
        x3_hi = over("x3_high", "arena", 22528, [P, KC, T])
        x3_lo = over("x3_rest", "act_feature_major", 0, [P, KC, T])
        hidden_hi = over("hidden_high", "arena", 26624, [P, 2, T])
        hidden_lo = over("hidden_rest", "arena", 27136, [P, 2, T])
        h0 = sb("state_from_context", [P, 2, HH, P])
        mods = sb("modulation", [P, 48, 2])
        modsb = sb("modulation_sums", [P, 64])
        small = sb("small", [P, 1024])
        column_onehots = sb("column_onehots", [P, 2, 4, P])

        ring_loaded = [sem(f"ring_loaded{s}") for s in range(RING)]
        ffn_loaded = [sem(f"ffn_loaded{s}") for s in range(FRING)]
        tiles_begun = sem("tiles_begun")
        in_x = sem("x_loaded")
        in_mem = sem("mem_loaded")
        in_const = sem("const_loaded")
        in_ctx = sem("ctx_loaded")
        in_keys = sem("subkeys_loaded")
        in_gain = sem("first_gain_loaded")
        in_second = sem("second_consts_loaded")
        out_done = sem("out_stored")
        names = """norm_sq norm_ms norm_root xn_ready act_ready rope_ready xbc_ready attn_masked attn_exp
            attn_prob dt_abs dt_l adt_ready acs_ready acs_exp seg_exp m_ready adtb_ready xdtd_ready
            second_chunk y_ready mem_v merged_ready cl_ready cprob gate_sc gate_exp idx_ready onehot_ready
            p_ready silu_c ctx_abs ctx_l ctx_nk ctx_f ctx_k ctx_kd rope_arg rope_sin g_abs g_l g_nk g_logf
            g_k g_kd g_H z_made z_pool rows_made dve_columns o_ms o_root v_ms v_root rows_used v_ready
            oc_ready gdiag x3_ready ffn_conv ffn_gelu x4_ready out_ready act_step dve_step zeros_ready
            neg_a m_hi_ready m_lo_ready at_hi_ready at_lo_ready y_hi_ready y_lo_ready mg_hi_ready
            mg_lo_ready a2_hi_ready a2_lo_ready co_hi_ready pq_hi_ready pq_lo_ready y_seeded a3_hi_ready
            a3_lo_ready x3_hi_ready x3_lo_ready hi_ready hi_used lo_ready ffn_lo_ready ffn_down_lo_ready
            x1_hi_ready x1_lo_ready x2_hi_ready x2_lo_ready rest_ready column_ready square_made
            slots_negated gated_made hidden_ready hidden_made""".split()
        S = {n: sem(n) for n in names}

        def C(name):
            o, w = CONST[name]
            return const[:, o:o + w]

        def col(name):
            o, w = COLS[name]
            return cols[:, o:o + w]

        def row(name):
            o, w = ROWS[name]
            return rows[:, o:o + w]

        def area(off, *dims):
            n = int(np.prod(dims))
            assert off + n <= 32768, (off, dims)
            v = arena[:, off:off + n]
            if len(dims) == 1:
                return v
            names_ = "abcd"[:len(dims)]
            return v.rearrange(f"p ({' '.join(names_)}) -> p {' '.join(names_)}",
                               **{k: d for k, d in zip(names_[1:], dims[1:])})

        def raw(e):
            if e < F0:
                g = e if e < FRONT else EXP0 + e - X0
                return ring[:, g % RING, :], ring_loaded[g % RING], 16 * (g // RING + 1), 32
            r = e - F0
            return FR[:, r % FRING, :], ffn_loaded[r % FRING], 16 * (r // FRING + 1), 16

        def rest_count(e):
            if e < FRONT:
                return S["rest_ready"], e + 1
            if e < I0:
                return S["lo_ready"], e - X0 + 1
            return S["rest_ready"], FRONT + e - I0 + 1

        def bank(name):
            return ps[:, B.at[name][0], :]

        def claim(name, turn=None):
            b, n = B.at[name]
            if turn is not None:
                nc.tensor.wait_ge(bank_free[b], turn + (n - 1))
            elif n > 1:
                nc.tensor.wait_ge(bank_free[b], n - 1)
            return ps[:, b, :]

        def filled(ins, name):
            ins.then_inc(bank_full[B.at[name][0]], 1)

        def arrived(eng, name, turn=None):
            b, n = B.at[name]
            eng.wait_ge(bank_full[b], n if turn is None else turn + n)
            return ps[:, b, :]

        def freed(eng, name, turn=None):
            b, n = B.at[name]
            eng.wait_ge(bank_free[b], n if turn is None else turn + n)

        def free(ins, name):
            ins.then_inc(bank_free[B.at[name][0]], 1)

        TOK = area(0, TT, 2048)
        XBC = area(4096, 24, T)
        ZT = area(10240, TT, 2048)
        GT = area(14336, 16, T)
        QT = area(18432, 8, T)
        KT = area(20480, 2, T)
        IQT = area(20992, 2, T)
        IKT = area(21504, T)
        IKD = area(21760, TT, P)
        RELU = area(22016, 4, 2, T)
        SC = area(24064, 4, T)
        LG = [area(25088, 8, P), area(26112, 8, T)]
        PT = area(28160, 2, 8, P)
        AT = area(30208, 8, T)
        ROPE = area(32256, 2, TT, 24)
        ROPET = area(22016, 5, 96)
        RT = area(22656, 2, TT * 160)
        XS = area(18432, TT, 2048)
        YT_ = area(22528, TT, 2048)
        BTOK = area(0, SG, P)
        EM = area(26624, 2, 8, P)
        ADTB = scratch[:, :].rearrange("p (b h l) -> p b h l", b=2, h=8)
        CBM = area(28672, TT, SG, P)
        XDTD = area(4096, 2048)
        STATE = area(6144, SG, 512)
        YT = area(4096, 16, T)
        MT = area(0, KC, T)
        MEMX = area(2048, TT, D)
        MKT = area(18432, KC, T)
        MV = area(20480, TT, D)
        MG = area(26624, KC, T)
        CQT = area(8192, KC, T)
        CL = area(0, 4, T)
        CPT = area(2048, 2, 4, T)
        COT = area(10240, KC, T)
        QPT = area(0, 16, T)
        SK = area(4096, TT, 16, P)
        SK2 = area(8192, 16, P)
        CAND = area(10240, PH, 256)
        CAND2 = area(12288, PH, 256)
        ADA = small[0:2, :].rearrange("p (b n) -> p b n", b=2)
        OH = area(14336, 2048)
        TOPV = area(16384, 16, PTOP)
        TOPI = area(16640, 16, PTOP)
        TOPIF = area(16896, 16, PTOP)
        SCV = area(17152, PH, PTOP)
        SCI = area(17280, PH, PTOP)
        CIA = area(17408, 2, P)
        CIAF = area(17664, 2, P)
        EAB = area(31744, TT, 3, P)
        SMX = area(18304, 8)
        KEYS = area(18432, 16, P)
        CX = area(20480, TT, D)
        CXT = area(22528, KC, T)
        CPJ = area(24576, TT, 1536)
        CLF = area(27648, TT, 1024)
        CKK = area(29696, TT, 1024)
        WT = area(0, P, T)
        FR = area(0, FRING, 1024)
        PJ = area(6144, TT, 3584)
        LF = area(13312, TT, 1024)
        K2 = area(15360, TT, 1024)
        K2T = area(17408, 2, HH, T)
        Q2T = area(19456, HH, T)
        ZQ = area(20480, HH, 8, P)
        ZK = area(24576, HH, 7, P)
        SM = area(28160, HH, P)
        ZP = area(28672, 2, HH, P)
        HS = area(29696, 2, HH, P)
        LEV = area(30720, 15, P)
        GSPAN = scratch[:, :].rearrange("p (d n) -> p d n", d=2)
        SQO = area(20480, TT, 512)
        SQV = area(22528, TT, 512)
        T512 = area(22528, 4, 512)
        GB = area(24576, 2, D)
        GBD = area(22528, 2, KC, P)
        FIN1 = small[:, 0:D]
        R2 = area(4096, N_ROWS2)
        FIN2 = area(30720, D)
        CV = area(17408, 2, T)
        GC = area(18432, 2, T)
        GE = area(19456, 2, T)
        HF = area(20480, T)
        WSP = small[:, 0:512].rearrange("p (h n) -> p h n", h=HH)

        smx = sb("softmax_stats", [P, TT, 4, 8])
        warmed = sb("warmed", [P, 16])
        c2s = sb("silu_of_conditions", [P, KC, 2])
        gst = sb("mixer_stats", [P, 4, 2, TT, HH])
        lo = lambda a, b: small[:, a:b]
        DT = lo(0, 64).rearrange("p (c h) -> p c h", c=TT)
        DTS = lo(64, 128).rearrange("p (c h) -> p c h", c=TT)
        DTL = lo(128, 192).rearrange("p (c h) -> p c h", c=TT)
        ADT = lo(256, 320).rearrange("p (c h) -> p c h", c=TT)
        ACS = lo(320, 448).rearrange("p (c h) -> p c h", c=4)
        EAC = lo(448, 512).rearrange("p (c h) -> p c h", c=TT)
        DTE = lo(544, 576)
        NEGA = lo(576, 608)
        IW = lo(608, 616).rearrange("p (c h) -> p c h", c=TT)
        ident = C("ident")
        XN = scratch[:, :].rearrange("p (t d) -> p t d", t=TT)
        ROWHOT = scratch[:, :].rearrange("p (u v n) -> p u v n", u=4, v=4)
        COLUMN = [column_onehots[:, 0], column_onehots[:, 1]] + [small[:, 512 * k:512 * k + 512].rearrange(
            "p (v n) -> p v n", v=4) for k in range(2)]
        GELU = scratch[:, 0:512].rearrange("p (b t) -> p b t", b=2)
        GATED = scratch[:, 1536:1792]
        CEX = CX
        KD = area(20480, 2, 512)
        KS = area(15360, HH, T)
        TOTE = modsb[:, 32:40]
        ZEROS = area(29696, 512)
        by_head = lambda ap: ap.rearrange("p (h d) -> p h d", d=SP_)
        tsl = lambda t: slice(t * P, (t + 1) * P)
        hsl = lambda h: slice(h * P, (h + 1) * P)
        block = ctx.enter_context(nc.Block())

        @block.sync
        def _(sp):
            stream = A["stream"]
            for t in range(TT):
                sp.dma_start(hres[:, t, :], A["x"][0, t * P:(t + 1) * P, :]).then_inc(in_x, 16)
            sp.dma_start(const[:, :], A["const"]).then_inc(in_const, 16)
            sp.dma_start(cols[:, :], A["cols"]).then_inc(in_const, 16)
            sp.dma_start(rows[:, :], A["rows"].partition_broadcast(P)).then_inc(in_const, 16)
            sp.dma_start(small[:, 616:618].bitcast(I32), A["pos"]).then_inc(in_const, 16)
            def fetch(g, s):
                sp.dma_start(ring[:, s, :], stream[g]).then_inc(ring_loaded[s], 16)

            for s in range(RING):
                fetch(s, s)
            with sp.Fori(1, FRONT // RING) as i:
                for s in range(RING):
                    sp.wait_ge(S["rest_ready"], i * RING + (s - RING + 1))
                    fetch(i * RING + s, s)
            for s in range(RING):
                sp.wait_ge(S["rest_ready"], FRONT + s - RING + 1)
                fetch(FRONT + s, s)
            with sp.Fori(1, (EXP0 - FRONT) // RING) as i:
                for s in range(RING):
                    sp.wait_ge(tiles_begun, i * RING + (s - RING + 2))
                    fetch(i * RING + (FRONT + s), s)
            for s in range(RING):
                if s < RING - 1:
                    sp.wait_ge(tiles_begun, EXP0 - FRONT + s - RING + 2)
                else:
                    freed(sp, ("ad2", ADA_JOB[3, 1]))
                fetch(EXP0 + s, s)
            with sp.Fori(1, EXPERTS // RING) as i:
                for s in range(RING):
                    sp.wait_ge(S["lo_ready"], i * RING + (s - RING + 1))
                    fetch(i * RING + (EXP0 + s), s)
            for s in range(RING):
                sp.wait_ge(S["lo_ready"], EXPERTS + s - RING + 1)
                fetch(AFTER + s, s)
            with sp.Fori(1, N_IN2 // RING) as i:
                for s in range(RING):
                    sp.wait_ge(S["rest_ready"], i * RING + (FRONT + s - RING + 1))
                    fetch(i * RING + (AFTER + s), s)
            for s in range(RING):
                sp.wait_ge(S["rest_ready"], FRONT + N_IN2 + s - RING + 1)
                fetch(FIRST["out2"] + s, s)
            for s in range(RING):
                if s < RING - 1:
                    sp.wait_ge(tiles_begun, EXP0 - FRONT + s + 2)
                else:
                    arrived(sp, ("w2", 0, TT - 1))
                fetch(FIRST["out2"] + RING + s, s)
            sp.wait_ge(S["rows_used"], 1)
            for s in range(FRING):
                sp.dma_start(FR[:, s, :], stream[FFN0 + s]).then_inc(ffn_loaded[s], 16)
            with sp.Fori(1, N_FFN // FRING) as i:
                for s in range(FRING):
                    sp.wait_ge(S["hi_used"], i * FRING + (F0 + s - FRING + 2))
                    sp.dma_start(FR[:, s, :], stream[i * FRING + (FFN0 + s)]).then_inc(ffn_loaded[s], 16)
            for t in range(TT):
                sp.wait_ge(S["out_ready"], t + 1)
                sp.dma_start(A["out"][0, t * P:(t + 1) * P, :], XN[:, t, :]).then_inc(out_done, 16)
            sp.wait_ge(out_done, 16 * TT)

        @block.gpsimd
        def _(pool):
            def split_rest(e, turn=None, n=8):
                i_ = 0 if turn is None else turn
                pool.wait_ge(S["hi_ready"], i_ * n + (e + 1))
                if e > 1:
                    pool.wait_ge(S["hi_used"], i_ * n + e)
                nc.gpsimd.tensor_tensor(w_lo[:, e % 2, :], raw(e)[0], w_hi[:, e % 2, :],
                                        ALU.subtract).then_inc(S["rest_ready"], 1)

            for e in range(8):
                split_rest(e)
            with pool.Fori(0, FIRST["mem_k"] // 8 - 1) as i:
                for e in range(8):
                    split_rest(e + 8, i)
            split_rest(FIRST["mem_k"])
            def adt_rows(k):
                c, g = k // SG, k % SG
                if k > 1:
                    arrived(pool, ("row", (k - 2) // SG, (k - 2) % SG, 1))
                nc.gpsimd.tensor_copy(ADTB[:, k % 2], bc(ADT[:, c, 8 * g:8 * g + 8], 2, P)).then_inc(S["adtb_ready"], 1)

            pool.wait_ge(S["adt_ready"], 1)
            for k in range(2):
                adt_rows(k)
            arrived(pool, ("oT", 1, 1))
            for t in range(TT):
                pool.dma_start(MEMX[:, t, :], A["mem"][0, t * P:(t + 1) * P, :]).then_inc(in_mem, 16)
            for q in range(4):
                freed(pool, ("xsTr", 1, q))
            freed(pool, ("PTr", 1, 3))
            nc.gpsimd.tensor_tensor(by_head(YT_[:, 1, :]), by_head(XS[:, 1, :]), bc(row("d_skip"), 2, SP_),
                                    ALU.mult).then_inc(S["second_chunk"], 1)
            adt_rows(2)
            nc.gpsimd.tensor_tensor(by_head(XS[:, 1, :]), by_head(XS[:, 1, :]), bc(DT[:, 1, :], 2, SP_),
                                    ALU.mult).then_inc(S["second_chunk"], 1)
            for k in range(3, TT * SG):
                adt_rows(k)
            with pool.Fori(0, (FIRST["cross_out"] - FIRST["mem_k"]) // 8) as i:
                for e in range(8):
                    split_rest(FIRST["mem_k"] + 1 + e, i)
            arrived(pool, ("co", MH - 1))
            pool.dma_start(KEYS, A["keys"]).then_inc(in_keys, 16)
            for t in range(TT):
                pool.dma_start(CX[:, t, :], A["ctx"][0, t * P:(t + 1) * P, :]).then_inc(in_ctx, 16)
            for e in range(FIRST["cross_out"] + 1, FIRST["ada0"]):
                split_rest(e)
            pool.wait_ge(S["a3_hi_ready"], 1)
            nc.gpsimd.tensor_tensor(a3_lo[:, :, :], actT[:, :, :], a3_hi[:, :, :],
                                    ALU.subtract).then_inc(S["a3_lo_ready"], 1)
            for t in range(TT):
                freed(pool, ("eTr", t))
            with pool.Fori(0, T // 16) as i:
                for u in range(4):
                    pool.wait_ge(S["rows_made"], i * 4 + (u + 1))
                    pool.wait_ge(S["rows_made"], 1)
                    nc.gpsimd.tensor_tensor(ROWHOT[:, u], ROWHOT[:, u],
                                            bc(slots[:, 2, bass.ds(i * 16 + 4 * u, 4)], 2, P),
                                            ALU.mult).then_inc(S["onehot_ready"], 1)
            for u in range(4):
                freed(pool, ("w", u), T // 16 - 1)
            pool.dma_start(FIN1, A["fin1"].partition_broadcast(P)).then_inc(in_gain, 16)
            pool.wait_ge(S["p_ready"], P)
            pool.dma_start(R2, A["rows2"].partition_broadcast(P)).then_inc(in_second, 16)
            pool.dma_start(LEV[:, 0:14, :], A["levels"]).then_inc(in_second, 16)
            arrived(pool, ("x2T", 1, 1))
            pool.dma_start(WSP, A["wsp"]).then_inc(in_second, 16)
            pool.dma_start(GSPAN, A["span"]).then_inc(in_second, 16)
            with pool.Fori(0, N_IN2 // RING) as i:
                for s in range(RING):
                    split_rest(I0 + s, i, RING)
            pool.wait_ge(S["g_H"], 1)
            for t in range(TT):
                for d in range(2):
                    for h in range(HH):
                        freed(pool, ("e", t, d, h, 0))
                        z = ZQ[:, h, 0:POOL_LEVELS, :]
                        nc.gpsimd.tensor_tensor(ZK[:, h, 0:POOL_LEVELS, :], z,
                                                bc(K2T[:, d, h, tsl(t)], 1, POOL_LEVELS), ALU.mult)
                        ins = nc.gpsimd.tensor_tensor(z, z, bc(Q2T[:, h, tsl(t)], 1, POOL_LEVELS), ALU.mult)
                    ins.then_inc(S["z_pool"], 1)
            freed(pool, ("gr", 1, 1, N_LEVELS - 1))
            pool.dma_start(FIN2, A["fin2"].partition_broadcast(P)).then_inc(in_second, 16)

            def split_down(r, turn=None):
                e = F0 + r
                n = 0 if turn is None else turn * 6
                pool.wait_ge(S["hi_ready"], n + (e + 1))
                pool.wait_ge(S["hi_used"], n + e)
                nc.gpsimd.tensor_tensor(w_lo[:, e % 2, :], raw(e)[0], w_hi[:, e % 2, :],
                                        ALU.subtract).then_inc(S["ffn_down_lo_ready"], 1)

            def hidden_rest(value_job, c, par, turn=None):
                pool.wait_ge(S["hidden_made"], c + 1)
                freed(pool, value_job, turn)
                nc.gpsimd.tensor_tensor(hidden_lo[:, par, :], HF, hidden_hi[:, par, :],
                                        ALU.subtract).then_inc(S["hidden_ready"], 1)

            hidden_rest(("a0",), 0, 0)
            with pool.Fori(0, (FC - 2) // 2) as i:
                for u in range(2):
                    split_down(4 + 3 * u, i)
                    hidden_rest(("ga", 2 * u + 1), i * 2 + (u + 1), (u + 1) % 2, i)
            split_down(64)
            hidden_rest(("ae",), FC - 1, 1)
            split_down(65)

        @block.tensor
        def _(pe):
            begun = [False]

            def mm(out, lhsT, rhs, start=True, stop=True):
                ins = nc.tensor.matmul(out, lhsT, rhs, start=start, stop=stop, skip_group_check=True)
                if begun[0]:
                    ins.then_inc(tiles_begun, 1)
                    begun[0] = False
                return ins

            def weights(g, turn=None, per=8):
                s, n = g % RING, g // RING
                pe.wait_ge(ring_loaded[s], 16 * (n + 1) if turn is None else turn * (16 * per // RING) + 16 * (n + 1))
                begun[0] = True
                return ring[:, s, :]

            def transposes(job, pairs):
                b = claim(job)
                for k, src in enumerate(pairs):
                    ins = nc.tensor.transpose(b[:, k * P:(k + 1) * P], src, ident)
                filled(ins, job)

            def token_block(sec, b, name, lhs):
                banks = [claim((name, b, t)) for t in range(TT)]
                for j in range(4):
                    w = weights(FIRST[sec] + 4 * b + j)
                    for t in range(TT):
                        for k in range(2):
                            ins = mm(banks[t], lhs[:, 2 * j + k, tsl(t)], w[:, k * 512:(k + 1) * 512],
                                     start=(j == 0 and k == 0), stop=(j == 3 and k == 1))
                        if j == 3:
                            filled(ins, (name, b, t))

            def norm_transposes(name, src, n):
                for t in range(TT):
                    pe.wait_ge(S["xn_ready"], n * TT + t + 1)
                    for h in range(2):
                        transposes((name, t, h), [src[:, t, hsl(4 * h + k)] for k in range(4)])

            pe.wait_ge(in_const, 64)
            def split_tile(e, turn, n, high, rest, rest_ready, rest_count):
                more = 0 if turn is None else turn * n
                pe.wait_ge(S["hi_ready"], more + (e + 1))
                high(w_hi[:, e % 2, :]).then_inc(S["hi_used"], 1)
                pe.wait_ge(rest_ready, rest_count)
                return rest(w_lo[:, e % 2, :])

            def split_block(e, name, b, hi, lo_, turn=None):
                banks = [claim((name, b, t)) for t in range(TT)]
                for j in range(4):
                    def high(w):
                        for t in range(TT):
                            for k in range(2):
                                r = w[:, k * 512:(k + 1) * 512]
                                mm(banks[t], hi[:, 2 * j + k, tsl(t)], r, start=(j == k == 0), stop=False)
                                ins = mm(banks[t], lo_[:, 2 * j + k, tsl(t)], r, start=False, stop=False)
                        return ins

                    def rest(w):
                        for t in range(TT):
                            for k in range(2):
                                ins = mm(banks[t], hi[:, 2 * j + k, tsl(t)], w[:, k * 512:(k + 1) * 512],
                                         start=False, stop=(j == 3 and k == 1))
                            if j == 3:
                                filled(ins, (name, b, t))

                    split_tile(e + j, None, 0, high, rest, *rest_count(e + j))

            def split_channels(e, job, hi, lo_, turn, n, rest_ready, rest_count, part=0, parts=1):
                b = claim(job, turn) if part == 0 else bank(job)
                at = KC * part

                def high(w):
                    for k in range(KC):
                        mm(b[:, 0:T], w[:, hsl(k)], hi[:, at + k, :], start=(part == k == 0), stop=False)
                        ins = mm(b[:, 0:T], w[:, hsl(k)], lo_[:, at + k, :], start=False, stop=False)
                    return ins

                def rest(w):
                    for k in range(KC):
                        ins = mm(b[:, 0:T], w[:, hsl(k)], hi[:, at + k, :], start=False,
                                 stop=(part == parts - 1 and k == KC - 1))
                    return ins

                ins = split_tile(e, turn, n, high, rest, rest_ready, rest_count)
                if part == parts - 1:
                    filled(ins, job)

            def both_ready(name, count):
                pe.wait_ge(S[name + "_hi_ready"], count)
                pe.wait_ge(S[name + "_lo_ready"], count)

            norm_transposes("xT", XN, 0)
            pe.wait_ge(S["x1_hi_ready"], 4)
            pe.wait_ge(S["x1_lo_ready"], 4)
            for b in range(4):
                split_block(4 * b, "tok", b, x1_hi, x1_lo)
            with pe.Fori(0, 3) as i:
                for j in range(8):
                    e = FIRST["in_xbc"] + j
                    split_channels(e, ("xbc", j), x1_hi, x1_lo, i, 8, S["rest_ready"], i * 8 + (e + 1))
            for b in range(4):
                split_block(FIRST["in_z"] + 4 * b, "z", b, x1_hi, x1_lo)
            pe.wait_ge(S["rope_ready"], 1)
            for t in range(TT):
                for h in range(2):
                    transposes(("qTr", t, h), [TOK[:, t, hsl(4 * h + k)] for k in range(4)])
            transposes(("kTr",), [TOK[:, t, 1024 + kv * P:1024 + (kv + 1) * P] for kv in range(KVH) for t in range(TT)])
            transposes(("iqTr",), [TOK[:, t, 1280 + b * P:1280 + (b + 1) * P] for b in range(2) for t in range(TT)])
            transposes(("ikTr",), [IKD[:, t, :] for t in range(TT)])
            for name in (("qTr", 1, 1), ("kTr",), ("iqTr",), ("ikTr",)):
                freed(pe, name)
            for t in range(TT):
                for r in range(2):
                    b = claim(("idx", t, r))
                    rs = slice(r * IDH, (r + 1) * IDH)
                    for c in range(2):
                        ins = mm(b[:, c * T:(c + 1) * T], IQT[rs, c, tsl(t)], IKT[rs, :])
                    filled(ins, ("idx", t, r))
            with pe.Fori(0, 2) as i:
                for j in range(8):
                    e = FIRST["in_gate"] + j
                    split_channels(e, ("gate", j), x1_hi, x1_lo, i, 8, S["rest_ready"], i * 8 + (e + 1))
            for t in range(TT):
                w = P * (t + 1)
                for p in range(4):
                    b = claim(("lg", t, p))
                    for c in range(2):
                        h = 2 * p + c
                        ins = mm(b[:, c * T:c * T + w], QT[:, h, tsl(t)], KT[:, h // 4, 0:w])
                    filled(ins, ("lg", t, p))
            pe.wait_ge(S["xbc_ready"], 24)
            for t in range(TT):
                for q in range(4):
                    transposes(("xsTr", t, q), [XBC[:, 4 * q + k, tsl(t)] for k in range(4)])
            transposes(("BTr",), [XBC[:, 16 + g, 0:P] for g in range(SG)])
            pe.wait_ge(S["adt_ready"], 1)
            b = claim(("acs",))
            for c in range(TT):
                mm(b[:, c * 32:(c + 1) * 32], C("upto"), ADT[:, c, :])
            for c in range(TT):
                ins = mm(b[:, 64 + c * 32:64 + (c + 1) * 32], C("ones"), ADT[:, c, :])
            filled(ins, ("acs",))
            for t in range(TT):
                pe.wait_ge(S["attn_prob"], t + 1)
                blocks = [(s, h) for s in range(t + 1) for h in range(QH)]
                for n in range(2 * (t + 1)):
                    transposes(("PTr", t, n), [LG[t][:, h, tsl(s)] for s, h in blocks[4 * n:4 * n + 4]])
                for kv in range(KVH):
                    b = claim(("oT", t, kv))
                    for s in range(t + 1):
                        freed(pe, ("PTr", t, 2 * s + kv))
                        ins = mm(b, TOK[:, s, 1600 + kv * P:1600 + (kv + 1) * P],
                                 PT[:, s, 4 * kv:4 * kv + 4, :].rearrange("p h t -> p (h t)"),
                                 start=(s == 0), stop=(s == t))
                    filled(ins, ("oT", t, kv))
            for c in range(TT):
                b = claim(("cb", c))
                for g in range(SG):
                    ins = mm(b[:, hsl(g)], XBC[:, 16 + g, tsl(c)], XBC[:, 20 + g, tsl(c)])
                filled(ins, ("cb", c))
            groups = [(c, g) for c in range(TT) for g in range(SG)]
            for k in range(len(groups) + 1):
                if k < len(groups):
                    c, g = groups[k]
                    pe.wait_ge(S["adtb_ready"], k + 1)
                    for half in range(2):
                        b = claim(("row", c, g, half))
                        for j in range(4):
                            ins = mm(b[:, hsl(j)], ADTB[:, k % 2, 4 * half + j, :], C("upto"))
                        filled(ins, ("row", c, g, half))
                if k >= 1:
                    c, g = groups[k - 1]
                    if k == 1:
                        pe.wait_ge(S["xdtd_ready"], 1)
                        freed(pe, ("BTr",))
                    if k == SG + 1:
                        pe.wait_ge(S["second_chunk"], 2)
                    pe.wait_ge(S["m_ready"], k)
                    b = claim(("yd", c, g))
                    for j in range(8):
                        h = 8 * g + j
                        ins = mm(b[:, j * SP_:(j + 1) * SP_], EM[:, (k - 1) % 2, j, :],
                                 XS[:, c, h * SP_:(h + 1) * SP_])
                    filled(ins, ("yd", c, g))
                    if c == 0:
                        b = claim(("st", g))
                        filled(mm(b, BTOK[:, g, :], XDTD[:, g * 512:(g + 1) * 512]), ("st", g))
                    else:
                        freed(pe, ("st", g))
                        b = claim(("yo", g))
                        filled(mm(b, XBC[:, 20 + g, P:T], STATE[:, g, :]), ("yo", g))
            norm_transposes("mT", XN, 1)
            both_ready("m", 4)
            for n in range(8):
                e = FIRST["mem_k"] + n
                split_channels(e, ("mk", n), m_hi, m_lo, None, 0, *rest_count(e))
            for t in range(TT):
                pe.wait_ge(S["xn_ready"], 2 * TT + t + 1)
                for q in range(4):
                    transposes(("yTr", t, q), [YT_[:, t, hsl(4 * q + k)] for k in range(4)])
            for b in range(2):
                split_block(FIRST["mem_v"] + 4 * b, "mv", b, m_hi, m_lo)
            both_ready("at", 1)
            for n in range(8):
                e = FIRST["merge"] + 3 * n
                split_channels(e, ("ma", n), at_hi, at_lo, None, 0, *rest_count(e))
                if n == 0:
                    both_ready("y", 8)
                for part in range(2):
                    split_channels(e + 1 + part, ("ms", n), y_hi, y_lo, None, 0, *rest_count(e + 1 + part), part, 2)
            both_ready("mg", 8)
            for b in range(2):
                split_block(FIRST["w_out"] + 4 * b, "wo", b, mg_hi, mg_lo)
            norm_transposes("a2T", XN, 3)
            both_ready("a2", 4)
            for n in range(8):
                e = FIRST["cross_q"] + n
                split_channels(e, ("cq", n), a2_hi, a2_lo, None, 0, *rest_count(e))
            for n in range(8):
                freed(pe, ("mk", n))
                freed(pe, ("cq", n))
            for t in range(TT):
                for p in range(2):
                    b = claim(("cl", t, p))
                    for c in range(2):
                        h = 2 * p + c
                        for k in range(2):
                            ins = mm(b[:, c * T:(c + 1) * T], CQT[:, 2 * h + k, tsl(t)], MKT[:, 2 * h + k, :],
                                     start=(k == 0), stop=(k == 1))
                    filled(ins, ("cl", t, p))
            for t in range(TT):
                pe.wait_ge(S["cprob"], t + 1)
                for m in range(TT):
                    transposes(("cP", t, m), [CL[:, h, tsl(m)] for h in range(MH)])
            for b in range(2):
                for t in range(TT):
                    freed(pe, ("mv", b, t))
                    freed(pe, ("cP", b, t))
            for h in range(MH):
                b = claim(("co", h))
                for c in range(2):
                    for m in range(TT):
                        ins = mm(b[:, c * T:(c + 1) * T], MV[:, m, h * MD + c * P:h * MD + (c + 1) * P],
                                 CPT[:, m, h, :], start=(m == 0), stop=(m == 1))
                filled(ins, ("co", h))
            for h in range(MH):
                freed(pe, ("co", h))
            for b in range(2):
                split_block(FIRST["cross_out"] + 4 * b, "cw", b, co_hi, co_lo)
            norm_transposes("a3T", XN, 4)
            both_ready("pq", 4)
            with pe.Fori(0, 2) as i:
                for j in range(8):
                    e = FIRST["peer_q"] + j
                    split_channels(e, ("pq", j), pq_hi, pq_lo, i, 8, S["rest_ready"], i * 8 + (e + 1))
            for j in range(8):
                freed(pe, ("pq", j), 1)
            pe.wait_ge(in_keys, 16)
            for t in range(TT):
                for q in range(4):
                    b = claim(("sk", t, q))
                    for j in range(4):
                        ins = mm(b[:, hsl(j)], QPT[:, 4 * q + j, tsl(t)], KEYS[:, 4 * q + j, :])
                    filled(ins, ("sk", t, q))
            norm_transposes("cT", XN, 5)

            def modulation(name):
                def rows_(j):
                    b = claim((name, ADA_JOB[j, 0]))
                    for m in range(4):
                        w = weights(FIRST[name.replace("ad", "ada")] + 4 * j + m)
                        for k in range(2):
                            ins = mm(b[0:2, :], c2s[:, 2 * m + k, :], w[:, k * 512:(k + 1) * 512],
                                     start=(m == 0 and k == 0), stop=(m == 3 and k == 1))
                    filled(ins, (name, ADA_JOB[j, 0]))

                def turned(j):
                    freed(pe, (name, ADA_JOB[j, 0]))
                    b = claim((name, ADA_JOB[j, 1]))
                    for k in range(4):
                        ins = mm(b[:, 2 * k:2 * k + 2], ADA[:, j % 2, hsl(k)], ident[0:2, 0:2])
                    filled(ins, (name, ADA_JOB[j, 1]))

                rows_(0)
                for j in range(1, 4):
                    rows_(j)
                    turned(j - 1)
                turned(3)

            pe.wait_ge(S["silu_c"], 1)
            modulation("ad0")
            pe.wait_ge(S["act_ready"], 4)
            for b in range(3):
                token_block("ctx", b, "cp", CXT)
            for t in range(TT):
                for h in range(2):
                    b = claim(("y", t, h))
                    ins = mm(b, ident, hres[:, t, h * 512:(h + 1) * 512], start=True, stop=False)
            ins.then_inc(S["y_seeded"], 1)
            modulation("ad1")
            pe.wait_ge(S["ctx_f"], 1)
            for d in range(2):
                tri = C("after") if d == 0 else C("before")
                for t in range(TT):
                    b = claim(("ce", d, t))
                    far = (t == 0) if d == 0 else (t == 1)
                    ins = mm(b, tri, CLF[:, t, d * 512:(d + 1) * 512], start=True, stop=not far)
                    if far:
                        ins = mm(b, C("ones"), CLF[:, 1 - t, d * 512:(d + 1) * 512], start=False, stop=True)
                    filled(ins, ("ce", d, t))
            pe.wait_ge(S["ctx_kd"], 1)
            for d in range(2):
                b = claim(("cH", d))
                for h in range(HH):
                    for t in range(TT):
                        ins = mm(b[:, hsl(h)], CKK[:, t, d * 512 + h * P:d * 512 + (h + 1) * P],
                                 CPJ[:, t, 1024 + h * P:1024 + (h + 1) * P], start=(t == 0), stop=(t == 1))
                filled(ins, ("cH", d))
            modulation("ad2")
            for t in range(TT):
                pe.wait_ge(S["idx_ready"], t + 1)
                transposes(("eTr", t), [EAB[:, t, x, :] for x in range(3)])
            with pe.Fori(0, T // 16) as i:
                for u in range(4):
                    pe.wait_ge(S["onehot_ready"], i * 4 + (u + 1))
                    if u == 0:
                        pe.wait_ge(S["column_ready"], i + 1)
                    else:
                        pe.wait_ge(S["dve_columns"], i * 3 + u)
                    b = claim(("w", u), i)
                    for v in range(4):
                        ins = mm(b[:, hsl(v)], COLUMN[u][:, v, :], ROWHOT[:, u, v, :])
                    filled(ins, ("w", u))

            def split_sums(e, name, hi, lo_, turn, n, rest_ready, rest_count, last=False):
                def high(w):
                    for t in range(TT):
                        for h in range(2):
                            o = bank((name, t, h))
                            mm(o, hi[:, tsl(t)], w[:, h * 512:(h + 1) * 512], start=False, stop=False)
                            ins = mm(o, lo_[:, tsl(t)], w[:, h * 512:(h + 1) * 512], start=False, stop=False)
                    return ins

                def rest(w):
                    for t in range(TT):
                        for h in range(2):
                            ins = mm(bank((name, t, h)), hi[:, tsl(t)], w[:, h * 512:(h + 1) * 512],
                                     start=False, stop=last)
                            if last:
                                filled(ins, (name, t, h))

                split_tile(e, turn, n, high, rest, rest_ready, rest_count)

            def units(e, job, turn=None):
                split_channels(X0 + e, job, a3_hi, a3_lo, turn, 8, S["lo_ready"],
                               e + 1 if turn is None else turn * 8 + (e + 1))

            def values(e, a, par, turn=None, last=False):
                pe.wait_ge(S["p_ready"], a + 1)
                split_sums(X0 + e, "y", gated_hi[:, par, :], gated_lo[:, par, :], turn, 8, S["lo_ready"],
                           e + 1 if turn is None else turn * 8 + (e + 1), last)

            pe.wait_ge(S["a3_hi_ready"], 1)
            pe.wait_ge(S["a3_lo_ready"], 1)
            units(0, ("h0",))
            with pe.Fori(0, 31) as i:
                for u in range(4):
                    units(1 + 2 * u, ("h", u), i)
                    values(2 + 2 * u, i * 4 + u, u % 2, i)
            for u in range(3):
                a = 124 + u
                units(1 + 2 * a, ("he", u))
                values(2 + 2 * a, a, a % 2)
            values(255, 127, 1, last=True)
            norm_transposes("x2T", XN, 7)
            pe.wait_ge(S["x2_hi_ready"], 4)
            pe.wait_ge(S["x2_lo_ready"], 4)
            for n, b in enumerate(P_ORDER):
                split_block(I0 + 4 * n, "p", b, x2_hi, x2_lo)
            for t in range(TT):
                freed(pe, ("p", 3, t))
                transposes(("qT2", t), [PJ[:, t, 1536 + h * P:1536 + (h + 1) * P] for h in range(HH)])
            pe.wait_ge(S["v_ready"], 1)
            pe.wait_ge(in_second, 4 * 16)
            for t in range(TT):
                b = claim(("sg", t))
                for h in range(HH):
                    ins = mm(b[:, hsl(h)], WSP[:, h, :], PJ[:, t, 3072 + h * P:3072 + (h + 1) * P])
                filled(ins, ("sg", t))
            pe.wait_ge(S["g_k"], 1)
            for d in range(2):
                for t in range(TT):
                    transposes(("kT2", d, t), [K2[:, t, d * 512 + h * P:d * 512 + (h + 1) * P] for h in range(HH)])
            pe.wait_ge(S["g_logf"], 1)
            for d in range(2):
                b = claim(("as", d))
                filled(mm(b, C("after") if d == 0 else C("before"), LF[:, d, d * 512:(d + 1) * 512]), ("as", d))
            b = claim(("tot",))
            for d in range(2):
                for h in range(HH):
                    ins = mm(b[:, d * 4 + h:d * 4 + h + 1], LF[:, d, d * 512 + h * P:d * 512 + (h + 1) * P],
                             C("ones")[:, 0:1])
            filled(ins, ("tot",))
            for d in range(2):
                pe.wait_ge(S["g_kd"], d + 1)
                b = claim(("adv", d))
                for h in range(HH):
                    ins = mm(b[:, hsl(h)], KD[:, d, hsl(h)], PJ[:, d, 1024 + h * P:1024 + (h + 1) * P])
                filled(ins, ("adv", d))
            pe.wait_ge(in_second, 4 * 16)
            pe.wait_ge(S["g_H"], 1)
            for t in range(TT):
                freed(pe, ("qT2", t))
            for t in range(TT):
                b = claim(("dg", t))
                for h in range(HH):
                    ins = mm(b[:, hsl(h)], KS[:, h, tsl(t)], Q2T[:, h, tsl(t)])
                filled(ins, ("dg", t))
                for d in range(2):
                    for h in range(HH):
                        for half in range(2):
                            b = claim(("e", t, d, h, half))
                            filled(mm(b, LF[:, t, d * 512 + h * P:d * 512 + (h + 1) * P],
                                      GSPAN[:, d, half * 512:(half + 1) * 512]), ("e", t, d, h, half))
                    pe.wait_ge(S["z_made"], 2 * t + d + 1)
                    pe.wait_ge(S["z_pool"], 2 * t + d + 1)
                    for lev in range(N_LEVELS):
                        b = claim(("gr", t, d, lev))
                        for h in range(HH):
                            ins = mm(b[:, hsl(h)], ZK[:, h, lev, :], ZQ[:, h, lev, :])
                        filled(ins, ("gr", t, d, lev))
                freed(pe, ("gr", t, 1, N_LEVELS - 1))
                b = claim(("o", t))
                hf = h0[:, 0] if t == 0 else HS[:, 0]
                hb = h0[:, 1] if t == 1 else HS[:, 1]
                for h in range(HH):
                    mm(b[:, hsl(h)], SM[:, h, :], PJ[:, t, 1024 + h * P:1024 + (h + 1) * P], start=True, stop=False)
                    mm(b[:, hsl(h)], ZP[:, 0, h, :], hf[:, h, :], start=False, stop=False)
                    ins = mm(b[:, hsl(h)], ZP[:, 1, h, :], hb[:, h, :], start=False, stop=True)
                filled(ins, ("o", t))
            pe.wait_ge(S["gdiag"], 1)
            for r in range(4):
                b = claim(("gb", r))
                filled(mm(b, C("ones"), GBD[:, r // 2, 4 * (r % 2):4 * (r % 2) + 4, :].rearrange("p k n -> p (k n)")),
                       ("gb", r))
            for t in range(TT):
                pe.wait_ge(S["oc_ready"], t + 1)
                for h in range(2):
                    transposes(("ocT", t, h), [PJ[:, t, hsl(4 * h + k)] for k in range(4)])
            for t in range(TT):
                for h in range(2):
                    freed(pe, ("ocT", t, h))
            for b in range(2):
                token_block("out2", b, "w2", actT)
            norm_transposes("x3T", XN, 8)
            pe.wait_ge(S["act_ready"], 12)
            def channels(r, job, count, turn=None):
                split_channels(F0 + r, job, x3_hi, x3_lo, turn, 6, S["ffn_lo_ready"],
                               count if turn is None else turn * 4 + count)

            def down(r, c, par, turn=None, last=False):
                n = 0 if turn is None else turn * 2
                pe.wait_ge(S["hidden_ready"], n + (c + 1))
                split_sums(F0 + r, "f", hidden_hi[:, par, :], hidden_lo[:, par, :], turn, 6,
                           S["ffn_down_lo_ready"], n + (c + 1), last)

            pe.wait_ge(S["zeros_ready"], 1)
            for t in range(TT):
                for h in range(2):
                    mm(claim(("f", t, h)), ident, ZEROS, start=True, stop=False)
            pe.wait_ge(S["x3_hi_ready"], 1)
            pe.wait_ge(S["x3_lo_ready"], 1)
            channels(0, ("g0",), 1)
            channels(1, ("a0",), 2)
            with pe.Fori(0, (FC - 2) // 2) as i:
                for u in range(2):
                    channels(2 + 3 * u, ("ga", 2 * u), 3 + 2 * u, i)
                    channels(3 + 3 * u, ("ga", 2 * u + 1), 4 + 2 * u, i)
                    down(4 + 3 * u, u, u, i)
            channels(62, ("ge",), 43)
            channels(63, ("ae",), 44)
            down(64, FC - 2, 0)
            down(65, FC - 1, 1, last=True)

        @block.scalar
        def _(act):
            step = Chain(act, S["act_step"])

            def func(out, in_, f, **kw):
                return nc.scalar.activation(out, in_, f, **kw)

            def evacuate(job, out, turn=None, f=ACT.Copy, src=None, **kw):
                b = arrived(act, job, turn)
                free(func(out, b if src is None else src(b), f, **kw), job)

            warm_at = [0]

            def warm(f):
                n = warm_at[0]
                func(warmed[:, n:n + 1], C("ones")[:, 0:1], f)
                warm_at[0] += 1

            def norm(n, x, junk, ready=None):
                if n in (3, 4, 8, 9):
                    warm(ACT.Sqrt)
                for t in range(TT):
                    if ready is not None:
                        ready(t)
                    if n == 2 and t == 1:
                        act.wait_ge(S["norm_sq"], 2 * n + 1)
                    func(junk(t), x(t), ACT.Square, accum_out=stat[:, 0, n, t:t + 1]).then_inc(S["norm_sq"], 1)
                act.wait_ge(S["norm_ms"], n + 1)
                func(stat[:, 2, n, :], stat[:, 1, n, :], ACT.Sqrt).then_inc(S["norm_root"], 1)

            def halves(b):
                return b.rearrange("p (c t) -> p c t", c=2)

            def quarters(b):
                return b.rearrange("p (c t) -> p c t", c=4)

            def split_high(e, turn=None, n=8, rests=None):
                i_ = 0 if turn is None else turn
                src, loaded, count, per = raw(e)
                act.wait_ge(loaded, i_ * per + count)
                if e > 1:
                    act.wait_ge(S["hi_used"], i_ * n + (e - 1))
                    if rests is None:
                        rests = rest_count(e - 2)
                        if turn is not None:
                            rests = rests[0], turn * 8 + rests[1]
                    act.wait_ge(*rests)
                func(w_hi[:, e % 2, :], src, ACT.Copy).then_inc(S["hi_ready"], 1)

            norm(0, lambda t: hres[:, t, :], lambda t: XN[:, t, :], lambda t: act.wait_ge(in_x, 16 * TT))
            split_high(0)
            split_high(1)

            def high_quarter(n, hi, src, done, ready, per=2):
                t, h = n // per, n % per
                done(n)
                q = (slice(None), slice(4 * h, 4 * h + 4), tsl(t))
                func(hi[q], src[q], ACT.Copy).then_inc(S[ready], 1)

            def high_quarters(name, hi, done, ready, src=None):
                for n in range(4):
                    high_quarter(n, hi, actT if src is None else src, done, ready)

            def split_blocks(e, blocks, evacuation):
                for m in range(2, 4 * blocks):
                    split_high(e + m)
                    if m % 4 == 1:
                        evacuation(m // 4 - 1)

            high_quarters("xT", x1_hi, lambda n: freed(act, ("xT", n // 2, n % 2)), "x1_hi_ready")

            def evacuate_tok(b):
                for t in range(TT):
                    evacuate(("tok", b, t), TOK[:, t, b * 512:(b + 1) * 512])
                if b == 0:
                    act.wait_ge(S["rope_arg"], 1)
                    func(ROPE.rearrange("p a b c -> p (a b c)"), ROPET[:, 4, :], ACT.Sin).then_inc(S["rope_sin"], 1)

            split_blocks(0, 4, evacuate_tok)
            split_high(16)
            split_high(17)
            evacuate_tok(3)
            split_high(18)
            with act.Fori(0, 3) as i:
                for j in range(8):
                    split_high(FIRST["in_xbc"] + j + 3, i)
                    freed(act, ("xbc", j), i)
                    c = i * 8 + j
                    func(XBC[:, c, :], XBC[:, c, :], ACT.Silu).then_inc(S["xbc_ready"], 1)

            def evacuate_z(b):
                for t in range(TT):
                    evacuate(("z", b, t), ZT[:, t, b * 512:(b + 1) * 512], f=ACT.Silu)

            z0 = FIRST["in_z"]
            for e in range(z0 + 3, z0 + 18):
                split_high(e)
                if (e - z0) % 4 == 1:
                    evacuate_z((e - z0) // 4 - 1)
            for t in range(TT):
                for h in range(2):
                    evacuate(("qTr", t, h), QT[:, 4 * h:4 * h + 4, tsl(t)], src=quarters)
            evacuate(("kTr",), KT.rearrange("p k t -> p (k t)"))
            evacuate(("iqTr",), IQT.rearrange("p k t -> p (k t)"))
            evacuate(("ikTr",), IKT, src=lambda b: b[:, 0:T])
            act.wait_ge(S["dt_abs"], 1)
            func(NEGA, row("a_log"), ACT.Exp).then_inc(S["neg_a"], 1)
            step(func(DTS, DTS, ACT.Exp, scale=-1.0))
            func(DTL, DTS, ACT.Ln, bias=1.0).then_inc(S["dt_l"], 1)
            for t in range(TT):
                for r in range(2):
                    evacuate(("idx", t, r), RELU[:, 2 * t + r], f=ACT.Relu, scale=IDH ** -0.5, src=halves)
            with act.Fori(0, 2) as i:
                for j in range(8):
                    split_high(FIRST["in_gate"] + j + 2, i)
                    evacuate(("gate", j), GT[:, i * 8 + j, :], i, f=ACT.Sigmoid, src=lambda b: b[:, 0:T])
            warm(ACT.Exp)
            for t in range(TT):
                act.wait_ge(S["attn_masked"], t + 1)
                for h in range(QH):
                    ins = func(LG[t][:, h, :], LG[t][:, h, :], ACT.Exp, bias=smx[:, t, 1, h:h + 1],
                               scale=DH ** -0.5, accum_out=smx[:, t, 2, h:h + 1])
                ins.then_inc(S["attn_exp"], 1)
            for t in range(TT):
                for q in range(4):
                    evacuate(("xsTr", t, q), XS[:, t, q * 512:(q + 1) * 512])
            evacuate(("BTr",), BTOK.rearrange("p g n -> p (g n)"))
            act.wait_ge(S["acs_ready"], 1)
            step(func(EAC.rearrange("p c h -> p (c h)"), lo(320, 384), ACT.Exp))
            func(DTE, DTE, ACT.Exp).then_inc(S["acs_exp"], 1)
            for t in range(TT):
                for n in range(2 * (t + 1)):
                    s, h = n // 2, 4 * (n % 2)
                    if t == 1 and n == 0:
                        arrived(act, ("oT", 0, 1))
                    evacuate(("PTr", t, n), PT[:, s, h:h + 4, :], src=quarters)
                for kv in range(KVH):
                    evacuate(("oT", t, kv), AT[:, 4 * kv:4 * kv + 4, tsl(t)], src=quarters)
            for k in range(TT * SG):
                for half in range(2):
                    freed(act, ("row", k // SG, k % SG, half))
                func(EM[:, k % 2], EM[:, k % 2], ACT.Exp).then_inc(S["seg_exp"], 1)
                if 1 <= k <= SG:
                    evacuate(("st", k - 1), STATE[:, k - 1, :])
            norm(1, lambda t: MEMX[:, t, :], lambda t: XN[:, t, :], lambda t: act.wait_ge(in_mem, 16 * TT))
            high_quarters("mT", m_hi, lambda n: freed(act, ("mT", n // 2, n % 2)), "m_hi_ready", MT)
            norm(2, lambda t: YT_[:, t, :], lambda t: EM[:, :, :, :].rearrange("p u h l -> p (u h l)"),
                 lambda t: act.wait_ge(S["y_ready"], t + 1))
            for n in range(8):
                split_high(FIRST["mem_k"] + n + 2)
                evacuate(("mk", n), MKT[:, n, :], src=lambda b: b[:, 0:T])
            for m in range(2, 10):
                split_high(FIRST["mem_v"] + m)
                high_quarter(m - 2, y_hi, YT, lambda n: freed(act, ("yTr", n // 4, n % 4)), "y_hi_ready", 4)
                if m == 2:
                    func(at_hi[:, :, :], AT, ACT.Copy).then_inc(S["at_hi_ready"], 1)
                if m % 4 == 1:
                    for t in range(TT):
                        evacuate(("mv", m // 4 - 1, t), MV[:, t, (m // 4 - 1) * 512:(m // 4) * 512])

            def merged_high(n):
                act.wait_ge(S["merged_ready"], n + 1)
                func(mg_hi[:, n, :], MG[:, n, :], ACT.Copy).then_inc(S["mg_hi_ready"], 1)

            for m in range(2, 26):
                split_high(FIRST["merge"] + m)
                if m % 3 == 2 and m > 2:
                    merged_high(m // 3 - 1)
            merged_high(7)
            for m in range(2, 10):
                split_high(FIRST["w_out"] + m)
            norm(3, lambda t: hres[:, t, :], lambda t: XN[:, t, :], lambda t: [freed(act, ("wo", b, t)) for b in range(2)])
            high_quarters("a2T", a2_hi, lambda n: freed(act, ("a2T", n // 2, n % 2)), "a2_hi_ready")
            for n in range(8):
                split_high(FIRST["cross_q"] + n + 2)
                evacuate(("cq", n), CQT[:, n, :], src=lambda b: b[:, 0:T])
            warm(ACT.Exp)
            for t in range(TT):
                act.wait_ge(S["cl_ready"], t + 1)
                if t == 1:
                    arrived(act, ("cP", 0, 1))
                for p in range(2):
                    b = arrived(act, ("cl", t, p))
                    for c in range(2):
                        h = 2 * p + c
                        ins = func(CL[:, h, :], b[:, c * T:(c + 1) * T], ACT.Exp, bias=smx[:, t, 1, h:h + 1],
                                   scale=MD ** -0.5, accum_out=smx[:, t, 2, h:h + 1])
                    free(ins, ("cl", t, p))
                for m in range(TT):
                    evacuate(("cP", t, m), CPT[:, m, :, tsl(t)], src=quarters)
            for h in range(MH):
                b = halves(arrived(act, ("co", h)))
                func(COT[:, 2 * h:2 * h + 2, :], b, ACT.Copy)
                ins = func(co_hi[:, 2 * h:2 * h + 2, :], b, ACT.Copy)
                ins.then_inc(S["co_hi_ready"], 1)
            for m in range(2, 10):
                split_high(FIRST["cross_out"] + m)
            norm(4, lambda t: hres[:, t, :], lambda t: XN[:, t, :], lambda t: [freed(act, ("cw", b, t)) for b in range(2)])
            func(c2s[:, :, :].rearrange("p k c -> p (k c)"), col("c2"), ACT.Silu).then_inc(S["silu_c"], 1)
            high_quarters("a3T", pq_hi, lambda n: freed(act, ("a3T", n // 2, n % 2)), "pq_hi_ready")
            for n in range(16):
                if n < 14:
                    split_high(FIRST["peer_q"] + n + 2)
                evacuate(("pq", n % 8), QPT[:, n, :], n // 8, src=lambda b: b[:, 0:T])
            for t in range(TT):
                for q in range(4):
                    evacuate(("sk", t, q), SK[:, t, 4 * q:4 * q + 4, :], src=quarters)
            norm(5, lambda t: CX[:, t, :], lambda t: XN[:, t, :], lambda t: act.wait_ge(in_ctx, 16 * TT))

            def modulation(name):
                first = 16 * int(name[2])
                for n, (j, turned) in enumerate(ADA_ORDER):
                    if turned:
                        evacuate((name, n), mods[:, first + 4 * j:first + 4 * j + 4, :],
                                 src=lambda b: b[:, 0:8].rearrange("p (n c) -> p n c", c=2))
                    else:
                        evacuate((name, n), ADA[:, j % 2, :], src=lambda b: b[0:2, :])

            modulation("ad0")
            for b in range(3):
                for t in range(TT):
                    evacuate(("cp", b, t), CPJ[:, t, b * 512:(b + 1) * 512])
            act.wait_ge(S["ctx_abs"], 1)
            step(func(CLF, CLF, ACT.Exp, scale=-1.0))
            func(CLF, CLF, ACT.Ln, bias=1.0).then_inc(S["ctx_l"], 1)
            act.wait_ge(S["ctx_nk"], 1)
            func(CKK, CKK, ACT.Exp, scale=-1.0).then_inc(S["ctx_k"], 1)
            modulation("ad1")
            for d in range(2):
                for t in range(TT):
                    evacuate(("ce", d, t), CEX[:, t, d * 512:(d + 1) * 512], f=ACT.Exp)
            for d in range(2):
                evacuate(("cH", d), h0[:, d], src=quarters)
            for t in range(TT):
                if t == 1:
                    act.wait_ge(S["y_seeded"], 1)
                    func(a3_hi[:, :, :], actT[:, :, :], ACT.Copy).then_inc(S["a3_hi_ready"], 1)
                    modulation("ad2")
                act.wait_ge(S["gate_sc"], t + 1)
                func(EAB[:, t, 2, :], EAB[:, t, 2, :], ACT.Exp).then_inc(S["gate_exp"], 1)
            for t in range(TT):
                evacuate(("eTr", t), slots[:, 0:3, tsl(t)], src=lambda b: b[:, 0:384].rearrange("p (x n) -> p x n", x=3))
            act.wait_ge(S["slots_negated"], 1)

            def columns(turn):
                for v in range(4):
                    ins = func(COLUMN[0][:, v, :], C("iota"), ACT.Square,
                               bias=slots[:, 3, bass.ds(turn * 16 + v, 1)])
                ins.then_inc(S["square_made"], 1)
                act.wait_ge(S["square_made"], turn + 1)
                func(COLUMN[0], COLUMN[0], ACT.Relu, scale=-1.0, bias=1.0).then_inc(S["column_ready"], 1)

            def dense(turn, u):
                evacuate(("w", u), WT[:, :, bass.ds(turn * 16 + 4 * u, 4)].rearrange("p n v -> p v n"), turn,
                         src=quarters)

            columns(0)
            split_high(X0)
            split_high(X0 + 1)
            with act.Fori(0, T // 16 - 1) as i:
                dense(i, 0)
                columns(i + 1)
                for u in range(1, 4):
                    dense(i, u)
            for u in range(4):
                dense(T // 16 - 1, u)
            func(GELU[:, 0, :], arrived(act, ("h0",))[:, 0:T], ACT.Gelu).then_inc(bank_free[4], 1)
            split_high(X0 + 2)

            def expert_row(a, e, job, turn=None):
                b = arrived(act, job, turn)
                act.wait_ge(S["p_ready"], (0 if turn is None else turn * 4) + a)
                free(func(GELU[:, a % 2, :], b[:, 0:T], ACT.Gelu), job)
                split_high(X0 + e, turn)
                if e + 1 < EXPERTS:
                    split_high(X0 + e + 1, turn)

            with act.Fori(0, 31) as i:
                for u in range(4):
                    expert_row(u + 1, 2 * u + 3, ("h", u), i)
            for u in range(3):
                expert_row(125 + u, 2 * (124 + u) + 3, ("he", u))
            warm(ACT.Sqrt)
            for t in range(TT):
                for h in range(2):
                    evacuate(("y", t, h), hres[:, t, h * 512:(h + 1) * 512])
            for t in range(TT):
                freed(act, ("y", t, 1))
            norm(6, lambda t: hres[:, t, :], lambda t: XN[:, t, :], lambda t: act.wait_ge(S["p_ready"], P))
            norm(7, lambda t: hres[:, t, :], lambda t: XN[:, t, :], lambda t: act.wait_ge(S["xn_ready"], 6 * TT + t + 1))
            split_high(I0)
            split_high(I0 + 1)
            high_quarters("x2T", x2_hi, lambda n: act.wait_ge(S["act_ready"], 5 + n), "x2_hi_ready")

            def evacuate_p(b):
                for t in range(TT):
                    evacuate(("p", b, t), PJ[:, t, b * 512:(b + 1) * 512],
                             f=ACT.Copy if b < 3 else ACT.Silu if b < 5 else ACT.Gelu)

            def block_and_more(n):
                evacuate_p(P_ORDER[n])
                if n == 1:
                    act.wait_ge(S["v_ms"], 1)
                    func(gst[:, 2, 1], gst[:, 1, 1], ACT.Sqrt).then_inc(S["v_root"], 1)
                if n == 3:
                    act.wait_ge(S["g_abs"], 1)
                    step(func(LF, LF, ACT.Exp, scale=-1.0))
                    func(LF, LF, ACT.Ln, bias=1.0).then_inc(S["g_l"], 1)
                if n == 4:
                    act.wait_ge(S["g_nk"], 1)
                    func(K2, K2, ACT.Exp, scale=-1.0).then_inc(S["g_k"], 1)

            split_blocks(I0, 7, block_and_more)
            block_and_more(6)
            for t in range(TT):
                evacuate(("qT2", t), Q2T[:, :, tsl(t)], src=quarters, scale=P ** -0.5)
            for d in range(2):
                for t in range(TT):
                    evacuate(("kT2", d, t), K2T[:, d, :, tsl(t)], src=quarters)
            for d in range(2):
                evacuate(("as", d), KD[:, d, :], f=ACT.Exp)
            evacuate(("tot",), TOTE, f=ACT.Exp, src=lambda b: b[:, 0:8])
            act.wait_ge(S["g_H"], 1)
            for t in range(TT):
                for d in range(2):
                    if t or d:
                        arrived(act, ("gr", t, 0, 6) if d else ("gr", t - 1, 1, 6))
                    for h in range(HH):
                        for half in range(2):
                            evacuate(("e", t, d, h, half), ZQ[:, h, 4 * half:4 * half + 4, :], f=ACT.Exp, src=quarters)
            act.wait_ge(S["gdiag"], 1)
            for r in range(4):
                evacuate(("gb", r), GB[:, r // 2, 512 * (r % 2):512 * (r % 2) + 512])
            warm(ACT.Sqrt)
            act.wait_ge(S["o_ms"], 1)
            func(gst[:, 2, 0], gst[:, 1, 0], ACT.Sqrt).then_inc(S["o_root"], 1)
            for t in range(TT):
                for h in range(2):
                    evacuate(("ocT", t, h), actT[:, 4 * h:4 * h + 4, tsl(t)], src=quarters)
            norm(8, lambda t: hres[:, t, :], lambda t: XN[:, t, :], lambda t: act.wait_ge(S["x3_ready"], 4))

            for r in range(2):
                split_high(F0 + r)
            act.wait_ge(S["act_ready"], 12)
            func(x3_hi[:, :, :], actT[:, :, :], ACT.Copy).then_inc(S["x3_hi_ready"], 1)

            def ffn_gate(job, c, par, turn=None):
                b = arrived(act, job, turn)[:, 0:T]
                func(CV[:, par, :], b, ACT.Identity, scale=col("taps")[:, bass.ds(c * 9 + 4, 1)],
                     bias=col("fconv_b")[:, bass.ds(c, 1)])
                free(func(GC[:, par, :], b, ACT.Copy), job)

            def ffn_gelu(c, par):
                act.wait_ge(S["ffn_conv"], c + 1)
                func(GE[:, par, :], CV[:, par, :], ACT.Gelu).then_inc(S["ffn_gelu"], 1)

            ffn_gate(("g0",), 0, 0)
            split_high(F0 + 2, rests=(S["ffn_lo_ready"], 1))
            split_high(F0 + 3, rests=(S["ffn_lo_ready"], 2))
            with act.Fori(0, (FC - 2) // 2) as i:
                for u in range(2):
                    ffn_gelu(i * 2 + u, u)
                    ffn_gate(("ga", 2 * u), i * 2 + (u + 1), (u + 1) % 2, i)
                    split_high(F0 + 4 + 3 * u, i, 6, (S["ffn_lo_ready"], i * 4 + (3 + 2 * u)))
                    split_high(F0 + 5 + 3 * u, i, 6, (S["ffn_lo_ready"], i * 4 + (4 + 2 * u)))
                    split_high(F0 + 6 + 3 * u, i, 6, (S["ffn_down_lo_ready"], i * 2 + (u + 1)))
            ffn_gelu(FC - 2, 0)
            ffn_gate(("ge",), FC - 1, 1)
            split_high(F0 + 64, rests=(S["ffn_lo_ready"], 43))
            split_high(F0 + 65, rests=(S["ffn_lo_ready"], 44))
            ffn_gelu(FC - 1, 1)
            norm(9, lambda t: hres[:, t, :], lambda t: XN[:, t, :], lambda t: act.wait_ge(S["x4_ready"], 4))

        @block.vector
        def _(dve):
            V = nc.vector
            step = Chain(dve, S["dve_step"])
            ts, tt, stt, cp = V.tensor_scalar, V.tensor_tensor, V.scalar_tensor_tensor, V.tensor_copy

            def signal(ins, name, wait=None):
                ins.then_inc(S[name], 1)
                if wait is not None:
                    dve.wait_ge(S[name], wait)

            def scale_rows(n, width, x, out, gain=None):
                dve.wait_ge(S["norm_sq"], 2 * n + 2)
                signal(ts(stat[:, 1, n, :], stat[:, 0, n, :], 1.0 / width, EPS, ALU.mult, ALU.add), "norm_ms")
                dve.wait_ge(S["norm_root"], n + 1)
                step(V.reciprocal(stat[:, 3, n, :], stat[:, 2, n, :]))
                for t in range(TT):
                    if gain is None:
                        signal(ts(out(t), x(t), stat[:, 3, n, t:t + 1], None, ALU.mult), "xn_ready")
                    else:
                        signal(stt(out(t), x(t), stat[:, 3, n, t:t + 1], gain, ALU.mult, ALU.mult), "xn_ready")

            def features(name, out, gain, shift=None, chunks=2):
                for t in range(TT):
                    for h in range(chunks):
                        b = arrived(dve, (name, t, h)).rearrange("p (k n) -> p k n", k=4)
                        o = out[:, 4 * h:4 * h + 4, tsl(t)]
                        free(tt(o, b, bc(gain[:, 4 * h:4 * h + 4], 2, P), ALU.mult), (name, t, h))
                        if shift is not None:
                            freed(dve, (name, t, h))
                            signal(tt(o, o, bc(shift[:, 4 * h:4 * h + 4], 2, P), ALU.add), "act_ready")

            dve.wait_ge(in_const, 64)
            scale_rows(0, D, lambda t: hres[:, t, :], lambda t: XN[:, t, :])
            features("xT", actT, col("g_mix"))

            def rest_quarters(hi, lo_, hi_ready, ready, src=None, per=2):
                for n in range(2 * per):
                    t, h = n // per, n % per
                    dve.wait_ge(S[hi_ready], n + 1)
                    q = (slice(None), slice(4 * h, 4 * h + 4), tsl(t))
                    tt(lo_[q], (actT if src is None else src)[q], hi[q], ALU.subtract).then_inc(S[ready], 1)

            rest_quarters(x1_hi, x1_lo, "x1_hi_ready", "x1_lo_ready")
            F = ROPET[:, 0, 0:48].rearrange("p (t f) -> p t f", t=TT)
            posf = ROPET[:, 3, 0:2]
            step(cp(posf, small[:, 616:618].bitcast(I32)))
            step(tt(F, bc(posf, 2, 24), bc(C("freq"), 1, TT), ALU.mult))
            ang = ROPET[:, 0, 0:48]
            for s, (q, shift) in enumerate(((0.0, 0.0), (0.25, float(np.pi / 2)))):
                k = ROPET[:, 1 + s, 0:48]
                r = ROPET[:, 4, 48 * s:48 * s + 48]
                step(ts(k, ang, float(1 / (2 * np.pi)), q, ALU.mult, ALU.add))
                step(ts(k, k, 12582912.0, None, ALU.add))
                step(ts(k, k, -12582912.0, None, ALU.add))
                step(stt(r, k, -TWO_PI[0], ang, ALU.mult, ALU.add))
                step(stt(r, k, -TWO_PI[1], r, ALU.mult, ALU.add))
                step(stt(r, k, -TWO_PI[2], r, ALU.mult, ALU.add))
                step(ts(r, r, shift, float(np.float32(3.1415925)), ALU.add, ALU.min))
                ins = ts(r, r, float(np.float32(-3.1415925)), None, ALU.max)
                if s == 0:
                    step(ins)
            signal(ins, "rope_arg")
            with dve.Fori(0, 3) as i:
                for j in range(8):
                    b = arrived(dve, ("xbc", j), i)
                    o = XBC[:, i * 8 + j, :]
                    wcol = lambda k: col("conv_w")[:, bass.ds(i * 32 + 4 * j + k, 1)]
                    base = i * 24 + (step.c.n + 3 * j)
                    ts(o, b[:, 0:T], wcol(3), col("conv_b")[:, bass.ds(i * 8 + j, 1)], ALU.mult,
                       ALU.add).then_inc(step.c.sem, 1)
                    for m, k in enumerate((2, 1)):
                        dve.wait_ge(step.c.sem, base + (1 + m))
                        stt(o[:, 3 - k:T], b[:, 0:T - 3 + k], wcol(k), o[:, 3 - k:T], ALU.mult,
                            ALU.add).then_inc(step.c.sem, 1)
                    dve.wait_ge(step.c.sem, base + 3)
                    free(stt(o[:, 3:T], b[:, 0:T - 3], wcol(0), o[:, 3:T], ALU.mult, ALU.add), ("xbc", j))
            step.c.n += 72
            for b in range(4):
                for t in range(TT):
                    freed(dve, ("tok", b, t))
            dve.wait_ge(S["rope_sin"], 1)
            for t in range(TT):
                for a, b, hd, heads, f0 in ((0, 1280, DH, 10, 0), (1280, 1600, IDH, 5, 16)):
                    half = hd // 8
                    x = TOK[:, t, a:b].rearrange("p (h d) -> p h d", d=hd)
                    x1, x2 = x[:, :, 0:half], x[:, :, half:2 * half]
                    sin = bc(ROPE[:, 0, t, f0:f0 + half], 1, heads)
                    cos = bc(ROPE[:, 1, t, f0:f0 + half], 1, heads)
                    n = heads * half
                    m = [RT[:, k // 2, (k % 2) * 160:(k % 2) * 160 + n].rearrange("p (h d) -> p h d", d=half)
                         for k in range(4)]
                    tt(m[0], x1, cos, ALU.mult)
                    tt(m[1], x2, sin, ALU.mult)
                    tt(m[2], x2, cos, ALU.mult)
                    step(tt(m[3], x1, sin, ALU.mult))
                    step(tt(x1, m[0], m[1], ALU.subtract))
                    step(tt(x2, m[2], m[3], ALU.add))
                step(cp(IKD[:, t, :].rearrange("p (r d) -> p r d", r=2), bc(TOK[:, t, 1536:1600], 1, 2)))
            ins = ts(IW, TOK[:, :, 1856:1860], IH ** -0.5, None, ALU.mult)
            signal(ins, "rope_ready", 1)
            step(tt(DT, TOK[:, :, 1860:1892], bc(row("dt_bias"), 1, TT), ALU.add))
            signal(stt(DTS, DT, -1.0, DT, ALU.mult, ALU.max), "dt_abs")
            dve.wait_ge(S["dt_l"], 1)
            dve.wait_ge(S["neg_a"], 1)
            step(stt(DT, DT, 0.0, DTL, ALU.max, ALU.add))
            signal(stt(ADT, DT, -1.0, bc(NEGA, 1, TT), ALU.mult, ALU.mult), "adt_ready", 1)
            best = [smx[:, 0, 0, :], smx[:, 1, 0, :]]
            for t in range(TT):
                w = P * (t + 1)
                sc, left = SC[:, 2 * t, 0:w], SC[:, 2 * t + 1, 0:w]
                for r in range(2):
                    freed(dve, ("idx", t, r))
                step(ts(sc, RELU[:, 2 * t, 0, 0:w], IW[:, t, 0:1], None, ALU.mult))
                for h in range(1, IH):
                    step(stt(sc, RELU[:, 2 * t + h % 2, h // 2, 0:w], IW[:, t, h:h + 1], sc, ALU.mult, ALU.add))
                step(tt(sc[:, w - P:w], sc[:, w - P:w], C("causal"), ALU.add))
                for n in range(TOPK // 8):
                    src = sc if n == 0 else left
                    step(V.max(best[t], src))
                    step(V.match_replace(out=left, in_to_replace=best[t], in_values=src, imm_value=TAKEN))
                step(tt(left, left, sc, ALU.not_equal))
                step(stt(left, sc, -1.0e38, left, ALU.is_gt, ALU.mult))
                step(ts(left, left, -OFF, OFF, ALU.mult, ALU.add))
            for t in range(TT):
                w = P * (t + 1)
                for p in range(4):
                    b = arrived(dve, ("lg", t, p)).rearrange("p (c n) -> p c n", c=2)
                    free(tt(LG[t][:, 2 * p:2 * p + 2, :], b[:, :, 0:w], bc(SC[:, 2 * t + 1, 0:w], 1, 2), ALU.add),
                         ("lg", t, p))
                for p in range(4):
                    freed(dve, ("lg", t, p))
                step(V.tensor_reduce(smx[:, t, 0, :], LG[t], AX.X, ALU.max))
                signal(ts(smx[:, t, 1, :], smx[:, t, 0, :], -(DH ** -0.5), None, ALU.mult), "attn_masked")
            for t in range(TT):
                dve.wait_ge(S["attn_exp"], t + 1)
                step(V.reciprocal(smx[:, t, 3, :], smx[:, t, 2, :]))
                signal(tt(LG[t], LG[t], bc(smx[:, t, 3, :], 2, P * (t + 1)), ALU.mult), "attn_prob")
            b = arrived(dve, ("acs",))
            free(cp(ACS, b[:, 0:128].rearrange("p (c h) -> p c h", c=4)), ("acs",))
            freed(dve, ("acs",))
            signal(tt(DTE, ACS[:, 2, :], ACS[:, 0, :], ALU.subtract), "acs_ready")
            for t in range(TT):
                for q in range(4):
                    freed(dve, ("xsTr", t, q))
            tt(by_head(YT_[:, 0, :]), by_head(XS[:, 0, :]), bc(row("d_skip"), 2, SP_), ALU.mult)
            step(tt(by_head(XS[:, 0, :]), by_head(XS[:, 0, :]), bc(DT[:, 0, :], 2, SP_), ALU.mult))
            dve.wait_ge(S["acs_exp"], 1)
            signal(tt(by_head(XDTD), by_head(XS[:, 0, :]), bc(DTE, 2, SP_), ALU.mult), "xdtd_ready")
            for kv in range(KVH):
                arrived(dve, ("oT", 1, kv))
            for c in range(TT):
                b = arrived(dve, ("cb", c)).rearrange("p (g l) -> p g l", g=SG)
                free(tt(CBM[:, c], b, bc(C("upto"), 1, SG), ALU.mult), ("cb", c))
                freed(dve, ("cb", c))
            n_groups = TT * SG

            for k in range(n_groups + 1):
                if k < n_groups:
                    c, g = k // SG, k % SG
                    for half in range(2):
                        b = arrived(dve, ("row", c, g, half))
                        for j in range(4):
                            h = 8 * g + 4 * half + j
                            ins = ts(EM[:, k % 2, 4 * half + j, :], b[:, hsl(j)], ACS[:, c, h:h + 1], 0.0,
                                     ALU.subtract, ALU.min)
                        free(ins, ("row", c, g, half))
                if k >= 1:
                    c, g = (k - 1) // SG, (k - 1) % SG
                    gs = slice(g * 512, (g + 1) * 512)
                    if c == 0:
                        b = arrived(dve, ("yd", c, g))
                        free(tt(YT_[:, 0, gs], YT_[:, 0, gs], b, ALU.add), ("yd", c, g))
                    else:
                        if g == 0:
                            dve.wait_ge(S["second_chunk"], 2)
                        b = arrived(dve, ("yo", g))
                        free(tt(by_head(XDTD[:, gs]), by_head(b), bc(EAC[:, 1, 8 * g:8 * g + 8], 2, SP_), ALU.mult),
                             ("yo", g))
                        freed(dve, ("yo", g))
                        step(tt(YT_[:, 1, gs], YT_[:, 1, gs], XDTD[:, gs], ALU.add))
                        b = arrived(dve, ("yd", c, g))
                        free(tt(YT_[:, 1, gs], YT_[:, 1, gs], b, ALU.add), ("yd", c, g))
                if k < n_groups:
                    c, g = k // SG, k % SG
                    dve.wait_ge(S["seg_exp"], k + 1)
                    signal(tt(EM[:, k % 2], EM[:, k % 2], bc(CBM[:, c, g, :], 1, 8), ALU.mult), "m_ready")
            scale_rows(1, D, lambda t: MEMX[:, t, :], lambda t: XN[:, t, :])
            features("mT", MT, col("g_mem"))
            rest_quarters(m_hi, m_lo, "m_hi_ready", "m_lo_ready", MT)
            for b in range(4):
                for t in range(TT):
                    freed(dve, ("z", b, t))
            for g in range(SG):
                freed(dve, ("yd", 1, g))
            for t in range(TT):
                signal(tt(YT_[:, t, :], YT_[:, t, :], ZT[:, t, :], ALU.mult), "y_ready")
            scale_rows(2, SD, lambda t: YT_[:, t, :], lambda t: YT_[:, t, :])
            features("yTr", YT, col("g_ssd"), chunks=4)
            dve.wait_ge(S["at_hi_ready"], 1)
            tt(at_lo[:, :, :], AT, at_hi[:, :, :], ALU.subtract).then_inc(S["at_lo_ready"], 1)
            rest_quarters(y_hi, y_lo, "y_hi_ready", "y_lo_ready", YT, 4)

            def merged_rest(n):
                dve.wait_ge(S["mg_hi_ready"], n + 1)
                tt(mg_lo[:, n, :], MG[:, n, :], mg_hi[:, n, :], ALU.subtract).then_inc(S["mg_lo_ready"], 1)

            for j in range(8):
                freed(dve, ("gate", j), 1)
            for n in range(8):
                part = area(28672 + T * (n % 2), T)
                free(tt(part, GT[:, n, :], arrived(dve, ("ma", n))[:, 0:T], ALU.mult), ("ma", n))
                free(tt(MG[:, n, :], GT[:, 8 + n, :], arrived(dve, ("ms", n))[:, 0:T], ALU.mult), ("ms", n))
                freed(dve, ("ma", n))
                freed(dve, ("ms", n))
                signal(tt(MG[:, n, :], MG[:, n, :], part, ALU.add), "merged_ready")
                if n:
                    merged_rest(n - 1)
            merged_rest(7)

            def add_residual(name):
                for b in range(2):
                    for t in range(TT):
                        h = hres[:, t, b * 512:(b + 1) * 512]
                        free(tt(h, h, arrived(dve, (name, b, t)), ALU.add), (name, b, t))
                for b in range(2):
                    for t in range(TT):
                        freed(dve, (name, b, t))

            add_residual("wo")
            scale_rows(3, D, lambda t: hres[:, t, :], lambda t: XN[:, t, :])
            features("a2T", actT, col("g_cross"))
            rest_quarters(a2_hi, a2_lo, "a2_hi_ready", "a2_lo_ready")
            for t in range(TT):
                for p in range(2):
                    b = arrived(dve, ("cl", t, p)).rearrange("p (c n) -> p c n", c=2)
                    ins = V.tensor_reduce(smx[:, t, 0, 2 * p:2 * p + 2], b, AX.X, ALU.max)
                step(ins)
                signal(ts(smx[:, t, 1, 0:4], smx[:, t, 0, 0:4], -(MD ** -0.5), None, ALU.mult), "cl_ready")
                for p in range(2):
                    freed(dve, ("cl", t, p))
                step(V.reciprocal(smx[:, t, 3, 0:4], smx[:, t, 2, 0:4]))
                signal(tt(CL, CL, bc(smx[:, t, 3, 0:4], 2, T), ALU.mult), "cprob")
            for h in range(MH):
                dve.wait_ge(S["co_hi_ready"], h + 1)
                c = slice(2 * h, 2 * h + 2)
                free(tt(co_lo[:, c, :], COT[:, c, :], co_hi[:, c, :], ALU.subtract), ("co", h))
            add_residual("cw")
            scale_rows(4, D, lambda t: hres[:, t, :], lambda t: XN[:, t, :])
            features("a3T", actT, col("g_ffn"))
            rest_quarters(pq_hi, pq_lo, "pq_hi_ready", "pq_lo_ready")

            def top16(groups, src, work, val, idx):
                for g in groups:
                    ins = V.max(val(g)[:, 0:8], src(g))
                step(ins)
                for g in groups:
                    V.max_index(idx(g)[:, 0:8], val(g)[:, 0:8], src(g))
                    ins = V.match_replace(out=work(g), in_to_replace=val(g)[:, 0:8], in_values=src(g),
                                          imm_value=TAKEN)
                step(ins)
                for g in groups:
                    ins = V.max(val(g)[:, 8:16], work(g))
                step(ins)
                for g in groups:
                    ins = V.max_index(idx(g)[:, 8:16], val(g)[:, 8:16], work(g))
                step(ins)

            idxu = TOPI.bitcast(U32)
            sciu = SCI.bitcast(U32)
            ciau = CIA.bitcast(U32)

            def best_keys(t):
                for q in range(4):
                    freed(dve, ("sk", t, q))
                top16(range(16), lambda g: SK[:, t, g, :], lambda g: SK2[:, g, :], lambda g: TOPV[:, g, :],
                      lambda g: idxu[:, g, :])

            def best_pairs(t):
                v = TOPV.rearrange("p (h x) k -> p h x k", x=2)
                step(tt(CAND.rearrange("p h (i j) -> p h i j", j=PTOP), bc(v[:, :, 0, :], 3, PTOP),
                        bc(v[:, :, 1, :], 2, PTOP), ALU.add))
                top16(range(PH), lambda g: CAND[:, g, :], lambda g: CAND2[:, g, :], lambda g: SCV[:, g, :],
                      lambda g: sciu[:, g, :])
                flat = sciu.rearrange("p h k -> p (h k)")
                ts(ciau[:, 0, :], flat, 4, None, ALU.logical_shift_right)
                ts(ciau[:, 1, :], flat, 15, None, ALU.bitwise_and)
                step(cp(TOPIF, idxu))
                step(cp(CIAF, ciau))
                num = TOPIF.rearrange("p (h x) k -> p h x k", x=2)
                oh4 = OH.rearrange("p (h k j) -> p h k j", h=PH, k=PTOP)
                oh3 = OH.rearrange("p (s j) -> p s j", j=PTOP)
                for x in range(2):
                    step(tt(oh3, bc(CIAF[:, x, :], 2, PTOP), bc(C("iota16"), 1, P), ALU.is_equal))
                    step(tt(oh4, oh4, bc(num[:, :, x, :], 2, PTOP), ALU.mult))
                    step(V.tensor_reduce(EAB[:, t, x, :], oh3, AX.X, ALU.add))

            def gates(t):
                g3 = EAB[:, t, 2, :].rearrange("p (h k) -> p h k", h=PH)
                signal(tt(g3, SCV, bc(SCV[:, :, 0], 2, PTOP), ALU.subtract), "gate_sc")
                dve.wait_ge(S["gate_exp"], t + 1)
                step(V.tensor_reduce(SMX, g3, AX.X, ALU.add))
                step(V.reciprocal(SMX, SMX))
                signal(tt(g3, g3, bc(SMX, 2, PTOP), ALU.mult), "idx_ready")

            scale_rows(5, D, lambda t: CX[:, t, :], lambda t: XN[:, t, :])
            best_keys(0)
            freed(dve, ("ad0", ADA_JOB[3, 1]))
            step(tt(mods[:, 0:16, :], mods[:, 0:16, :], bc(col("b_ada")[:, 0:16], 2, 2), ALU.add))
            stt(modsb[:, 0:8], mods[:, 8:16, 0], 1.0, col("g_mix2"), ALU.add, ALU.mult)
            stt(modsb[:, 8:16], mods[:, 8:16, 1], 1.0, col("g_mix2"), ALU.add, ALU.mult)
            cp(modsb[:, 40:48], mods[:, 0:8, 0])
            step(cp(modsb[:, 48:56], mods[:, 0:8, 1]))
            features("cT", CXT, modsb[:, 8:16], modsb[:, 48:56])
            best_pairs(0)

            def gate_logs(f, lf, nk, names):
                signal(stt(lf, f, -1.0, f, ALU.mult, ALU.max), names[0])
                dve.wait_ge(S[names[1]], 1)
                signal(stt(nk, f, 0.0, lf, ALU.max, ALU.add), names[2])
                signal(stt(lf, f, 0.0, lf, ALU.min, ALU.subtract), names[3], 1)

            for b in range(3):
                for t in range(TT):
                    freed(dve, ("cp", b, t))
            gate_logs(CPJ[:, :, 0:1024], CLF, CKK, ("ctx_abs", "ctx_l", "ctx_nk", "ctx_f"))
            best_keys(1)
            dve.wait_ge(S["ctx_k"], 1)
            for d in range(2):
                for t in range(TT):
                    freed(dve, ("ce", d, t))
            signal(tt(CKK, CKK, CEX, ALU.mult), "ctx_kd")
            gates(0)
            best_pairs(1)
            gates(1)
            freed(dve, ("ad2", ADA_JOB[3, 1]))
            step(tt(mods[:, 16:48, :], mods[:, 16:48, :], bc(col("b_ada")[:, 16:48], 2, 2), ALU.add))
            stt(modsb[:, 16:24], mods[:, 32:40, 0], 1.0, col("g_ffn2"), ALU.add, ALU.mult)
            cp(modsb[:, 24:32], mods[:, 24:32, 0])
            for t in range(TT):
                freed(dve, ("eTr", t))
            ts(slots[:, 3, :], slots[:, 1, :], -1.0, None, ALU.mult).then_inc(S["slots_negated"], 1)
            with dve.Fori(0, T // 16) as i:
                for u in range(4):
                    b, n = B.at[("w", u)]
                    dve.wait_ge(bank_full[b], i + (n - 1))
                    quad = lambda x: bc(slots[:, x, bass.ds(i * 16 + 4 * u, 4)], 2, P)
                    tt(ROWHOT[:, u], bc(C("iota"), 1, 4), quad(0), ALU.is_equal).then_inc(S["rows_made"], 1)
                    if u:
                        tt(COLUMN[u], bc(C("iota"), 1, 4), quad(1), ALU.is_equal).then_inc(S["dve_columns"], 1)

            def split_rest(e, ready, turn=None, n=8):
                i_ = 0 if turn is None else turn
                dve.wait_ge(S["hi_ready"], i_ * n + (e + 1))
                dve.wait_ge(S["hi_used"], i_ * n + e)
                tt(w_lo[:, e % 2, :], raw(e)[0], w_hi[:, e % 2, :], ALU.subtract).then_inc(S[ready], 1)

            def split_product(out, hi, lo_, x, y, made, count, ready):
                tt(out, x, y, ALU.mult).then_inc(made, 1)
                ins = tt(hi, x, y, ALU.mult)
                ins.then_inc(made, 1)
                dve.wait_ge(made, count)
                tt(lo_, out, hi, ALU.subtract).then_inc(S[ready], 1)
                return ins

            for e in range(2):
                split_rest(X0 + e, "lo_ready")
            freed(dve, ("h0",))
            for u in range(4):
                freed(dve, ("w", u), T // 16 - 1)

            def gate_row(a, turn=None):
                n = 0 if turn is None else turn * 4
                row_ = WT[:, a, :] if turn is None else WT[:, turn * 4 + a, :]
                split_product(GATED, gated_hi[:, a % 2, :], gated_lo[:, a % 2, :], GELU[:, a % 2, :], row_,
                              S["gated_made"], n * 2 + (2 * a + 2), "p_ready")

            gate_row(0)
            split_rest(X0 + 2, "lo_ready")
            with dve.Fori(0, 31) as i:
                for u in range(4):
                    freed(dve, ("h", u), i)
                    gate_row(u + 1, i)
                    split_rest(X0 + 2 * u + 3, "lo_ready", i)
                    split_rest(X0 + 2 * u + 4, "lo_ready", i)
            for u in range(3):
                a = 125 + u
                freed(dve, ("he", u))
                gate_row(a)
                split_rest(X0 + 2 * a + 1, "lo_ready")
                if a < 127:
                    split_rest(X0 + 2 * a + 2, "lo_ready")
            dve.wait_ge(in_gain, 16)
            scale_rows(6, D, lambda t: hres[:, t, :], lambda t: hres[:, t, :], FIN1)
            scale_rows(7, D, lambda t: hres[:, t, :], lambda t: XN[:, t, :])
            features("x2T", actT, modsb[:, 0:8], modsb[:, 40:48])
            rest_quarters(x2_hi, x2_lo, "x2_hi_ready", "x2_lo_ready")
            h4 = lambda ap: ap.rearrange("p t (h n) -> p t h n", h=HH)
            O, VV = PJ[:, :, 0:512], PJ[:, :, 3072:3584]
            for b in P_ORDER:
                for t in range(TT):
                    freed(dve, ("p", b, t))
                if b == 6:
                    step(V.tensor_reduce(gst[:, 3, 1], h4(VV), AX.X, ALU.add))
                    step(ts(gst[:, 3, 1], gst[:, 3, 1], 1.0 / P, None, ALU.mult))
                    step(tt(h4(VV), h4(VV), bc(gst[:, 3, 1], 3, P), ALU.subtract))
                    step(tt(SQV, VV, VV, ALU.mult))
                    step(V.tensor_reduce(gst[:, 0, 1], h4(SQV), AX.X, ALU.add))
                    signal(ts(gst[:, 1, 1], gst[:, 0, 1], 1.0 / P, EPS, ALU.mult, ALU.add), "v_ms")
                    dve.wait_ge(S["v_root"], 1)
                    step(V.reciprocal(gst[:, 3, 1], gst[:, 2, 1]))
                    step(tt(h4(VV), h4(VV), bc(gst[:, 3, 1], 3, P), ALU.mult))
                    dve.wait_ge(in_second, 4 * 16)
                    step(tt(VV, VV, bc(R2[:, 512:1024], 1, TT), ALU.mult))
                    signal(tt(VV, VV, bc(R2[:, 1024:1536], 1, TT), ALU.add), "v_ready")
                if b == 1:
                    gate_logs(PJ[:, :, 0:1024], LF, K2, ("g_abs", "g_l", "g_nk", "g_logf"))
            for t in range(TT):
                b = arrived(dve, ("sg", t)).rearrange("p (h n) -> p h n", h=HH)
                v = PJ[:, t, 512:1024]
                free(tt(v.rearrange("p (h n) -> p h n", h=HH), b, bc(col("b_s"), 2, P), ALU.add), ("sg", t))
                freed(dve, ("sg", t))
                tt(v, v, PJ[:, t, 2560:3072], ALU.mult)
            dve.wait_ge(S["g_k"], 1)
            for d in range(2):
                freed(dve, ("as", d))
                signal(tt(KD[:, d, :], KD[:, d, :], K2[:, d, d * 512:(d + 1) * 512], ALU.mult), "g_kd")
            freed(dve, ("tot",))
            for d in range(2):
                b = arrived(dve, ("adv", d))
                for h in range(HH):
                    ins = stt(HS[:, d, h, :], h0[:, d, h, :], TOTE[:, d * 4 + h:d * 4 + h + 1], b[:, hsl(h)],
                              ALU.mult, ALU.add)
                free(ins, ("adv", d))
            for d in range(2):
                for t in range(TT):
                    freed(dve, ("kT2", d, t))
            for t in range(TT):
                freed(dve, ("qT2", t))
            signal(tt(KS, K2T[:, 0], K2T[:, 1], ALU.add), "g_H")
            dve.wait_ge(in_second, 4 * 16)
            for t in range(TT):
                b = arrived(dve, ("dg", t)).rearrange("p (h n) -> p h n", h=HH)
                free(tt(SM, b, bc(ident, 1, HH), ALU.mult), ("dg", t))
                freed(dve, ("dg", t))
                for d in range(2):
                    n = N_LEVELS - POOL_LEVELS
                    for h in range(HH):
                        for half in range(2):
                            freed(dve, ("e", t, d, h, half))
                        q = Q2T[:, h, tsl(t)]
                        z = ZQ[:, h, POOL_LEVELS:7, :]
                        tt(ZK[:, h, POOL_LEVELS:7, :], z, bc(K2T[:, d, h, tsl(t)], 1, n), ALU.mult)
                        tt(ZP[:, d, h, :], ZQ[:, h, 7, :], q, ALU.mult)
                        ins = tt(z, z, bc(q, 1, n), ALU.mult)
                    signal(ins, "z_made")
                    for lev in range(N_LEVELS):
                        b = arrived(dve, ("gr", t, d, lev)).rearrange("p (h n) -> p h n", h=HH)
                        m = bc(LEV[:, d * 7 + lev, :].bitcast(U32), 1, HH)
                        free(V.copy_predicated(SM, m, b), ("gr", t, d, lev))
                        freed(dve, ("gr", t, d, lev))
                if t == TT - 1:
                    tt(GBD[:, 0], bc(ident, 1, KC), bc(mods[:, 16:24, 0], 2, P), ALU.mult)
                    signal(tt(GBD[:, 1], bc(ident, 1, KC), bc(mods[:, 40:48, 0], 2, P), ALU.mult), "gdiag")
                free(cp(PJ[:, t, 0:512], arrived(dve, ("o", t))), ("o", t))
            for t in range(TT):
                freed(dve, ("o", t))
            step(tt(SQO, O, O, ALU.mult))
            step(V.tensor_reduce(gst[:, 0, 0], h4(SQO), AX.X, ALU.add))
            signal(ts(gst[:, 1, 0], gst[:, 0, 0], 1.0 / P, EPS, ALU.mult, ALU.add), "o_ms")
            dve.wait_ge(S["o_root"], 1)
            step(V.reciprocal(gst[:, 3, 0], gst[:, 2, 0]))
            step(tt(h4(O), h4(O), bc(gst[:, 3, 0], 3, P), ALU.mult))
            signal(tt(O, O, bc(R2[:, 0:512], 1, TT), ALU.mult), "rows_used", 1)
            for t in range(TT):
                signal(tt(O[:, t, :], O[:, t, :], PJ[:, t, 2048:2560], ALU.mult), "oc_ready")
            signal(V.memset(ZEROS, 0.0), "zeros_ready")
            for r in range(4):
                freed(dve, ("gb", r))

            def add_gated(name, g, done, order):
                for n, (b, t) in enumerate(order):
                    s = slice(b * 512, (b + 1) * 512)
                    job = (name, b, t) if name == "w2" else (name, t, b)
                    free(tt(T512[:, n, :], arrived(dve, job), GB[:, g, s], ALU.mult), job)
                    freed(dve, job)
                    signal(tt(hres[:, t, s], hres[:, t, s], T512[:, n, :], ALU.add), done)
                dve.wait_ge(S[done], 4)

            add_gated("w2", 0, "x3_ready", [(b, t) for b in range(2) for t in range(TT)])
            scale_rows(8, D, lambda t: hres[:, t, :], lambda t: XN[:, t, :])
            features("x3T", actT, modsb[:, 16:24], modsb[:, 24:32])

            grid = lambda ap: ap.rearrange("p (r w) -> p r w", w=GW)
            R = T // GW

            dve.wait_ge(S["x3_hi_ready"], 1)
            tt(x3_lo[:, :, :], actT[:, :, :], x3_hi[:, :, :], ALU.subtract).then_inc(S["x3_lo_ready"], 1)
            for r in range(2):
                split_rest(F0 + r, "ffn_lo_ready")

            def conv_channels(gate_job, c, base, par, turn=None, meanwhile=None):
                freed(dve, gate_job, turn)
                tap = lambda k: col("taps")[:, bass.ds(c * 9 + k, 1)]
                x, o = grid(GC[:, par, :]), grid(CV[:, par, :])
                for n, k in enumerate((0, 1, 2, 3, 5, 6, 7, 8)):
                    dr, dw = k // 3 - 1, k % 3 - 1
                    ro, wo = slice(max(0, -dr), R - max(0, dr)), slice(max(0, -dw), GW - max(0, dw))
                    ri, wi = slice(max(0, dr), R + min(0, dr)), slice(max(0, dw), GW + min(0, dw))
                    if n:
                        dve.wait_ge(step.c.sem, base + n)
                    ins = stt(o[:, ro, wo], x[:, ri, wi], tap(k), o[:, ro, wo], ALU.mult, ALU.add)
                    ins.then_inc(step.c.sem if k < 8 else S["ffn_conv"], 1)
                    if n == 5 and meanwhile:
                        meanwhile()

            def hidden_channels(value_job, c, par, turn=None, second=True):
                dve.wait_ge(S["ffn_gelu"], c + 1)
                b = arrived(dve, value_job, turn)[:, 0:T]
                if second:
                    dve.wait_ge(S["hidden_ready"], c)
                tt(HF, GE[:, par, :], b, ALU.mult).then_inc(S["hidden_made"], 1)
                free(tt(hidden_hi[:, par, :], GE[:, par, :], b, ALU.mult), value_job)

            n0 = step.c.n
            per = 7
            conv_channels(("g0",), 0, n0, 0, meanwhile=lambda: split_rest(F0 + 2, "ffn_lo_ready"))
            split_rest(F0 + 3, "ffn_lo_ready")
            hidden_channels(("a0",), 0, 0, second=False)
            with dve.Fori(0, (FC - 2) // 2) as i:
                for u in range(2):
                    conv_channels(("ga", 2 * u), i * 2 + (u + 1), i * (2 * per) + (n0 + per * (u + 1)), (u + 1) % 2, i,
                                  lambda: split_rest(F0 + 5 + 3 * u, "ffn_lo_ready", i, 6))
                    split_rest(F0 + 6 + 3 * u, "ffn_lo_ready", i, 6)
                    hidden_channels(("ga", 2 * u + 1), i * 2 + (u + 1), (u + 1) % 2, i)
            conv_channels(("ge",), FC - 1, n0 + per * (FC - 1), 1)
            hidden_channels(("ae",), FC - 1, 1)
            step.c.n = n0 + per * FC
            add_gated("f", 1, "x4_ready", [(b, t) for t in range(TT) for b in range(2)])
            scale_rows(9, D, lambda t: hres[:, t, :], lambda t: XN[:, t, :])
            dve.wait_ge(in_second, 5 * 16)
            for t in range(TT):
                dve.wait_ge(S["xn_ready"], 9 * TT + t + 1)
                signal(tt(XN[:, t, :], XN[:, t, :], FIN2, ALU.mult), "out_ready")


def chunk_columns(v):
    return v.reshape(-1, P).T


def token_tiles(w):
    n = w.shape[1] // 512
    return w.reshape(4, 2, P, n, 512).transpose(3, 0, 2, 1, 4).reshape(4 * n, P, 1024)


def feature_tiles(w):
    n = w.shape[1] // P
    return w.reshape(KC, P, n, P).transpose(2, 1, 0, 3).reshape(n, P, 1024)


def constants():
    i = np.arange(P)
    c = np.zeros((P, N_CONST), np.float32)

    def put(name, v):
        o, w = CONST[name]
        c[:, o:o + w] = v

    put("ident", np.eye(P))
    put("upto", i[:, None] <= i[None, :])
    put("ones", 1.0)
    put("after", i[:, None] > i[None, :])
    put("before", i[:, None] < i[None, :])
    put("causal", np.where(i[None, :] <= i[:, None], 0.0, NEG))
    put("iota", i[None, :])
    put("iota16", np.arange(16)[None, :])
    f = np.float32(THETA) ** (np.float32(-2.0) * np.arange(16, dtype=np.float32) / np.float32(32))
    g = np.float32(THETA) ** (np.float32(-2.0) * np.arange(8, dtype=np.float32) / np.float32(16))
    put("freq", np.concatenate([f, g])[None, :])
    u, pos = i[:, None], i[None, :]
    span = np.zeros((P, 2, N_LEVELS + 1, P), np.float32)
    lev = np.zeros((P, 14, P), np.float32)
    s, t = i[:, None], i[None, :]
    for m in range(N_LEVELS):
        w = 1 << m
        mid = pos // (2 * w) * (2 * w) + w
        up = pos >= mid
        span[:, 0, m] = np.where(up, (u >= mid) & (u <= pos), (u > pos) & (u < mid))
        span[:, 1, m] = np.where(up, (u >= mid) & (u < pos), (u >= pos) & (u < mid))
        same = s // (2 * w) == t // (2 * w)
        lev[:, m] = same & (s % (2 * w) < w) & (t % (2 * w) >= w)
        lev[:, 7 + m] = same & (s % (2 * w) >= w) & (t % (2 * w) < w)
    span[:, 0, N_LEVELS] = u <= pos
    span[:, 1, N_LEVELS] = u >= pos
    return c, span.reshape(P, 2, -1), lev


def kernel(**inputs):
    import concourse.bacc as _bacc
    from concourse.bass_utils import run_bass_kernel_spmd as _run

    a = {k: np.asarray(v) for k, v in inputs.items()}
    w_in = a["w_in"][0]
    o = np.cumsum([0, 1024, 256, 256, 256, 64, 4, 2048, 3072, 32, 2048])
    q, k, v, iq, ik, iw, z, xbc, dt, gate = (w_in[:, o[n]:o[n + 1]] for n in range(10))
    tok = np.concatenate([q, k, iq, ik, v, iw, dt, np.zeros((D, 2048 - 1892), np.float32)], axis=1)
    ws = a["w_ssd_branch"][0]
    wa, ws0, ws1 = feature_tiles(a["w_attn_branch"][0]), feature_tiles(ws[:1024]), feature_tiles(ws[1024:])
    merge = np.stack([wa, ws0, ws1], axis=1).reshape(24, P, 1024)
    kv = a["w_cross_kv"][0]
    w2 = a["w_in_2"][0]
    ut = a["peer_u"][0].reshape(P, P, KC, P).transpose(0, 3, 2, 1).reshape(P, P, 1024)
    vt = a["peer_v"][0].reshape(P, P, 1024)
    up = a["w_up_2"][0]
    gt, at = feature_tiles(up[:, FF:]), feature_tiles(up[:, :FF])
    dn = a["w_down_2"][0].reshape(FC, P, 1024)
    ada = token_tiles(a["w_ada_2"][0])
    parts = [token_tiles(tok), feature_tiles(xbc), token_tiles(z), feature_tiles(gate), feature_tiles(kv[:, :1024]),
             token_tiles(kv[:, 1024:]), merge, token_tiles(a["w_out"][0]), feature_tiles(a["w_cross_q"][0]),
             token_tiles(a["w_cross_out"][0]), feature_tiles(a["w_peer_q"][0]), ada[:16],
             token_tiles(w2[:, :1536]), ada[16:],
             ut[0:1], np.stack([ut[1:], vt[:-1]], axis=1).reshape(254, P, 1024), vt[-1:],
             np.concatenate([token_tiles(w2)[4 * b:4 * b + 4] for b in P_ORDER]), token_tiles(a["w_out_2"][0]),
             gt[0:1], at[0:1], np.stack([gt[1:], at[1:], dn[:-1]], axis=1).reshape(63, P, 1024), dn[-1:]]
    stream = np.concatenate(parts, axis=0)
    assert stream.shape[0] == N_RING + N_FFN
    cols = np.zeros((P, N_COLS), np.float32)
    pc = chunk_columns
    conv = a["conv_w"][0][:, 0, :].T.reshape(24, P, 4).transpose(1, 0, 2).reshape(P, 96)
    taps = a["conv_w_2"][0].reshape(9, FC, P).transpose(2, 1, 0).reshape(P, 198)
    cc = np.stack([pc(a["c_2"][0]), pc(a["c_ctx_2"])], axis=2).reshape(P, 16)
    for name, val in [("g_mix", pc(a["norm_mix_g"][0])), ("g_cross", pc(a["norm_cross_g"][0])),
                      ("g_mem", pc(a["norm_mem_g"][0])), ("g_ffn", pc(a["norm_ffn_g"][0])),
                      ("g_ssd", pc(a["ssd_norm_g"][0])), ("conv_w", conv), ("conv_b", pc(a["conv_b"][0])),
                      ("c2", cc), ("b_ada", pc(a["b_ada_2"][0])), ("g_mix2", pc(a["norm_mix_2"][0])),
                      ("g_ffn2", pc(a["norm_ffn_2"][0])), ("taps", taps), ("fconv_b", pc(a["conv_b_2"][0])),
                      ("b_s", a["b_spatial_2"][0].T)]:
        c0, w = COLS[name]
        cols[:, c0:c0 + w] = val
    const, span, lev = constants()
    arrays = {
        "stream": stream, "x": a["x"], "mem": a["mem"], "ctx": a["ctx_2"], "const": const, "cols": cols,
        "rows": np.concatenate([a["dt_bias"][0], a["a_log"][0], a["d_skip"][0]]),
        "pos": np.ascontiguousarray(a["positions"][0].reshape(TT, P).T.astype(np.int32)),
        "keys": np.ascontiguousarray(a["peer_sub_keys"][0].transpose(3, 0, 1, 2).reshape(P, 16, P)),
        "fin1": a["norm_final_g"], "fin2": a["norm_final_2"],
        "rows2": np.concatenate([a["hg_norm_2"][0], a["sgu_norm_g_2"][0], a["sgu_norm_b_2"][0]]),
        "levels": lev, "span": span,
        "wsp": np.ascontiguousarray(a["w_spatial_2"][0].transpose(2, 0, 1)),
    }
    nc = _bacc.Bacc("TRN2", target_bir_lowering=False, num_devices=1)
    aps = {n: nc.dram_tensor(f"in_{n}", list(v.shape), mybir.dt.from_np(v.dtype), kind="ExternalInput").ap()
           for n, v in arrays.items()}
    aps["out"] = nc.dram_tensor("out", [1, T, D], F32, kind="ExternalOutput").ap()
    build(nc, aps)
    r = _run(nc, [{f"in_{n}": v for n, v in arrays.items()}], core_ids=[0])
    return r.results[0]["out"]
```
